# Optimizing a Trainium2 kernel written in Bass

```python
import jax, jax.numpy as jnp
from jax import lax
import numpy as np

D_MODEL = 1024
BATCH = 1
SEQ = 512
DEPTH = 2

GRID_W = 64
CTX_LEN = 256
D_MIX = D_MODEL
D_FOURIER = D_MIX // 2
FOURIER_GROUPS = 8
FOURIER_GW = D_FOURIER // FOURIER_GROUPS
D_MLSTM = D_MIX - D_FOURIER
MLSTM_HEADS = 4
MLSTM_HD = D_MLSTM // MLSTM_HEADS
N_GATE = 4 * MLSTM_HEADS
D_IN = D_FOURIER + 2 * D_MLSTM + N_GATE
CONV_K = 3
CHUNK = 128
D_FF = 2816
N_MOD = 9
FFN_RES = 0.5
EPS = 1e-6

kernel_name = "hybrid_fourier_mlstm_macaron_dit"

def rmsnorm(x, w):
    xf = x.astype(jnp.float32)
    y = xf * lax.rsqrt(jnp.mean(xf * xf, axis=-1, keepdims=True) + EPS)
    return (y * w.astype(jnp.float32)).astype(x.dtype)

def _mod(m, j):
    return m[..., 3 * j, :], m[..., 3 * j + 1, :], m[..., 3 * j + 2, :]

def _pre(x, nw, shift, scale):
    return rmsnorm(x, nw) * (1 + scale) + shift

def swiglu(h, w_in_ff, w_out_ff):
    gu = h @ w_in_ff
    g, u = gu[..., :D_FF], gu[..., D_FF:]
    return (jax.nn.silu(g) * u) @ w_out_ff

def _ffn_sublayer(x, mod, j, nw_pre, nw_post, w_in_ff, w_out_ff):
    shift, scale, gate = _mod(mod, j)
    y = swiglu(_pre(x, nw_pre, shift, scale), w_in_ff, w_out_ff)
    return x + FFN_RES * gate * rmsnorm(y, nw_post)

def fourier_mix(xf, w_fmix):
    b_, s_, _ = xf.shape
    xg = xf.astype(jnp.float32).reshape(b_, s_, FOURIER_GROUPS, FOURIER_GW)
    y = jnp.fft.fft2(xg, axes=(1, 3), norm="ortho").real.astype(xf.dtype)
    y = jnp.einsum("bsgc,gcd->bsgd", y, w_fmix)
    return y.reshape(b_, s_, D_FOURIER)

def grid_conv(x, w, b):
    b_, s_, c_ = x.shape
    rows = s_ // GRID_W
    img = x.reshape(b_, rows, GRID_W, c_)
    y = lax.conv_general_dilated(img, w[:, :, None, :].astype(x.dtype), (1, 1), "SAME",
                                 dimension_numbers=("NHWC", "HWIO", "NHWC"),
                                 feature_group_count=c_)
    return y.reshape(b_, s_, c_) + b

def seq_conv(x, w, b):
    c_ = x.shape[-1]
    y = lax.conv_general_dilated(x, w[:, None, :].astype(x.dtype), (1,), "SAME",
                                 dimension_numbers=("NWC", "WIO", "NWC"),
                                 feature_group_count=c_)
    return y + b

def _split_proj(u):
    xf = u[..., :D_FOURIER]
    xm = u[..., D_FOURIER:D_FOURIER + D_MLSTM]
    z = u[..., D_FOURIER + D_MLSTM:D_FOURIER + 2 * D_MLSTM]
    g = u[..., D_FOURIER + 2 * D_MLSTM:]
    return xf, xm, z, g

def _mlstm_inputs(xm, xconv, g, w_qkv, gate_b):
    b_, s_, _ = xm.shape
    heads = lambda t: t.reshape(b_, s_, MLSTM_HEADS, MLSTM_HD)
    q = jnp.einsum("bshd,hde->bhse", heads(xconv), w_qkv[0]).astype(jnp.float32)
    k = (jnp.einsum("bshd,hde->bhse", heads(xconv), w_qkv[1]) * MLSTM_HD ** -0.5).astype(jnp.float32)
    v = jnp.einsum("bshd,hde->bhse", heads(xm), w_qkv[2]).astype(jnp.float32)
    gp = g.astype(jnp.float32) + gate_b.reshape(-1).astype(jnp.float32)
    gp = jnp.transpose(gp.reshape(b_, s_, 4, MLSTM_HEADS), (2, 0, 3, 1))
    gates = (gp[0], jax.nn.log_sigmoid(gp[1]), gp[2], jax.nn.log_sigmoid(gp[3]))
    return q, k, v, gates

def _flip(t):
    return jnp.flip(t, axis=2)

def _chunk(t):
    return t.reshape(t.shape[:2] + (t.shape[2] // CHUNK, CHUNK) + t.shape[3:])

def mlstm_states(k, v, ig, lf, state0):
    kc, vc = _chunk(k), _chunk(v)
    igc, lfc = _chunk(ig), _chunk(lf)
    b = jnp.cumsum(lfc, axis=-1)
    b_tot = b[..., -1]
    a = b_tot[..., None] - b + igc
    m_loc = jnp.max(a, axis=-1)
    w = jnp.exp(a - m_loc[..., None])
    c_loc = jnp.einsum("bhcsd,bhcse->bhcde", vc * w[..., None], kc)
    n_loc = jnp.einsum("bhcs,bhcse->bhce", w, kc)

    def step(carry, xs):
        c_st, n_st, m_st = carry
        cl, nl, ml, bt = xs
        m_new = jnp.maximum(bt + m_st, ml)
        dec = jnp.exp(bt + m_st - m_new)
        inj = jnp.exp(ml - m_new)
        c_new = dec[..., None, None] * c_st + inj[..., None, None] * cl
        n_new = dec[..., None] * n_st + inj[..., None] * nl
        return (c_new, n_new, m_new), (c_st, n_st, m_st)

    xs = (jnp.moveaxis(c_loc, 2, 0), jnp.moveaxis(n_loc, 2, 0),
          jnp.moveaxis(m_loc, 2, 0), jnp.moveaxis(b_tot, 2, 0))
    final, prev = lax.scan(step, state0, xs)
    prev = tuple(jnp.moveaxis(t, 0, 2) for t in prev)
    return prev, final

def mlstm_outputs(q, k, v, ig, lf, prev):
    c_prev, n_prev, m_prev = prev
    qc, kc, vc = _chunk(q), _chunk(k), _chunk(v)
    igc, lfc = _chunk(ig), _chunk(lf)
    b = jnp.cumsum(lfc, axis=-1)
    log_inter = b + m_prev[..., None]
    log_intra = b[..., :, None] - b[..., None, :] + igc[..., None, :]
    scan_order = jnp.tril(jnp.ones((CHUNK, CHUNK), dtype=bool))
    log_intra = jnp.where(scan_order, log_intra, -jnp.inf)
    m_t = jnp.maximum(log_inter, jnp.max(log_intra, axis=-1))
    w_intra = jnp.exp(log_intra - m_t[..., None])
    w_inter = jnp.exp(log_inter - m_t)
    s = jnp.einsum("bhctd,bhcsd->bhcts", qc, kc) * w_intra
    num = (jnp.einsum("bhcts,bhcsd->bhctd", s, vc)
           + w_inter[..., None] * jnp.einsum("bhcde,bhcte->bhctd", c_prev, qc))
    den = jnp.sum(s, axis=-1) + w_inter * jnp.einsum("bhce,bhcte->bhct", n_prev, qc)
    h = num / jnp.maximum(jnp.abs(den), jnp.exp(-m_t))[..., None]
    return h.reshape(q.shape)

def _bidir_outputs(q, k, v, gates, prev_f, prev_b):
    i_f, f_f, i_b, f_b = gates
    h_f = mlstm_outputs(q, k, v, i_f, f_f, prev_f)
    h_b = mlstm_outputs(_flip(q), _flip(k), _flip(v), _flip(i_b), _flip(f_b), prev_b)
    return h_f + _flip(h_b)

def head_norm(h, w):
    mu = jnp.mean(h, axis=-1, keepdims=True)
    var = jnp.mean(jnp.square(h - mu), axis=-1, keepdims=True)
    hn = (h - mu) * lax.rsqrt(var + EPS)
    b_, _, s_, _ = h.shape
    hn = jnp.transpose(hn, (0, 2, 1, 3)).reshape(b_, s_, D_MLSTM)
    return hn * w.astype(jnp.float32)

def _combine(xf, h_sum, z, w_fmix, hn_w, w_out):
    yf = fourier_mix(xf, w_fmix)
    ym = head_norm(h_sum, hn_w).astype(z.dtype) * jax.nn.sigmoid(z)
    return jnp.concatenate([yf, ym], axis=-1) @ w_out

def setup_inputs(seed: int = 0) -> dict:
    key = jax.random.key(seed)
    ks = jax.random.split(key, 20)
    nrm = lambda k, shape, s: jax.random.normal(k, shape, jnp.float32) * s
    forget_bias = jnp.linspace(3.0, 6.0, MLSTM_HEADS, dtype=jnp.float32)
    gb = nrm(ks[14], (DEPTH, 4, MLSTM_HEADS), 0.1)
    gb = gb + jnp.stack([jnp.zeros_like(forget_bias), forget_bias,
                         jnp.zeros_like(forget_bias), forget_bias])[None]
    return {
        "x": nrm(ks[0], (BATCH, SEQ, D_MODEL), 1.0),
        "c": nrm(ks[1], (BATCH, D_MODEL), 1.0),
        "ctx": nrm(ks[2], (BATCH, CTX_LEN, D_MODEL), 1.0),
        "c_ctx": nrm(ks[3], (D_MODEL,), 1.0),
        "w_ada": nrm(ks[4], (DEPTH, D_MODEL, N_MOD * D_MODEL), 0.5 * D_MODEL ** -0.5),
        "b_ada": nrm(ks[5], (DEPTH, N_MOD * D_MODEL), 0.02),
        "norm_w": 1.0 + nrm(ks[6], (DEPTH, 6, D_MODEL), 0.05),
        "w_ff_in": nrm(ks[7], (DEPTH, 2, D_MODEL, 2 * D_FF), D_MODEL ** -0.5),
        "w_ff_out": nrm(ks[8], (DEPTH, 2, D_FF, D_MODEL), D_FF ** -0.5),
        "w_in": nrm(ks[9], (DEPTH, D_MODEL, D_IN), D_MODEL ** -0.5),
        "w_fmix": nrm(ks[10], (DEPTH, FOURIER_GROUPS, FOURIER_GW, FOURIER_GW), FOURIER_GW ** -0.5),
        "conv_w": nrm(ks[11], (DEPTH, CONV_K, CONV_K, D_MLSTM), (CONV_K * CONV_K) ** -0.5),
        "conv_b": nrm(ks[12], (DEPTH, D_MLSTM), 0.02),
        "w_qkv": nrm(ks[13], (DEPTH, 3, MLSTM_HEADS, MLSTM_HD, MLSTM_HD), MLSTM_HD ** -0.5),
        "gate_b": gb,
        "mlstm_norm_w": 1.0 + nrm(ks[15], (DEPTH, D_MLSTM), 0.05),
        "w_out": nrm(ks[16], (DEPTH, D_MIX, D_MODEL), D_MIX ** -0.5),
    }

def reference(x, c, ctx, c_ctx, w_ada, b_ada, norm_w, w_ff_in, w_ff_out, w_in, w_fmix,
              conv_w, conv_b, w_qkv, gate_b, mlstm_norm_w, w_out):
    b_ = x.shape[0]
    xl, xc = x, ctx
    zero = (jnp.zeros((b_, MLSTM_HEADS, MLSTM_HD, MLSTM_HD), jnp.float32),
            jnp.zeros((b_, MLSTM_HEADS, MLSTM_HD), jnp.float32),
            jnp.zeros((b_, MLSTM_HEADS), jnp.float32))
    for l in range(DEPTH):
        last = l == DEPTH - 1
        nw = norm_w[l]
        mod_l = (jax.nn.silu(c) @ w_ada[l] + b_ada[l]).reshape(b_, 1, N_MOD, D_MODEL)
        mod_c = (jax.nn.silu(c_ctx) @ w_ada[l] + b_ada[l]).reshape(N_MOD, D_MODEL)

        xl = _ffn_sublayer(xl, mod_l, 0, nw[0], nw[1], w_ff_in[l, 0], w_ff_out[l, 0])
        xc = _ffn_sublayer(xc, mod_c, 0, nw[0], nw[1], w_ff_in[l, 0], w_ff_out[l, 0])

        sh_l, sc_l, g_l = _mod(mod_l, 1)
        sh_c, sc_c, g_c = _mod(mod_c, 1)
        ul = _pre(xl, nw[2], sh_l, sc_l) @ w_in[l]
        uc = _pre(xc, nw[2], sh_c, sc_c) @ w_in[l]
        xf_l, xm_l, z_l, gp_l = _split_proj(ul)
        xf_c, xm_c, z_c, gp_c = _split_proj(uc)

        cv_l = jax.nn.silu(grid_conv(xm_l, conv_w[l], conv_b[l]))
        cv_c = jax.nn.silu(seq_conv(xm_c, conv_w[l, 1], conv_b[l]))
        q_l, k_l, v_l, gates_l = _mlstm_inputs(xm_l, cv_l, gp_l, w_qkv[l], gate_b[l])
        q_c, k_c, v_c, gates_c = _mlstm_inputs(xm_c, cv_c, gp_c, w_qkv[l], gate_b[l])

        prev_cf, st_f = mlstm_states(k_c, v_c, gates_c[0], gates_c[1], zero)
        prev_cb, st_b = mlstm_states(_flip(k_c), _flip(v_c), _flip(gates_c[2]),
                                     _flip(gates_c[3]), zero)
        prev_lf, _ = mlstm_states(k_l, v_l, gates_l[0], gates_l[1], st_f)
        prev_lb, _ = mlstm_states(_flip(k_l), _flip(v_l), _flip(gates_l[2]),
                                  _flip(gates_l[3]), st_b)
        h_l = _bidir_outputs(q_l, k_l, v_l, gates_l, prev_lf, prev_lb)
        y_l = _combine(xf_l, h_l, z_l, w_fmix[l], mlstm_norm_w[l], w_out[l])
        xl = xl + g_l * rmsnorm(y_l, nw[3])
        xl = _ffn_sublayer(xl, mod_l, 2, nw[4], nw[5], w_ff_in[l, 1], w_ff_out[l, 1])

        if not last:
            h_c = _bidir_outputs(q_c, k_c, v_c, gates_c, prev_cf, prev_cb)
            y_c = _combine(xf_c, h_c, z_c, w_fmix[l], mlstm_norm_w[l], w_out[l])
            xc = xc + g_c * rmsnorm(y_c, nw[3])
            xc = _ffn_sublayer(xc, mod_c, 2, nw[4], nw[5], w_ff_in[l, 1], w_ff_out[l, 1])
    return xl


_drawn_inputs = setup_inputs


def setup_inputs(seed=0):
    import zlib

    import numpy as np

    out = dict(_drawn_inputs(seed))
    spreads = {}
    factors = {'conv_b': 3.072, 'mlstm_norm_w': 4.469}
    for name, (base, spread) in spreads.items():
        noise = np.random.default_rng([zlib.crc32(name.encode()), seed]).standard_normal(out[name].shape)
        drawn = base * np.exp(spread * noise) if base else spread * noise
        out[name] = __import__('jax').numpy.asarray(drawn.astype(out[name].dtype))
    for name, factor in factors.items():
        out[name] = (out[name] * factor).astype(out[name].dtype)
    return out
```

```python
from contextlib import ExitStack, contextmanager

import numpy as np

import concourse.bass as bass
from concourse import mybir

F32 = mybir.dt.float32
F32R = mybir.dt.float32r
BF16 = mybir.dt.bfloat16
ALU = mybir.AluOpType
ACT = mybir.ActivationFunctionType
AX_X = mybir.AxisListType.X

P = 128
D = 1024
KC = D // P
SEQ, CTX = 512, 256
TOK = SEQ + CTX
NT, NTL = TOK // P, SEQ // P
DEPTH = 2
D_FF = 2816
FC = D_FF // P
HEADS, HD = 4, 128
GW = 384
GT = GW // P
SLOT = 2048
HB = 512
EPS = 1e-6
NEG = -1e30
START = 1
FREE = 2
HV = HD + 1

XN = 2 * KC * TOK
HG = FC * GW
A_H = XN
A_YS = A_H + 8 * GW
A_DUMMY = A_YS + 3 * D
A_XM = A_YS
A_QKVW = A_XM + HEADS * TOK
A_DFT = A_H + HG + 8 * GW
A_FW = A_QKVW + 12 * P
A_TRI = A_FW + 4 * P
A_DFTG = A_DFT + 8 * SEQ + 4 * CTX
A_XAB = 0
A_AB = A_XAB + NT * 256
A_CONV = 7168
A_GATE = A_CONV + HEADS * TOK


def plan():
    subs = []
    slot = hj = y = xn = proj = unit = half = mix = gate = 0
    xn = NT
    half = 4
    for l in range(DEPTH):
        for j in range(3):
            kind = "mix" if j == 1 else "ffn"
            last = l == DEPTH - 1
            final = last and j == 2
            groups = [GT, NTL - GT] if last and j >= 1 else [GT, GT]
            k_slots = 4 if kind == "mix" else FC // 2
            s = dict(l=l, j=j, kind=kind, final=final, groups=groups, k_slots=k_slots, slot=slot, hj=hj, y=y,
                     xn=xn, proj=proj, unit=unit, half=half, mix=mix, gate=gate,
                     next=None if final else ((l, j + 1) if j < 2 else (l + 1, 0)))
            s["in_slots"] = 7 if kind == "mix" else FC
            s["in_groups"] = [GT, NTL - GT] if final else [GT, GT]
            subs.append(s)
            slot += s["in_slots"] + 2 * k_slots
            hj += 4 * k_slots
            y += sum(groups)
            xn += 0 if final else sum(groups)
            halves = 2 if final else 6
            unit += 4 * halves
            half += halves
            s["half_end"] = half
            gate += 1
            if kind == "mix":
                mix += 1
            else:
                proj += FC
    return subs


SUBS = plan()


class Count:

    def __init__(self, eng, sem):
        self.eng, self.sem, self.n, self.term = eng, sem, 0, 0

    def mark(self, ins):
        ins.then_inc(self.sem, 1)
        self.n += 1

    def wait(self):
        self.eng.wait_ge(self.sem, self.n + self.term)

    def link(self, ins):
        self.mark(ins)
        self.wait()

    def wait_back(self, back):
        self.eng.wait_ge(self.sem, self.n - back + self.term)

    @contextmanager
    def loop(self, trips, per):
        base = self.n
        with self.eng.Fori(0, trips) as i:
            self.term = i * per
            yield i
        assert self.n - base == per, (self.n - base, per)
        self.term = 0
        self.n = base + trips * per


def scan_k(d, t):
    return (t + 2) % NT if d == 0 else NT - 1 - t


def scan_t(d, k):
    return (k + 4) % NT if d == 0 else NT - 1 - k


def scan_col(d, k, h):
    return d * 32 + k * 4 + h


def tiles_of(sub):
    return [list(range(GT)), list(range(GT, GT + sub["groups"][1]))]


def build(nc, x_in, w_ada, norm_w, w_ff_in, w_ff_out, w_in, w_gates, w_out, w_qkv, b_ada, cvec_in, gate_b_in,
          b_col_in, nw_col_in, convw_in, convb_in, hn_w_in, fmix_in, dft_l_in, dft_c_in, dft_g_in, tri_in, out):
    ctx = ExitStack()
    with ctx:
        def sb(name, shape, dt=F32):
            return ctx.enter_context(nc.sbuf_tensor(name, shape, dt))

        x = sb("x", [P, NT, D])
        inner = ExitStack()
        xn_hi = inner.enter_context(nc.sbuf_tensor("xn_hi", [P, KC, TOK], F32R))
        xn_lo = inner.enter_context(nc.sbuf_tensor("xn_lo", [P, KC, TOK], F32R))
        inner.close()
        arena = sb("arena", [P, XN + 2 * HG])
        hj_hi = [sb(f"hj_hi{i}", [P, GW], F32R) for i in range(2)]
        hj_lo = [sb(f"hj_lo{i}", [P, GW], F32R) for i in range(2)]
        raw = sb("raw", [P, SLOT])
        w_hi = [sb(f"w_hi{i}", [P, SLOT], F32R) for i in range(2)]
        w_lo = [sb(f"w_lo{i}", [P, SLOT], F32R) for i in range(2)]
        raw_ada = sb("raw_ada", [P, 2, HB])
        acc = sb("acc", [P, 2, HB])
        gate_row = sb("gate_row", [P, 2, D])
        b_gate = sb("b_gate", [1, D])
        ident = sb("ident", [P, P])
        neg_ident = sb("neg_ident", [64, 64])
        mask = sb("mask", [P, 2, P], BF16)
        ident_bf = sb("ident_bf", [P, P], BF16)
        ones = sb("ones", [P, P])
        cvec = sb("cvec", [P, KC, 2])
        silu_c = sb("silu_c", [P, KC, 2])
        b_col = sb("b_col", [P, DEPTH, 9 * KC])
        nw_col = sb("nw_col", [P, DEPTH, 3, KC])
        mcol = sb("mcol", [P, 4, 4, 2])
        m_scale = sb("m_scale", [P, KC, 2])
        m_shift = sb("m_shift", [P, KC, 2])
        stat = sb("stat", [P, 6, 8])
        convw = sb("convw", [P, DEPTH, HEADS, 9])
        convb = sb("convb", [P, DEPTH, HEADS])
        hn_w = sb("hn_w", [P, DEPTH, HEADS])
        gate_b = sb("gate_b", [P, DEPTH, 16])
        eps = sb("eps", [P, 1])
        ps = ctx.enter_context(nc.psum_tensor("ps", [P, 8, 512], F32))

        def at(off, n):
            return arena[:, off:off + n]

        hid = at(A_H, 2 * HG).rearrange("p (g c w) -> p g c w", g=2, c=FC)
        dummy = at(A_DUMMY, D)

        def ada0(i):
            off = i * KC * HB if i < 3 else A_TRI + 2 * P
            return at(off, KC * HB).rearrange("p (k n) -> p k n", k=KC)

        def ys(i):
            return at(A_YS + i * D, D) if i < 3 else at(A_H + (i - 3) * D, D)

        mixT = hid
        xmT = at(A_XM, HEADS * TOK).rearrange("p (h t) -> p h t", h=HEADS)
        convT = at(A_CONV, HEADS * TOK).rearrange("p (h t) -> p h t", h=HEADS)
        qkv_w = at(A_QKVW, 12 * P).rearrange("p (a h e) -> p a h e", a=3, h=HEADS)
        fmix_w = at(A_FW, 4 * P).rearrange("p (f n) -> p f n", f=4)
        dft_l = at(A_DFT, 8 * SEQ).rearrange("p (t c s) -> p t c s", t=4, c=2)
        dft_c = at(A_DFT + 8 * SEQ, 4 * CTX).rearrange("p (t c s) -> p t c s", t=2, c=2)
        dft_g = at(A_DFTG, 256)
        tri = at(A_TRI, 2 * P).rearrange("p (d t) -> p d t", d=2)
        xab = at(A_XAB, NT * 256).rearrange("p (t n) -> p t n", t=NT)
        ab = at(A_AB, 256)
        place = {"gate": A_GATE, "head": 0}

        def small(n, which="gate", end=XN):
            place[which] += n
            assert place[which] <= end
            return at(place[which] - n, n)

        g16 = small(NT * 16)
        g_abs = small(48).rearrange("p (a h) -> p a h", h=4)
        lfs = small(64).rearrange("p (d k h) -> p d k h", d=2, k=8)
        igs = small(64).rearrange("p (d k h) -> p d k h", d=2, k=8)
        b_tok = small(64)
        r_tok = small(64)
        r_row = small(P)
        cm_row = small(P)
        m_row = small(P)
        d_row = small(P)
        rw_row = small(P)
        p0 = small(6 * 64)
        rmax0, btot0, m0, mprev0, mlast0, dec0 = (p0[0:1, 64 * i:64 * i + 64] for i in range(6))
        cols = small(4)
        dec = small(64)
        em_arg = small(64)
        wi, em, wst = (small(48).rearrange("p (d t h) -> p d t h", d=2, t=NT) for _ in range(3))

        def head(n):
            return small(n, "head", A_CONV)

        qT, kT = head(TOK), head(TOK)
        ktok = head(TOK).rearrange("p (t n) -> p t n", t=NT)
        vtok = head(NT * HV).rearrange("p (t n) -> p t n", t=NT)
        wv = head(NT * HV).rearrange("p (t n) -> p t n", t=NT)
        wt = head(TOK).rearrange("p (t n) -> p t n", t=NT)
        cst = head(NT * HV).rearrange("p (k n) -> p k n", k=NT)
        num = head(NT * HV).rearrange("p (t n) -> p t n", t=NT)
        hsum = head(TOK).rearrange("p (t n) -> p t n", t=NT)
        bn = head(NT * 6).rearrange("p (t n) -> p t n", t=NT)
        mv = head(NT * 2).rearrange("p (t n) -> p t n", t=NT)
        den = head(4 * NT).rearrange("p (a t) -> p a t", a=4)

        S = {}
        for name in (
            "consts pool_consts dve_consts x_in "
            "w_raw w_hi w_lo w_used "
            "ada_raw ada_used acc_first fin_mm fin_read silu_c "
            "silu h_done hj_hi hj_lo "
            "y_sq y_copied std1 x_new std2 rs2 xs xT modded xn_hi xn_done "
            "gate_in out_dma dve act_ms act_ms2 "
            "win_evac mix_const g_abs g_exp g_ln g_lf g_b g_r g_rT g_rmx g_rr g_m g_dec g_bc g_rows g_T g_arg g_w "
            "ab_mm ab_sb xab_mm xab_sb f_mm f_sb conv conv_silu "
            "qkv_mm qkv_sb st_mm mb_mm wt_sb wv_sb cloc_mm cst_sb p_sb io_mm comb hvar hstd hn hnT mix_done"
        ).split():
            S[name] = ctx.enter_context(nc.semaphore("s_" + name))

        S["ada_first"] = [ctx.enter_context(nc.semaphore(f"s_ada_first{i}")) for i in range(4)]
        N_SLOTS = SUBS[-1]["slot"] + SUBS[-1]["in_slots"] + 2 * SUBS[-1]["k_slots"]
        block = ctx.enter_context(nc.Block())

        def in_steps(sub, loop, per):
            n0 = sub["slot"]
            if sub["next"]:
                with loop(4, per[0]) as i:
                    for s in range(4):
                        yield i * 4 + s, i * 4 + (n0 + s), s, i, s
                with loop(3, per[1]) as i:
                    for s in range(2):
                        yield i * 2 + (16 + s), i * 2 + (n0 + 16 + s), s, None, None
            else:
                with loop(FC // 2, per[1]) as i:
                    for s in range(2):
                        yield i * 2 + s, i * 2 + (n0 + s), s, None, None

        def out_steps(sub, g, loop, per):
            k = sub["k_slots"]
            n0 = sub["slot"] + sub["in_slots"] + g * k
            s = 0
            if g == 0 and sub["kind"] == "ffn":
                for i in range(2):
                    for u in range(4):
                        yield i * 4 + u, i * 4 + (n0 + u), i * 4 + u, i, u, None
                s = 8
            while g == 1 and s < min(6, k):
                yield s, n0 + s, s, None, None, s
                s += 1
            pairs = (k - 1 - s) // 2
            if pairs > 1:
                with loop(pairs, per[1]) as i:
                    for u in range(2):
                        yield i * 2 + (s + u), i * 2 + (n0 + s + u), s + u, None, None, None
                s += 2 * pairs
            while s < k:
                yield s, n0 + s, s, None, None, None
                s += 1

        def norm_stages(sub, g):
            return sub["groups"][g] + 3

        def plain_loop(eng):
            return lambda trips, per: eng.Fori(0, trips)

        def mixer_act(act, sub, split_w):
            m, n0 = sub["mix"], sub["slot"]
            outs = tiles_of(sub)
            n_out = sum(sub["groups"])
            ctx_out = n_out == NT
            for s in range(6):
                split_w(n0 + s + 1, (n0 + s + 1) % 2, KC * 16 if s == 5 else SLOT)
                act.wait_ge(S["w_used"], 2 * (n0 + s) + 2 + START)
                for c in range(2):
                    for g in range(2):
                        w = GW if s < 2 else sub["groups"][g] * P
                        if s < 2:
                            dst = xmT[:, 2 * s + c, g * GW:g * GW + w]
                        else:
                            dst = mixT[:, g, 2 * (s - 2) + c, 0:w]
                        ins = nc.scalar.activation(dst, ps[:, (s % 2) * 4 + c * 2 + g, 0:w], ACT.Sigmoid if s >= 4 else ACT.Copy)
                ins.then_inc(S["win_evac"], 1)
            split_w(n0 + 7, (n0 + 7) % 2)
            act.wait_ge(S["g_abs"], m + 1)
            nc.scalar.activation(g_abs, g_abs, ACT.Exp, scale=-1.0).then_inc(S["g_exp"], 1)
            act.wait_ge(S["g_exp"], m + 1)
            nc.scalar.activation(g_abs, g_abs, ACT.Ln, bias=ones[:, 0:1]).then_inc(S["g_ln"], 1)

            def fourier(f):
                k = 4 * m + f
                act.wait_ge(S["ab_mm"], k + 1)
                nc.scalar.activation(ab, ps[:, 0, 0:256], ACT.Copy).then_inc(S["ab_sb"], 1)
                act.wait_ge(S["xab_mm"], k + 1)
                for b in range(n_out // 2):
                    ins = nc.scalar.activation(xab[:, 2 * b:2 * b + 2, :].rearrange("p t n -> p (t n)"), ps[:, 1 + b, :], ACT.Copy)
                ins.then_inc(S["xab_sb"], 1)

            def fourier_out(f):
                k = 4 * m + f
                act.wait_ge(S["f_mm"], k + 1)
                nc.scalar.activation(mixT[:, 0, f, :], ps[:, 4, 0:GW], ACT.Copy)
                ins = nc.scalar.activation(mixT[:, 1, f, 0:P], ps[:, 4, GW:512], ACT.Copy)
                if ctx_out:
                    ins = nc.scalar.activation(mixT[:, 1, f, P:GW], ps[:, 0, 256:512], ACT.Copy)
                ins.then_inc(S["f_sb"], 1)

            def conv_silu(h):
                act.wait_ge(S["conv"], 4 * m + h + 1)
                nc.scalar.activation(convT[:, h, :], convT[:, h, :], ACT.Silu).then_inc(S["conv_silu"], 1)

            fourier(0)
            fourier_out(0)
            fourier(1)
            fourier_out(1)
            act.wait_ge(S["g_m"], m + 1)
            nc.scalar.activation(dec0, dec0, ACT.Exp).then_inc(S["g_dec"], 1)
            fourier(2)
            fourier_out(2)
            act.wait_ge(S["g_arg"], m + 1)
            em_v = em_arg.rearrange("p (d k h) -> p d k h", d=2, k=8)
            t_v = ps[:, 7, 0:192].rearrange("p (a d k h) -> p a d k h", a=3, d=2, k=8)
            for dst, src in ((em, em_v), (wi, t_v[:, 1]), (wst, t_v[:, 2])):
                nc.scalar.activation(dst[:, 0, 0:4, :], src[:, 0, 2:6, :], ACT.Exp)
                nc.scalar.activation(dst[:, 0, 4:6, :], src[:, 0, 0:2, :], ACT.Exp)
                ins = nc.scalar.activation(dst[:, 1, 0:6, :], src[:, 1, 5::-1, :], ACT.Exp)
            ins.then_inc(S["g_w"], 1)
            fourier(3)
            fourier_out(3)
            for h in range(HEADS):
                conv_silu(h)
            for h in range(HEADS):
                mh = 4 * m + h
                scale_k = float(HD) ** -0.5
                for a, dst, b0 in ((0, qT, 0), (1, kT, 2), (2, ktok, 4), (3, vtok, 6)):
                    act.wait_ge(S["qkv_mm"], 4 * mh + a + 1)
                    for g in range(2):
                        w = outs[g] if a == 0 else [0] * GT
                        w = len(w) * P
                        src = ps[:, b0 + g, 0:w]
                        if a < 2:
                            d_ = dst[:, g * GW:g * GW + w]
                        else:
                            d_ = dst[:, g * GT:(g + 1) * GT, 0:HD]
                            src = src.rearrange("p (t n) -> p t n", n=P)
                        ins = nc.scalar.activation(d_, src, ACT.Copy, scale=scale_k if a in (1, 2) else 1.0)
                    ins.then_inc(S["qkv_sb"], 1)
                for d in range(2):
                    md = 2 * mh + d
                    act.wait_ge(S["mb_mm"], md + 1)
                    if md:
                        act.wait_ge(S["io_mm"], md)
                    for t in outs[0] + outs[1]:
                        col = scan_col(d, scan_k(d, t), h)
                        ins = nc.scalar.activation(wt[:, t, :], ps[:, 2 + t // GT, (t % GT) * P:(t % GT + 1) * P], ACT.Exp,
                                                   bias=r_tok[:, col:col + 1])
                    ins.then_inc(S["wt_sb"], 1)
                act.wait_ge(S["hvar"], mh + 1)
                nc.scalar.activation(den[:, 0, 0:n_out], mv[:, 0:n_out, 1], ACT.Sqrt, bias=eps[:, 0:1]).then_inc(S["hstd"], 1)

        def mixer_dve(dve, own, sub, split_w, unit, finish_col, finish_gate):
            m, n0, l = sub["mix"], sub["slot"], sub["l"]
            u0, half0 = sub["unit"], sub["half"]
            nl, nj = sub["next"]
            outs = tiles_of(sub)
            n_out = sum(sub["groups"])
            link = own.link
            for s in range(6):
                split_w(n0 + s + 1, (n0 + s + 1) % 2, KC * 16 if s == 5 else SLOT)
                for u in range(4):
                    unit(u0 + 4 * s + u, u)
                if s < 4:
                    finish_col(half0 + s, s, 3 * nj * KC, nl, 4 * ((s + 1) % 2))
                else:
                    finish_gate(half0 + s, s - 4, 4 if s == 4 else 0, 1.0, sub)
            split_w(n0 + 7, (n0 + 7) % 2)
            dve.wait_ge(S["w_used"], 2 * (n0 + 7) + START)
            gv = g16.rearrange("p (a b h) -> p a b h", b=2, h=4)
            link(nc.vector.tensor_tensor(g16.rearrange("p (t j) -> p t j", t=NT), ps[:, 5, 0:96].rearrange("p (t j) -> p t j", t=NT),
                                         gate_b[:, l, :].unsqueeze(1).to_broadcast([P, NT, 16]), ALU.add))
            nc.vector.scalar_tensor_tensor(out=g_abs, in0=gv[:, :, 1, :], scalar=-1.0, in1=gv[:, :, 1, :], op0=ALU.mult,
                                           op1=ALU.max).then_inc(S["g_abs"], 1)
            nc.vector.memset(lfs, 0.0)
            link(nc.vector.memset(igs, 0.0))
            g5 = g16.rearrange("p (t d b h) -> p t d b h", t=NT, d=2, b=2)
            a4 = g_abs.rearrange("p (t d) h -> p t d h", d=2)
            dve.wait_ge(S["g_ln"], m + 1)
            for d, dst, src in ((0, slice(2, 6), slice(0, 4)), (0, slice(0, 2), slice(4, 6)), (1, slice(0, 6), slice(5, None, -1))):
                nc.vector.tensor_copy(igs[:, d, dst, :], g5[:, src, d, 0, :])
                ins = nc.vector.scalar_tensor_tensor(out=lfs[:, d, dst, :], in0=g5[:, src, d, 1, :], scalar=0.0,
                                                     in1=a4[:, src, d, :], op0=ALU.min, op1=ALU.subtract)
            ins.then_inc(S["g_lf"], 1)

            def conv(h):
                src = xmT[:, h, 0:SEQ].rearrange("p (r c) -> p r c", c=64)
                dst = convT[:, h, 0:SEQ].rearrange("p (r c) -> p r c", c=64)
                csrc, cdst = xmT[:, h, SEQ:TOK], convT[:, h, SEQ:TOK]
                w = convw[:, l, h, :]
                nc.vector.tensor_scalar(convT[:, h, 0:SEQ], xmT[:, h, 0:SEQ], w[:, 4:5], convb[:, l, h:h + 1], ALU.mult, ALU.add)
                link(nc.vector.tensor_scalar(cdst, csrc, w[:, 4:5], convb[:, l, h:h + 1], ALU.mult, ALU.add))

                def tap(o, s, k):
                    return nc.vector.scalar_tensor_tensor(out=o, in0=s, scalar=w[:, k:k + 1], in1=o, op0=ALU.mult, op1=ALU.add)

                R, C = SEQ // 64, 64
                for dy in (-1, 0, 1):
                    for dx in (-1, 0, 1):
                        if dy == 0 and dx == 0:
                            continue
                        r0, r1 = max(0, -dy), R - max(0, dy)
                        c0, c1 = max(0, -dx), C - max(0, dx)
                        link(tap(dst[:, r0:r1, c0:c1], src[:, r0 + dy:r1 + dy, c0 + dx:c1 + dx], (dy + 1) * 3 + dx + 1))
                link(tap(cdst[:, 1:CTX], csrc[:, 0:CTX - 1], 3))
                tap(cdst[:, 0:CTX - 1], csrc[:, 1:CTX], 5).then_inc(S["conv"], 1)

            conv(0)
            dve.wait_ge(S["g_b"], m + 1)
            nc.vector.tensor_copy(b_tok, ps[:, 6, 0:64])
            nc.vector.tensor_copy(btot0, ps[0:1, 6, 64:128])
            nc.vector.tensor_tensor(r_tok, igs.rearrange("p d k h -> p (d k h)"), ps[:, 6, 0:64], ALU.subtract).then_inc(S["g_r"], 1)
            conv(1)
            dve.wait_ge(S["g_rT"], m + 1)
            link(nc.vector.tensor_copy(r_row[0:64], ps[0:64, 6, P:2 * P]))
            nc.vector.tensor_reduce(cols[0:64, 2:3], r_row[0:64], AX_X, ALU.max).then_inc(S["g_rmx"], 1)
            nc.vector.tensor_tensor_scan(cm_row[0:32], r_row[0:32], r_row[0:32], NEG, ALU.max, ALU.max)
            nc.vector.tensor_tensor_scan(cm_row[32:64, P - 1::-1], r_row[32:64, P - 1::-1], r_row[32:64, P - 1::-1], NEG, ALU.max, ALU.max)
            conv(2)
            dve.wait_ge(S["g_rr"], m + 1)
            link(nc.vector.tensor_copy(rmax0, ps[0:1, 6, 256:320]))
            link(nc.vector.memset(mprev0, 0.0))
            for d in range(2):
                for h in range(HEADS):
                    sl = slice(d * 32 + h, d * 32 + h + 21, 4)
                    ins = nc.vector.tensor_tensor_scan(m0[:, sl], rmax0[:, sl], btot0[:, sl], 0.0, ALU.max, ALU.add)
            link(ins)
            v8 = lambda a: a.rearrange("p (d c) -> p d c", d=2)
            link(nc.vector.tensor_copy(v8(mprev0)[:, :, 4:24], v8(m0)[:, :, 0:20]))
            link(nc.vector.tensor_tensor(mlast0, mprev0, rmax0, ALU.max))
            nc.vector.tensor_tensor(dec0, mprev0, mlast0, ALU.subtract).then_inc(S["g_m"], 1)
            conv(3)
            dve.wait_ge(S["g_bc"], m + 1)
            nc.vector.tensor_copy(dec, ps[:, 6, 384:448])
            link(nc.vector.tensor_copy(cols[0:64, 0:2], ps[0:64, 6, 320:322]))
            link(nc.vector.tensor_scalar(m_row[0:64], cm_row[0:64], cols[0:64, 0:1], None, ALU.max))
            nc.vector.tensor_scalar(d_row[0:64], m_row[0:64], -1.0, cols[0:64, 0:1], ALU.mult, ALU.add)
            nc.vector.tensor_scalar(rw_row[0:64], r_row[0:64], cols[0:64, 1:2], None, ALU.subtract).then_inc(S["g_rows"], 1)
            dve.wait_ge(S["g_T"], m + 1)
            nc.vector.scalar_tensor_tensor(out=em_arg, in0=ps[:, 7, 0:64], scalar=-1.0, in1=b_tok, op0=ALU.mult,
                                           op1=ALU.subtract).then_inc(S["g_arg"], 1)
            dve.wait_ge(S["xab_mm"], 4 * m + 4)
            dve.wait_ge(S["f_mm"], 4 * m + 4)
            link(nc.vector.memset(vtok[:, :, HD:HV], 1.0))
            dve.wait_ge(S["g_w"], m + 1)
            for h in range(HEADS):
                mh = 4 * m + h
                for d in range(2):
                    md = 2 * mh + d
                    if d == 0:
                        dve.wait_ge(S["qkv_sb"], 4 * mh + 4)
                    if md:
                        dve.wait_ge(S["io_mm"], md)
                    nc.vector.tensor_tensor(wv, vtok, wst[:, d, :, h].unsqueeze(2).to_broadcast([P, NT, HV]), ALU.mult).then_inc(S["wv_sb"], 1)
                    link(nc.vector.memset(cst[:, 0, :], 0.0))
                    dve.wait_ge(S["cloc_mm"], md + 1)
                    for k in range(NT - 1):
                        col = scan_col(d, k, h)
                        ins = nc.vector.scalar_tensor_tensor(out=cst[:, k + 1, :], in0=cst[:, k, :], scalar=dec[:, col:col + 1],
                                                             in1=ps[:, 4 + k // 3, (k % 3) * HV:(k % 3 + 1) * HV],
                                                             op0=ALU.mult, op1=ALU.add)
                        if k < NT - 2:
                            link(ins)
                    ins.then_inc(S["cst_sb"], 1)
                    dve.wait_ge(S["wt_sb"], md + 1)
                    dve.wait_ge(S["st_mm"], mh + 1)
                    for g in range(2):
                        nt = len(outs[g])
                        wg = wt[:, g * GT:g * GT + nt, :].rearrange("p t n -> p (t n)")
                        ins = nc.vector.tensor_tensor(wg, wg, ps[:, g, 0:nt * P], ALU.mult)
                    ins.then_inc(S["p_sb"], 1)
                    dve.wait_ge(S["io_mm"], md + 1)
                    for g in range(2):
                        nt = len(outs[g])
                        sl = slice(g * GT, g * GT + nt)
                        ng = num[:, sl, :]
                        link(nc.vector.tensor_tensor(ng, ps[:, 2 + g, 0:nt * HV].rearrange("p (t n) -> p t n", n=HV),
                                                     wi[:, d, sl, h].unsqueeze(2).to_broadcast([P, nt, HV]), ALU.mult))
                        ins = nc.vector.tensor_tensor(ng, ng, ps[:, 6 + g, 0:nt * HV].rearrange("p (t n) -> p t n", n=HV), ALU.add)
                        if g == 0:
                            own.mark(ins)
                    ins.then_inc(S["comb"], 1)
                    dve.wait_ge(S["comb"], md + 1)
                    dn = num[:, 0:n_out, HD]
                    link(nc.vector.scalar_tensor_tensor(out=den[:, 1, 0:n_out], in0=dn, scalar=-1.0, in1=dn, op0=ALU.mult, op1=ALU.max))
                    link(nc.vector.tensor_tensor(den[:, 2, 0:n_out], den[:, 1, 0:n_out], em[:, d, 0:n_out, h], ALU.max))
                    link(nc.vector.reciprocal(den[:, 3, 0:n_out], den[:, 2, 0:n_out]))
                    rd = den[:, 3, 0:n_out].unsqueeze(2).to_broadcast([P, n_out, HD])
                    if d == 0:
                        link(nc.vector.tensor_tensor(hsum[:, 0:n_out, :], num[:, 0:n_out, 0:HD], rd, ALU.mult))
                    else:
                        link(nc.vector.tensor_tensor(num[:, 0:n_out, 0:HD], num[:, 0:n_out, 0:HD], rd, ALU.mult))
                        link(nc.vector.tensor_tensor(hsum[:, 0:n_out, :], hsum[:, 0:n_out, :], num[:, 0:n_out, 0:HD], ALU.add))
                for t in range(n_out):
                    ins = nc.vector.bn_stats(bn[:, t, :], hsum[:, t, :])
                link(ins)
                for t in range(n_out):
                    ins = nc.vector.bn_aggr(mv[:, t, :], bn[:, t, :])
                ins.then_inc(S["hvar"], 1)
                dve.wait_ge(S["hstd"], mh + 1)
                link(nc.vector.reciprocal(den[:, 1, 0:n_out], den[:, 0, 0:n_out]))
                for t in range(n_out):
                    ins = nc.vector.tensor_scalar(hsum[:, t, :], hsum[:, t, :], mv[:, t, 0:1], den[:, 1, t:t + 1], ALU.subtract, ALU.mult)
                ins.then_inc(S["hn"], 1)
                dve.wait_ge(S["hnT"], mh + 1)
                for g in range(2):
                    w = len(outs[g]) * P
                    mg = mixT[:, g, 4 + h, 0:w]
                    ins = nc.vector.scalar_tensor_tensor(out=mg, in0=ps[:, g, 0:w], scalar=hn_w[:, l, h:h + 1], in1=mg,
                                                         op0=ALU.mult, op1=ALU.mult)
                ins.then_inc(S["mix_done"], 1)

        def mixer_pe(pe, sub, project_in, finish_col, finish_gate):
            mm = nc.tensor.matmul
            m, n0 = sub["mix"], sub["slot"]
            u0, half0 = sub["unit"], sub["half"]
            outs = tiles_of(sub)
            n_out = sum(sub["groups"])
            ctx_out = n_out == NT
            for s in range(6):
                if s >= 2:
                    pe.wait_ge(S["win_evac"], 6 * m + s - 1)
                if s == 5:
                    pe.wait_ge(S["fin_read"], half0 + 5)
                project_in(n0 + s, (n0 + s) % 2, s % 2, [GT, GT] if s < 2 else sub["groups"])
                if s < 4:
                    finish_col(half0 + s, u0 + 4 * s + 4, 4 * ((s + 1) % 2))
                    pe.wait_ge(S["fin_read"], half0 + s + 1)
                else:
                    pe.wait_ge(S["win_evac"], 6 * m + s)
                    finish_gate(half0 + s, u0 + 4 * s + 4, s - 4, 4 if s == 4 else 0, sub)
            n = n0 + 6
            pe.wait_ge(S["w_lo"], n + 1 + START)
            pe.wait_ge(S["win_evac"], 6 * m + 6)
            hi = w_hi[n % 2][:, 0:KC * 16].rearrange("p (k j) -> p k j", k=KC)
            lo = w_lo[n % 2][:, 0:KC * 16].rearrange("p (k j) -> p k j", k=KC)
            for t in range(NT):
                for k in range(KC):
                    for i, (xx, w) in enumerate(((xn_hi, hi), (xn_hi, lo), (xn_lo, hi))):
                        ins = mm(ps[:, 5, t * 16:t * 16 + 16], xx[:, k, t * P:(t + 1) * P], w[:, k, :],
                                 start=(k == 0 and i == 0), stop=(k == KC - 1 and i == 2))
            ins.then_inc(S["w_used"], 2)

            def tile_of(a, t):
                return a[:, t // GT, :, (t % GT) * P:(t % GT + 1) * P]

            def fourier(f):
                k = 4 * m + f
                if k:
                    pe.wait_ge(S["f_sb"], k)
                if f == 0:
                    pe.wait_ge(S["mix_const"], 96 * (m + 1))
                    pe.wait_ge(S["fin_read"], half0 + 6)
                mm(ps[:, 0, 0:P], dft_g[:, 0:P], fmix_w[:, f, :], start=True, stop=True)
                mm(ps[:, 0, P:2 * P], dft_g[:, P:2 * P], fmix_w[:, f, :], start=True, stop=True).then_inc(S["ab_mm"], 1)
                pe.wait_ge(S["ab_sb"], k + 1)
                for t in range(n_out):
                    ins = mm(ps[:, 1 + t // 2, (t % 2) * 256:(t % 2) * 256 + 256], tile_of(mixT, t)[:, f, :], ab, start=True, stop=True)
                ins.then_inc(S["xab_mm"], 1)

            def fourier_out(f):
                k = 4 * m + f
                pe.wait_ge(S["xab_sb"], k + 1)
                for t in range(NTL):
                    for c in range(2):
                        ins = mm(ps[:, 4, :], xab[:, t, c * P:(c + 1) * P], dft_l[:, t, c, :], start=(t == 0 and c == 0),
                                 stop=(t == NTL - 1 and c == 1))
                if ctx_out:
                    for t in range(2):
                        for c in range(2):
                            ins = mm(ps[:, 0, 256:512], xab[:, NTL + t, c * P:(c + 1) * P], dft_c[:, t, c, :],
                                     start=(t == 0 and c == 0), stop=(t == 1 and c == 1))
                ins.then_inc(S["f_mm"], 1)

            fourier(0)
            pe.wait_ge(S["g_lf"], m + 1)
            for d in range(2):
                mm(ps[:, 6, 32 * d:32 * d + 32], tri[:, d, :], lfs[:, d].rearrange("p k h -> p (k h)"), start=True, stop=True)
            mm(ps[0:1, 6, 64:128], ones[:, 0:1], lfs.rearrange("p d k h -> p (d k h)"), start=True, stop=True).then_inc(S["g_b"], 1)
            fourier_out(0)
            pe.wait_ge(S["g_r"], m + 1)
            nc.tensor.transpose(ps[0:64, 6, P:2 * P], r_tok, ident[:]).then_inc(S["g_rT"], 1)
            fourier(1)
            pe.wait_ge(S["g_rmx"], m + 1)
            mm(ps[0:1, 6, 256:320], cols[0:64, 2:3], ident[0:64, 0:64], start=True, stop=True).then_inc(S["g_rr"], 1)
            fourier_out(1)
            pe.wait_ge(S["g_dec"], m + 1)
            mm(ps[0:64, 6, 320:321], mprev0, ones[0:1, 0:1], start=True, stop=True)
            mm(ps[0:64, 6, 321:322], mlast0, ones[0:1, 0:1], start=True, stop=True)
            mm(ps[:, 6, 384:448], ones[0:1, :], dec0, start=True, stop=True).then_inc(S["g_bc"], 1)
            fourier(2)
            pe.wait_ge(S["g_rows"], m + 1)
            for i, row in enumerate((m_row, d_row, rw_row)):
                ins = nc.tensor.transpose(ps[:, 7, 64 * i:64 * i + 64], row[0:64], ident[0:64, 0:64])
            ins.then_inc(S["g_T"], 1)
            fourier_out(2)
            fourier(3)
            fourier_out(3)

            for h in range(HEADS):
                mh = 4 * m + h
                if h == 0:
                    pe.wait_ge(S["f_sb"], 4 * m + 4)
                    pe.wait_ge(S["g_w"], m + 1)
                    pe.wait_ge(S["conv_silu"], 4 * m + 4)
                else:
                    pe.wait_ge(S["mix_done"], mh)
                for a in range(4):
                    if a < 2:
                        for g in range(2):
                            w = (len(outs[g]) if a == 0 else GT) * P
                            ins = mm(ps[:, 2 * a + g, 0:w], qkv_w[:, a, h, :], convT[:, h, g * GW:g * GW + w], start=True, stop=True)
                    else:
                        for t in range(NT):
                            src = (convT if a == 2 else xmT)[:, h, t * P:(t + 1) * P]
                            ins = mm(ps[:, 2 * a + t // GT, (t % GT) * P:(t % GT + 1) * P], src, qkv_w[:, a - 1, h, :], start=True, stop=True)
                    ins.then_inc(S["qkv_mm"], 1)
                pe.wait_ge(S["qkv_sb"], 4 * mh + 2)
                for t in outs[0] + outs[1]:
                    sl = slice(t * P, (t + 1) * P)
                    ins = mm(ps[:, t // GT, (t % GT) * P:(t % GT + 1) * P], kT[:, sl], qT[:, sl], start=True, stop=True)
                ins.then_inc(S["st_mm"], 1)
                for d in range(2):
                    md = 2 * mh + d
                    if d == 1:
                        pe.wait_ge(S["comb"], md)
                    for g in range(2):
                        nt = len(outs[g])
                        mm(ps[:, 2 + g, 0:nt * P], ident_bf[:], mask[:, d, :].unsqueeze(1).to_broadcast([P, nt, P]), start=True, stop=False)
                        for i, t in enumerate(outs[g]):
                            col = scan_col(d, scan_k(d, t), h)
                            ins = mm(ps[:, 2 + g, i * P:(i + 1) * P], neg_ident[0:64, col:col + 1].to_broadcast([64, P]), m_row[0:64],
                                     start=False, stop=(i == nt - 1))
                    ins.then_inc(S["mb_mm"], 1)
                    pe.wait_ge(S["wv_sb"], md + 1)
                    pe.wait_ge(S["qkv_sb"], 4 * mh + 4)
                    for k in range(NT - 1):
                        t = scan_t(d, k)
                        ins = mm(ps[:, 4 + k // 3, (k % 3) * HV:(k % 3 + 1) * HV], ktok[:, t, :], wv[:, t, :], start=True, stop=True)
                    ins.then_inc(S["cloc_mm"], 1)
                    pe.wait_ge(S["p_sb"], md + 1)
                    pe.wait_ge(S["cst_sb"], md + 1)
                    for t in outs[0] + outs[1]:
                        g, i = t // GT, t % GT
                        mm(ps[:, 6 + g, i * HV:(i + 1) * HV], wt[:, t, :], vtok[:, t, :], start=True, stop=True)
                        ins = mm(ps[:, 2 + g, i * HV:(i + 1) * HV], qT[:, t * P:(t + 1) * P], cst[:, scan_k(d, t), :], start=True, stop=True)
                    ins.then_inc(S["io_mm"], 1)
                pe.wait_ge(S["hn"], mh + 1)
                for t in range(n_out):
                    ins = nc.tensor.transpose(ps[:, t // GT, (t % GT) * P:(t % GT + 1) * P], hsum[:, t, :], ident[:])
                ins.then_inc(S["hnT"], 1)
            pe.wait_ge(S["mix_done"], HEADS * (m + 1))

        @block.sync
        def _(sp):
            loop = plain_loop(sp)

            def load(n, src, width=SLOT):
                if not isinstance(n, int) or n > 0:
                    sp.wait_ge(S["w_lo"], n + START)
                sp.dma_start(raw[:, 0:width], src).then_inc(S["w_raw"], 16)

            def unit(count, l, col, u):
                sp.wait_ge(S["ada_used"], count + START)
                src = w_ada[l].rearrange("(u c p) n -> u p c n", c=2, p=P)[u, :, :, bass.ds(col, HB)]
                sp.dma_start(raw_ada[:], src).then_inc(S["ada_raw"], 16)

            for dst, src in ((cvec[:], cvec_in), (b_col[:], b_col_in), (nw_col[:], nw_col_in), (convw[:], convw_in),
                             (convb[:], convb_in), (hn_w[:], hn_w_in), (tri, tri_in), (gate_b[:], gate_b_in)):
                sp.dma_start(dst, src).then_inc(S["consts"], 16)
            for i in range(4):
                src = w_ada[0].rearrange("(k p) n -> p k n", p=P)[:, :, i * HB:(i + 1) * HB]
                sp.dma_start(ada0(i), src).then_inc(S["ada_first"][i], 16)

            for sub in SUBS:
                l, j, n0 = sub["l"], sub["j"], sub["slot"]
                u0 = sub["unit"]
                if sub["kind"] == "ffn":
                    for f, n, s, half, u in in_steps(sub, loop, (0, 0)):
                        load(n, w_ff_in[l, j // 2, f])
                        if half is not None:
                            nl, nj = sub["next"]
                            unit(half * 4 + (u0 + u), nl, half * HB + 3 * nj * D, u)
                    w = w_ff_out[l, j // 2].rearrange("(s c p) n -> s p c n", c=2, p=P)
                    u0 += 16 if sub["next"] else 0
                else:
                    nl, nj = sub["next"]
                    for s in range(7):
                        src = w_in[l].rearrange("(k p) n -> p k n", p=P)
                        c0 = (D // 2, 3 * D // 4, 0, D // 4, D, 5 * D // 4)[s % 6]
                        if s < 6:
                            sp.wait_ge(S["w_lo"], n0 + s + START)
                            sp.dma_start(raw[:].rearrange("p (k n) -> p k n", k=KC), src[:, :, c0:c0 + 256]).then_inc(S["w_raw"], 16)
                        else:
                            load(n0 + 6, w_gates[l], KC * 16)
                        if s >= 1:
                            for u in range(4):
                                col = (3 * nj * D + (s - 1) * HB) if s <= 4 else (3 * j + 2) * D + (s - 5) * HB
                                unit(u0 + 4 * (s - 1) + u, nl if s <= 4 else l, col, u)
                    w = w_out[l].rearrange("(s c p) n -> s p c n", c=2, p=P)
                for g in range(2):
                    for s, n, par, half, u, st in out_steps(sub, g, loop, (0, 0)):
                        sp.wait_ge(S["w_lo"], n + START)
                        sp.dma_start(raw[:].rearrange("p (c n) -> p c n", c=2), w[s]).then_inc(S["w_raw"], 16)
                        if half is not None:
                            unit(half * 4 + (u0 + u), l, half * HB + (3 * j + 2) * D, u)
            for p_ in range(NTL):
                sp.wait_ge(S["x_new"], SUBS[-1]["y"] + p_ + 1)
                sp.dma_start(out[p_], x[:, p_, :]).then_inc(S["out_dma"], 16)
            sp.wait_ge(S["out_dma"], 16 * NTL)

        @block.gpsimd
        def _(pool):
            nc.gpsimd.memset(ones[:], 1.0)
            nc.gpsimd.memset(eps[:], EPS)
            nc.gpsimd.memset(ident[:], 0.0).then_inc(S["pool_consts"], 1)
            pool.wait_ge(S["pool_consts"], 1)
            nc.gpsimd.affine_select(out=ident[:], in_=ident[:], compare_op=ALU.not_equal, fill=1.0, base=0,
                                    pattern=[[-1, P]], channel_multiplier=1).then_inc(S["pool_consts"], 1)

        @block.scalar
        def _(act):
            loop = plain_loop(act)

            def split_w(n, par, width=SLOT):
                if isinstance(n, int) and n >= N_SLOTS:
                    return
                act.wait_ge(S["w_raw"], n * 16 + 16)
                if not isinstance(n, int) or n >= 2:
                    act.wait_ge(S["w_used"], n * 2 - 2 + START)
                nc.scalar.activation(w_hi[par][:, 0:width], raw[:, 0:width], ACT.Copy).then_inc(S["w_hi"], 1)

            def hj(sub, g, c, hs, b):
                w = sub["groups"][g] * P
                if g == 0:
                    if sub["kind"] == "ffn":
                        act.wait_ge(S["h_done"], c + (sub["proj"] + 1 + FREE))
                    else:
                        act.wait_ge(S["mix_done"], HEADS * (sub["mix"] + 1))
                act.wait_ge(S["w_used"], hs - 1 + START)
                src = hid[:, g, c, 0:w] if isinstance(c, int) else hid[:, g, bass.ds(c, 1), 0:w].rearrange("p a w -> p (a w)")
                nc.scalar.activation(hj_hi[b][:, 0:w], src, ACT.Copy).then_inc(S["hj_hi"], 1)

            def stage(sub, g, s):
                tiles, y0, x0 = tiles_of(sub)[g], sub["y"] + g * GT, sub["xn"] + g * GT
                if 0 <= s - 3 < len(tiles) and not sub["final"]:
                    prenorm_split(x0 + s - 3, tiles[s - 3])
                if 0 <= s - 1 < len(tiles) and not sub["final"]:
                    prenorm_scale(x0 + s - 1, tiles[s - 1], s - 1)
                if 0 <= s < len(tiles):
                    act.wait_ge(S["y_sq"], y0 + s + 1)
                    nc.scalar.activation(stat[:, s, 1:2], stat[:, s, 0:1], ACT.Sqrt, bias=eps[:, 0:1]).then_inc(S["std1"], 1)
                    if not sub["final"]:
                        act.wait_ge(S["x_new"], y0 + s + 1)
                        prenorm_stat(x0 + s, tiles[s], s)

            def prenorm_stat(xi, t, i):
                nc.scalar.activation(dummy, x[:, t, :], ACT.Square, scale=1.0 / 32,
                                     accum_out=stat[:, i, 3:4]).then_inc(S["act_ms2"], 1)
                act.wait_ge(S["act_ms2"], xi + 1)
                nc.scalar.activation(stat[:, i, 4:5], stat[:, i, 3:4], ACT.Sqrt, bias=eps[:, 0:1]).then_inc(S["std2"], 1)

            def prenorm_scale(xi, t, i):
                act.wait_ge(S["rs2"], xi + 1)
                nc.scalar.activation(ys(i), x[:, t, :], ACT.Copy, scale=stat[:, i, 5:6]).then_inc(S["xs"], 1)

            def prenorm_split(xi, t):
                act.wait_ge(S["modded"], xi + 1)
                nc.scalar.activation(xn_hi[:, :, t * P:(t + 1) * P], ps[:, 6:8, :].rearrange("p b (c w) -> p (b c) w", w=P),
                                     ACT.Copy).then_inc(S["xn_hi"], 1)

            def evacuate(sub, g):
                for i in range(sub["groups"][g]):
                    act.wait_ge(S["y_copied"], sub["y"] + g * GT + i + 1)
                    nc.scalar.activation(dummy, ys(i), ACT.Square, scale=1.0 / 32, accum_out=stat[:, i, 0:1]).then_inc(S["y_sq"], 1)
                    act.wait_ge(S["y_sq"], sub["y"] + g * GT + i + 1)

            def load_constants(sub):
                l, j = sub["l"], sub["j"]
                if sub["y"]:
                    act.wait_ge(S["x_new"], sub["y"])
                nw = norm_w[l, 2 * j + 1:2 * j + 2, :]
                for s in range(2):
                    act.dma_start(gate_row[:, s, :], nw.to_broadcast([P, D])).then_inc(S["gate_in"], 16)
                act.dma_start(b_gate[:], b_ada[l:l + 1, (3 * j + 2) * D:(3 * j + 3) * D]).then_inc(S["gate_in"], 16)
                if sub["kind"] == "mix":
                    act.wait_ge(S["xn_done"], sub["xn"])
                    act.dma_start(qkv_w, w_qkv[l].rearrange("a h d e -> d a h e")).then_inc(S["mix_const"], 16)
                    for dst, src in ((fmix_w, fmix_in[l]), (dft_l, dft_l_in), (dft_c, dft_c_in), (dft_g, dft_g_in), (tri, tri_in)):
                        act.dma_start(dst, src).then_inc(S["mix_const"], 16)

            for t in range(NT):
                act.dma_start(x[:, t, :], x_in[t]).then_inc(S["x_in"], 16)
            act.wait_ge(S["consts"], 16 * 8)
            nc.scalar.activation(silu_c[:], cvec[:], ACT.Silu).then_inc(S["silu_c"], 1)
            act.wait_ge(S["x_in"], 16 * NT)
            act.wait_ge(S["pool_consts"], 2)
            for t in range(NT):
                prenorm_stat(t, t, t)
            for t in range(NT):
                prenorm_scale(t, t, t)
            split_w(0, 0)
            for t in range(NT):
                prenorm_split(t, t)

            for sub in SUBS:
                l, j, n0 = sub["l"], sub["j"], sub["slot"]
                par0 = n0 % 2
                load_constants(sub)
                if sub["kind"] == "ffn":
                    for f, n, s, half, u in in_steps(sub, loop, (0, 0)):
                        split_w(n + 1, (par0 + s + 1) % 2)
                        act.wait_ge(S["w_used"], n * 2 + 2 + START)
                        for g in range(2):
                            w = sub["in_groups"][g] * P
                            dst = hid[:, g, bass.ds(f, 1), 0:w].rearrange("p a w -> p (a w)")
                            ins = nc.scalar.activation(dst, ps[:, (s % 2) * 4 + g, 0:w], ACT.Silu)
                        ins.then_inc(S["silu"], 1)
                else:
                    mixer_act(act, sub, split_w)
                for g in range(2):
                    nb = n0 + sub["in_slots"] + g * sub["k_slots"]
                    pb = nb % 2
                    hj(sub, g, 0, 2 * nb, 0)
                    if g == 1:
                        evacuate(sub, 0)
                    done = 0
                    for s, n, par, half, u, st in out_steps(sub, g, loop, (0, 0)):
                        hj(sub, g, s * 2 + 1, n * 2 + 1, 1)
                        split_w(n + 1, (pb + par + 1) % 2)
                        if not (isinstance(s, int) and s == sub["k_slots"] - 1):
                            hj(sub, g, s * 2 + 2, n * 2 + 2, 0)
                        if st is not None:
                            stage(sub, 0, st)
                            done = st + 1
                for s in range(done, norm_stages(sub, 0)):
                    stage(sub, 0, s)
                evacuate(sub, 1)
                for s in range(norm_stages(sub, 1)):
                    stage(sub, 1, s)

        @block.vector
        def _(dve):
            own = Count(dve, S["dve"])
            dve.sem_inc(S["w_lo"], START)
            dve.sem_inc(S["ada_used"], START)

            def split_w(n, par, width=SLOT):
                if isinstance(n, int) and n >= N_SLOTS:
                    return
                dve.wait_ge(S["w_hi"], n + 1)
                if not isinstance(n, int) or n >= 2:
                    dve.wait_ge(S["w_used"], n * 2 - 2 + START)
                nc.vector.tensor_tensor(w_lo[par][:, 0:width], raw[:, 0:width], w_hi[par][:, 0:width].bitcast(F32),
                                        ALU.subtract).then_inc(S["w_lo"], 1)

            def hj(sub, g, c, q, hs, b):
                w = sub["groups"][g] * P
                dve.wait_ge(S["hj_hi"], q + 1)
                dve.wait_ge(S["w_used"], hs - 1 + START)
                src = hid[:, g, c, 0:w] if isinstance(c, int) else hid[:, g, bass.ds(c, 1), 0:w].rearrange("p a w -> p (a w)")
                nc.vector.tensor_tensor(hj_lo[b][:, 0:w], src, hj_hi[b][:, 0:w].bitcast(F32), ALU.subtract).then_inc(S["hj_lo"], 1)

            def unit(count, u):
                if u == 0:
                    own.link(nc.vector.memset(acc[:], 0.0))
                dve.wait_ge(S["ada_raw"], count * 16 + 16)
                for c in range(2):
                    for s in range(2):
                        k = 2 * u + c
                        if c == 1:
                            own.wait_back(1)
                        elif u and s == 0:
                            own.wait_back(0)
                        elif u:
                            dve.wait_ge(S["ada_used"], count + START)
                        ins = nc.vector.scalar_tensor_tensor(out=acc[:, s, :], in0=raw_ada[:, c, :], scalar=silu_c[:, k, s:s + 1],
                                                             in1=acc[:, s, :], op0=ALU.mult, op1=ALU.add)
                        if c == 1 and s == 1:
                            ins.then_inc(S["ada_used"], 1)
                        else:
                            own.mark(ins)

            def finish_col(half, i, b_off, l, bank_):
                dve.wait_ge(S["fin_mm"], half + 1)
                bias = b_col[:, l, bass.ds(i * 4 + b_off, 4)].unsqueeze(2).to_broadcast([P, 4, 2])
                dst = mcol[:, bass.ds(i, 1), :, :].rearrange("p a c s -> p (a c) s")
                nc.vector.tensor_tensor(dst, ps[:, bank_, GW:GW + 8].rearrange("p (c s) -> p c s", s=2), bias,
                                        ALU.add).then_inc(S["fin_read"], 1)

            def finish_gate(half, i, b0, factor, sub):
                dve.wait_ge(S["fin_mm"], half + 1)
                dve.wait_ge(S["gate_in"], 48 * (sub["gate"] + 1))
                for s in range(2):
                    row = gate_row[:, s, bass.ds(i * HB, HB)]
                    ins = nc.vector.scalar_tensor_tensor(out=row, in0=ps[:, b0 + s, :], scalar=factor, in1=row,
                                                         op0=ALU.mult, op1=ALU.mult)
                ins.then_inc(S["fin_read"], 1)

            def make_mod(l, j, half):
                dve.wait_ge(S["fin_read"], half)
                nc.vector.tensor_copy(m_shift[:], mcol[:, 0:2].rearrange("p a c s -> p (a c) s"))
                own.link(nc.vector.scalar_tensor_tensor(
                    out=m_scale[:], in0=mcol[:, 2:4].rearrange("p a c s -> p (a c) s"), scalar=1.0,
                    in1=nw_col[:, l, j, :].unsqueeze(2).to_broadcast([P, KC, 2]), op0=ALU.add, op1=ALU.mult))

            def prenorm_rs(xi, i):
                dve.wait_ge(S["std2"], xi + 1)
                nc.vector.reciprocal(stat[:, i, 5:6], stat[:, i, 4:5]).then_inc(S["rs2"], 1)

            def prenorm_mod(xi, t):
                s = 0 if t < NTL else 1
                tile = ps[:, 6:8, :].rearrange("p b (c w) -> p (b c) w", w=P)
                dve.wait_ge(S["xT"], xi + 1)
                own.link(nc.vector.tensor_tensor(tile, tile, m_scale[:, :, s].unsqueeze(2).to_broadcast([P, KC, P]), ALU.mult))
                nc.vector.tensor_tensor(tile, tile, m_shift[:, :, s].unsqueeze(2).to_broadcast([P, KC, P]),
                                        ALU.add).then_inc(S["modded"], 1)
                dve.wait_ge(S["xn_hi"], xi + 1)
                nc.vector.tensor_tensor(xn_lo[:, :, t * P:(t + 1) * P], tile, xn_hi[:, :, t * P:(t + 1) * P].bitcast(F32),
                                        ALU.subtract).then_inc(S["xn_done"], 1)

            def stage(sub, g, s):
                tiles, y0, x0 = tiles_of(sub)[g], sub["y"] + g * GT, sub["xn"] + g * GT
                if 0 <= s - 3 < len(tiles) and not sub["final"]:
                    prenorm_mod(x0 + s - 3, tiles[s - 3])
                if 0 <= s - 1 < len(tiles) and not sub["final"]:
                    prenorm_rs(x0 + s - 1, s - 1)
                if 0 <= s < len(tiles):
                    t = tiles[s]
                    dve.wait_ge(S["std1"], y0 + s + 1)
                    own.link(nc.vector.reciprocal(stat[:, s, 2:3], stat[:, s, 1:2]))
                    own.link(nc.vector.scalar_tensor_tensor(out=ys(s), in0=ys(s), scalar=stat[:, s, 2:3],
                                                            in1=gate_row[:, 0 if t < NTL else 1, :], op0=ALU.mult, op1=ALU.mult))
                    nc.vector.tensor_tensor(x[:, t, :], x[:, t, :], ys(s), ALU.add).then_inc(S["x_new"], 1)

            def evacuate(sub, g):
                n_end = sub["slot"] + sub["in_slots"] + (g + 1) * sub["k_slots"]
                dve.wait_ge(S["w_used"], 2 * n_end + START)
                for i in range(sub["groups"][g]):
                    nc.vector.tensor_copy(ys(i), ps[:, 2 * i:2 * i + 2, :].rearrange("p b n -> p (b n)")).then_inc(S["y_copied"], 1)
                dve.wait_ge(S["y_copied"], sub["y"] + g * GT + sub["groups"][g])

            dve.wait_ge(S["consts"], 16 * 8)
            dve.wait_ge(S["pool_consts"], 2)
            nc.vector.tensor_copy(ident_bf[:], ident[:]).then_inc(S["h_done"], FREE)
            nc.vector.tensor_scalar(neg_ident[:], ident[0:64, 0:64], -1.0, None, ALU.mult)
            nc.vector.tensor_scalar(mask[:], tri, -1.0, -NEG, ALU.add, ALU.mult).then_inc(S["dve_consts"], 1)
            for t in range(NT):
                prenorm_rs(t, t)
            dve.wait_ge(S["silu_c"], 1)
            for i in range(4):
                if i:
                    dve.wait_ge(S["fin_mm"], i)
                own.link(nc.vector.memset(acc[:], 0.0))
                dve.wait_ge(S["ada_first"][i], 16)
                for k in range(KC):
                    for s in range(2):
                        if k:
                            own.wait_back(1)
                        ins = nc.vector.scalar_tensor_tensor(out=acc[:, s, :], in0=ada0(i)[:, k, :], scalar=silu_c[:, k, s:s + 1],
                                                             in1=acc[:, s, :], op0=ALU.mult, op1=ALU.add)
                        if k == KC - 1 and s == 1:
                            ins.then_inc(S["acc_first"], 1)
                        else:
                            own.mark(ins)
                finish_col(i, i, 0, 0, 6)
            make_mod(0, 0, 4)
            split_w(0, 0)
            for t in range(NT):
                prenorm_mod(t, t)

            for sub in SUBS:
                l, j, n0 = sub["l"], sub["j"], sub["slot"]
                par0 = n0 % 2
                u0, half0 = sub["unit"], sub["half"]
                if sub["kind"] == "ffn":
                    for f, n, s, half, u in in_steps(sub, own.loop, (13, 0)):
                        split_w(n + 1, (par0 + s + 1) % 2)
                        if half is not None:
                            unit(half * 4 + (u0 + u), u)
                        dve.wait_ge(S["silu"], f + (sub["proj"] + 1))
                        for g in range(2):
                            w = sub["in_groups"][g] * P
                            hd = hid[:, g, bass.ds(f, 1), 0:w].rearrange("p a w -> p (a w)")
                            ins = nc.vector.tensor_tensor(hd, hd, ps[:, (s % 2) * 4 + 2 + g, 0:w], ALU.mult)
                        ins.then_inc(S["h_done"], 1)
                        if half is not None and u == 3:
                            finish_col(half + half0, half, 3 * sub["next"][1] * KC, sub["next"][0], 0)
                else:
                    mixer_dve(dve, own, sub, split_w, unit, finish_col, finish_gate)
                if sub["next"]:
                    make_mod(*sub["next"], half0 + 4)
                    u0, half0 = u0 + 16, half0 + 4
                for g in range(2):
                    nb = n0 + sub["in_slots"] + g * sub["k_slots"]
                    q0 = sub["hj"] + g * 2 * sub["k_slots"]
                    pb = nb % 2
                    hj(sub, g, 0, q0, 2 * nb, 0)
                    if g == 1:
                        evacuate(sub, 0)
                    done = 0
                    for s, n, par, half, u, st in out_steps(sub, g, own.loop, (13, 0)):
                        hj(sub, g, s * 2 + 1, s * 2 + (q0 + 1), n * 2 + 1, 1)
                        split_w(n + 1, (pb + par + 1) % 2)
                        if not (isinstance(s, int) and s == sub["k_slots"] - 1):
                            hj(sub, g, s * 2 + 2, s * 2 + (q0 + 2), n * 2 + 2, 0)
                        if half is not None:
                            unit(half * 4 + (u0 + u), u)
                            if u == 3:
                                finish_gate(half + half0, half, 6, 0.5, sub)
                        if st is not None:
                            stage(sub, 0, st)
                            done = st + 1
                for s in range(done, norm_stages(sub, 0)):
                    stage(sub, 0, s)
                evacuate(sub, 1)
                for s in range(norm_stages(sub, 1)):
                    stage(sub, 1, s)

        @block.tensor
        def _(pe):
            loop = plain_loop(pe)
            mm = nc.tensor.matmul
            pe.sem_inc(S["w_used"], START)

            def project_in(n, par, b, groups, chunks=2, width=P):
                pe.wait_ge(S["w_lo"], n + 1 + START)
                hi = w_hi[par][:].rearrange("p (k c n) -> p k c n", k=KC, c=2)
                lo = w_lo[par][:].rearrange("p (k c n) -> p k c n", k=KC, c=2)
                for c in range(2):
                    for k in range(KC):
                        for i, (w, xx) in enumerate(((hi, xn_hi), (hi, xn_lo), (lo, xn_hi))):
                            for g in range(2):
                                wd = groups[g] * P
                                ins = mm(ps[:, 4 * b + 2 * c + g, 0:wd], w[:, k, c, :], xx[:, k, g * GW:g * GW + wd],
                                         start=(k == 0 and i == 0), stop=(k == KC - 1 and i == 2))
                ins.then_inc(S["w_used"], 2)

            def project_out(sub, g, s, n, par, q0, first, last):
                hi = w_hi[par][:].rearrange("p (c n) -> p c n", c=2)
                lo = w_lo[par][:].rearrange("p (c n) -> p c n", c=2)
                pe.wait_ge(S["w_lo"], n + 1 + START)
                for c in range(2):
                    pe.wait_ge(S["hj_lo"], s * 2 + (q0 + c + 1))
                    for i in range(sub["groups"][g]):
                        for a, (xx, w) in enumerate(((hj_hi[c], hi), (hj_hi[c], lo), (hj_lo[c], hi))):
                            for hf in range(2):
                                ins = mm(ps[:, 2 * i + hf, :], xx[:, i * P:(i + 1) * P], w[:, c, hf * 512:(hf + 1) * 512],
                                         start=first and c == 0 and a == 0, stop=last and c == 1 and a == 2,
                                         skip_group_check=True)
                    ins.then_inc(S["w_used"], 1)

            def finish_col(half, units, bank_):
                if units is not None:
                    pe.wait_ge(S["ada_used"], units + START)
                pe.wait_ge(S["fin_read"], half)
                for c in range(4):
                    for s in range(2):
                        ins = mm(ps[:, bank_, GW + 2 * c + s:GW + 2 * c + s + 1], acc[:, s, c * P:(c + 1) * P], ones[:, 0:1],
                                 start=True, stop=True)
                ins.then_inc(S["fin_mm"], 1)

            def finish_gate(half, units, i, b0, sub):
                pe.wait_ge(S["ada_used"], units + START)
                pe.wait_ge(S["fin_read"], half)
                pe.wait_ge(S["gate_in"], 48 * (sub["gate"] + 1))
                for s in range(2):
                    mm(ps[:, b0 + s, :], ones[:], acc[:, s, :], start=True, stop=False)
                    ins = mm(ps[:, b0 + s, :], ones[0:1, :], b_gate[0:1, bass.ds(i * HB, HB)], start=False, stop=True)
                ins.then_inc(S["fin_mm"], 1)

            def turn(xi, i, half):
                pe.wait_ge(S["xs"], xi + 1)
                if xi:
                    pe.wait_ge(S["xn_done"], xi)
                pe.wait_ge(S["fin_read"], half)
                for c in range(KC):
                    ins = nc.tensor.transpose(ps[:, 6 + c // 4, (c % 4) * P:(c % 4 + 1) * P], ys(i)[:, c * P:(c + 1) * P], ident[:])
                ins.then_inc(S["xT"], 1)

            pe.wait_ge(S["pool_consts"], 2)
            pe.wait_ge(S["dve_consts"], 1)
            for i in range(4):
                pe.wait_ge(S["acc_first"], i + 1)
                finish_col(i, None, 6)
            for t in range(NT):
                turn(t, t, 4)

            for sub in SUBS:
                n0, half0, u0 = sub["slot"], sub["half"], sub["unit"]
                par0 = n0 % 2
                pe.wait_ge(S["xn_done"], sub["xn"])
                if sub["kind"] == "ffn":
                    for f, n, s, half, u in in_steps(sub, loop, (0, 0)):
                        pe.wait_ge(S["h_done"], f + (sub["proj"] + 1))
                        project_in(n, (par0 + s) % 2, s % 2, sub["in_groups"])
                        if half is not None and u == 3:
                            finish_col(half + half0, half * 4 + (u0 + 4), 0)
                            pe.wait_ge(S["fin_read"], half + (half0 + 1))
                    pe.wait_ge(S["h_done"], sub["proj"] + FC + FREE)
                else:
                    mixer_pe(pe, sub, project_in, finish_col, finish_gate)
                if sub["next"]:
                    u0, half0 = u0 + 16, half0 + 4
                for g in range(2):
                    nb = n0 + sub["in_slots"] + g * sub["k_slots"]
                    q0 = sub["hj"] + g * 2 * sub["k_slots"]
                    pb = nb % 2
                    if g == 1:
                        pe.wait_ge(S["y_copied"], sub["y"] + GT)
                    done = 0
                    for s, n, par, half, u, st in out_steps(sub, g, loop, (0, 0)):
                        dyn = not isinstance(s, int)
                        project_out(sub, g, s, n, (pb + par) % 2, q0,
                                    first=(not dyn and s == 0), last=(not dyn and s == sub["k_slots"] - 1))
                        if half is not None and u == 3:
                            finish_gate(half + half0, half * 4 + (u0 + 4), half, 6, sub)
                        if st is not None and not sub["final"]:
                            if 0 <= st - 2 < GT:
                                turn(sub["xn"] + st - 2, st - 2, sub["half_end"])
                            done = st + 1
                if not sub["final"]:
                    nh = sub["half_end"]
                    for s in range(max(2, done), GT + 2):
                        turn(sub["xn"] + s - 2, s - 2, nh)
                    for i in range(sub["groups"][1]):
                        turn(sub["xn"] + GT + i, i, nh)

def kernel(x, c, ctx, c_ctx, w_ada, b_ada, norm_w, w_ff_in, w_ff_out, w_in, w_fmix, conv_w, conv_b, w_qkv, gate_b,
           mlstm_norm_w, w_out):
    import concourse.bacc as bacc
    from concourse.bass_utils import run_bass_kernel_spmd

    def cols(a, n):
        a = a.reshape(a.shape[:-1] + (n, P))
        return np.ascontiguousarray(np.moveaxis(a, -1, 0))

    def dft(s, norm):
        a = np.outer(np.arange(s), np.arange(s)) % s * (2 * np.pi / s)
        both = np.stack([np.cos(a), -np.sin(a)], 1) / norm
        return np.ascontiguousarray(both.reshape(s // P, P, 2, s).transpose(1, 0, 2, 3).astype(np.float32))

    group = D // 2 // 8
    ag = np.outer(np.arange(group), np.arange(group)) % group * (2 * np.pi / group)
    dft_g = np.zeros((P, 2 * P), np.float32)
    fmix = np.zeros((DEPTH, P, 4, P), np.float32)
    for i in range(2):
        s = slice(i * group, (i + 1) * group)
        dft_g[s, s] = np.cos(ag)
        dft_g[s, P + i * group:P + (i + 1) * group] = np.sin(ag)
        fmix[:, s, :, s] = np.asarray(w_fmix)[:, i::2].transpose(0, 2, 1, 3)
    tri = np.stack([np.triu(np.ones((P, P), np.float32)), np.tril(np.ones((P, P), np.float32))], 1)
    arrays = {
        "x_in": np.concatenate([np.asarray(x)[0], np.asarray(ctx)[0]]).reshape(NT, P, D),
        "w_ada": np.asarray(w_ada),
        "norm_w": np.asarray(norm_w),
        "w_ff_in": np.ascontiguousarray(np.asarray(w_ff_in).reshape(DEPTH, 2, KC, P, 2, FC, P).transpose(0, 1, 5, 3, 2, 4, 6)
                                        ).reshape(DEPTH, 2, FC, P, SLOT),
        "w_ff_out": np.asarray(w_ff_out),
        "w_in": np.asarray(w_in),
        "w_gates": np.ascontiguousarray(np.asarray(w_in)[:, :, 1536:].reshape(DEPTH, KC, P, 16).transpose(0, 2, 1, 3)
                                        ).reshape(DEPTH, P, KC * 16),
        "w_out": np.asarray(w_out),
        "w_qkv": np.asarray(w_qkv),
        "b_ada": np.asarray(b_ada),
        "cvec_in": np.ascontiguousarray(np.stack([np.asarray(c)[0], np.asarray(c_ctx)]).reshape(2, KC, P).transpose(2, 1, 0)),
        "gate_b_in": np.ascontiguousarray(np.broadcast_to(np.asarray(gate_b).reshape(1, DEPTH, 16), (P, DEPTH, 16))),
        "b_col_in": cols(np.asarray(b_ada), 9 * KC),
        "nw_col_in": cols(np.asarray(norm_w)[:, 0::2], KC),
        "convw_in": np.ascontiguousarray(np.asarray(conv_w).reshape(DEPTH, 9, HEADS, P).transpose(3, 0, 2, 1)),
        "convb_in": cols(np.asarray(conv_b), HEADS),
        "hn_w_in": cols(np.asarray(mlstm_norm_w), HEADS),
        "fmix_in": fmix,
        "dft_l_in": dft(SEQ, np.sqrt(SEQ * group)),
        "dft_c_in": dft(CTX, np.sqrt(CTX * group)),
        "dft_g_in": dft_g,
        "tri_in": np.ascontiguousarray(tri),
    }
    nc = bacc.Bacc("TRN2", target_bir_lowering=False, num_devices=1)
    args = {k: nc.dram_tensor(k, a.shape, mybir.dt.from_np(a.dtype), kind="ExternalInput").ap() for k, a in arrays.items()}
    args["out"] = nc.dram_tensor("out", (NTL, P, D), F32, kind="ExternalOutput").ap()
    build(nc, **args)
    r = run_bass_kernel_spmd(nc, [arrays], core_ids=[0])
    return r.results[0]["out"].reshape(1, SEQ, D)
```

```python
from contextlib import ExitStack, contextmanager

import numpy as np

import concourse.bass as bass
from concourse import mybir

F32 = mybir.dt.float32
F32R = mybir.dt.float32r
BF16 = mybir.dt.bfloat16
ALU = mybir.AluOpType
ACT = mybir.ActivationFunctionType
AX_X = mybir.AxisListType.X

P = 128
D = 1024
KC = D // P
SEQ, CTX = 512, 256
TOK = SEQ + CTX
NT, NTL = TOK // P, SEQ // P
DEPTH = 2
D_FF = 2816
FC = D_FF // P
HEADS, HD = 4, 128
GW = 384
GT = GW // P
SLOT = 2048
HB = 512
EPS = 1e-6
NEG = -1e30
START = 1
HV = HD + 1

XN = 2 * KC * TOK
HG = FC * GW
A_H = XN
A_YS = A_H + 8 * GW
A_DUMMY = A_YS + 3 * D
A_XM = A_YS
A_QKVW = A_XM + HEADS * TOK
A_FW = A_QKVW + 12 * P
A_TRI = A_FW + 4 * P
A_DFTG = A_H + 2 * HG - 256
A_CONV = A_H + HG + 8 * GW
A_GATE = A_CONV + HEADS * TOK
A_DFT = 0
A_XAB = A_DFT + 8 * SEQ + 4 * CTX
A_HEAD = A_XAB + NT * 256


def plan():
    subs = []
    slot = hj = y = xn = proj = unit = half = mix = gate = 0
    xn = NT
    half = 4
    for l in range(DEPTH):
        for j in range(3):
            kind = "mix" if j == 1 else "ffn"
            last = l == DEPTH - 1
            final = last and j == 2
            groups = [GT, NTL - GT] if last and j >= 1 else [GT, GT]
            k_slots = 4 if kind == "mix" else FC // 2
            s = dict(l=l, j=j, kind=kind, final=final, groups=groups, k_slots=k_slots, slot=slot, hj=hj, y=y,
                     xn=xn, proj=proj, unit=unit, half=half, mix=mix, gate=gate,
                     next=None if final else ((l, j + 1) if j < 2 else (l + 1, 0)))
            s["in_slots"] = 7 if kind == "mix" else FC
            s["in_groups"] = [GT, NTL - GT] if final else [GT, GT]
            subs.append(s)
            slot += s["in_slots"] + 2 * k_slots
            hj += 4 * k_slots
            y += sum(groups)
            xn += 0 if final else sum(groups)
            halves = 2 if final else 6
            unit += 4 * halves
            half += halves
            s["half_end"] = half
            gate += 1
            if kind == "mix":
                mix += 1
            else:
                proj += FC
    return subs


SUBS = plan()


class Count:

    def __init__(self, eng, sem):
        self.eng, self.sem, self.n, self.term = eng, sem, 0, 0

    def mark(self, ins):
        ins.then_inc(self.sem, 1)
        self.n += 1

    def wait(self):
        self.eng.wait_ge(self.sem, self.n + self.term)

    def link(self, ins):
        self.mark(ins)
        self.wait()

    def wait_back(self, back):
        self.eng.wait_ge(self.sem, self.n - back + self.term)

    @contextmanager
    def loop(self, trips, per):
        base = self.n
        with self.eng.Fori(0, trips) as i:
            self.term = i * per
            yield i
        assert self.n - base == per, (self.n - base, per)
        self.term = 0
        self.n = base + trips * per


def scan_k(d, t):
    return (t + 2) % NT if d == 0 else NT - 1 - t


def scan_t(d, k):
    return (k + 4) % NT if d == 0 else NT - 1 - k


def scan_col(d, k, h):
    return d * 32 + k * 4 + h


def tiles_of(sub):
    return [list(range(GT)), list(range(GT, GT + sub["groups"][1]))]


def build(nc, x_in, w_ada, norm_w, w_ff_in, w_ff_out, w_in, w_gates, w_out, w_qkv, b_ada, cvec_in, gate_b_in,
          b_col_in, nw_col_in, convw_in, convb_in, hn_w_in, fmix_in, dft_l_in, dft_c_in, dft_g_in, tri_in, out):
    ctx = ExitStack()
    with ctx:
        def sb(name, shape, dt=F32):
            return ctx.enter_context(nc.sbuf_tensor(name, shape, dt))

        x = sb("x", [P, NT, D])
        inner = ExitStack()
        xn_hi = inner.enter_context(nc.sbuf_tensor("xn_hi", [P, KC, TOK], F32R))
        xn_lo = inner.enter_context(nc.sbuf_tensor("xn_lo", [P, KC, TOK], F32R))
        inner.close()
        arena = sb("arena", [P, XN + 2 * HG])
        hj_hi = [sb(f"hj_hi{i}", [P, GW], F32R) for i in range(2)]
        hj_lo = [sb(f"hj_lo{i}", [P, GW], F32R) for i in range(2)]
        raw = sb("raw", [P, SLOT])
        w_hi = [sb(f"w_hi{i}", [P, SLOT], F32R) for i in range(2)]
        w_lo = [sb(f"w_lo{i}", [P, SLOT], F32R) for i in range(2)]
        raw_ada = [sb(f"raw_ada{i}", [P, 2, HB]) for i in range(2)]
        acc = sb("acc", [P, 2, HB])
        gate_row = sb("gate_row", [P, 2, D])
        b_gate = sb("b_gate", [KC, P])
        ident = sb("ident", [P, P])
        mask = sb("mask", [P, 2, P], BF16)
        ident_bf = sb("ident_bf", [P, P], BF16)
        ones = sb("ones", [P, 8])
        cvec = sb("cvec", [P, KC, 2])
        silu_c = sb("silu_c", [P, KC, 2])
        b_col = sb("b_col", [P, DEPTH, 9 * KC])
        nw_col = sb("nw_col", [P, DEPTH, 3, KC])
        mcol = sb("mcol", [P, 4, 4, 2])
        m_scale = sb("m_scale", [P, KC, 2])
        m_shift = sb("m_shift", [P, KC, 2])
        stat = sb("stat", [P, 6, 8])
        convw = sb("convw", [P, DEPTH, HEADS, 9])
        convb = sb("convb", [P, DEPTH, HEADS])
        hn_w = sb("hn_w", [P, DEPTH, HEADS])
        gate_b = sb("gate_b", [P, DEPTH, 16])
        eps = sb("eps", [P, 1])
        ps = ctx.enter_context(nc.psum_tensor("ps", [P, 8, 512], F32))

        def at(off, n):
            return arena[:, off:off + n]

        hid = at(A_H, 2 * HG).rearrange("p (g c w) -> p g c w", g=2, c=FC)
        dummy = at(A_DUMMY, D)

        def ada0(i):
            off = i * KC * HB if i < 3 else A_TRI + 2 * P
            return at(off, KC * HB).rearrange("p (k n) -> p k n", k=KC)

        def ys(i):
            return at(A_YS + i * D, D) if i < 3 else at(A_H + (i - 3) * D, D)

        mixT = hid
        xmT = at(A_XM, HEADS * TOK).rearrange("p (h t) -> p h t", h=HEADS)
        convT = at(A_CONV, HEADS * TOK).rearrange("p (h t) -> p h t", h=HEADS)
        qkv_w = at(A_QKVW, 12 * P).rearrange("p (a h e) -> p a h e", a=3, h=HEADS)
        fmix_w = at(A_FW, 4 * P).rearrange("p (f n) -> p f n", f=4)
        dft_l = at(A_DFT, 8 * SEQ).rearrange("p (t c s) -> p t c s", t=4, c=2)
        dft_c = at(A_DFT + 8 * SEQ, 4 * CTX).rearrange("p (t c s) -> p t c s", t=2, c=2)
        dft_g = at(A_DFTG, 256)
        tri = at(A_TRI, 2 * P).rearrange("p (d t) -> p d t", d=2)
        xab = at(A_XAB, NT * 256).rearrange("p (t n) -> p t n", t=NT)
        place = {"gate": A_GATE, "head": A_HEAD}

        def small(n, which="gate", end=A_DFTG):
            place[which] += n
            assert place[which] <= end
            return at(place[which] - n, n)

        ab = at(A_GATE, 256)
        g16 = small(NT * 16)
        g_abs = small(48).rearrange("p (a h) -> p a h", h=4)
        lfs = small(64).rearrange("p (d k h) -> p d k h", d=2, k=8)
        igs = small(64).rearrange("p (d k h) -> p d k h", d=2, k=8)
        b_tok = small(64)
        r_tok = small(64)
        r_row = small(P)
        cm_row = small(P)
        m_row = small(P)
        nm_row = small(P)
        d_row = small(P)
        rw_row = small(P)
        p0 = small(6 * 64)
        rmax0, btot0, m0, mprev0, mlast0, dec0 = (p0[0:1, 64 * i:64 * i + 64] for i in range(6))
        cols = small(4)
        dec = small(64)
        em_arg = small(64)
        wi, em, wst = (small(48).rearrange("p (d t h) -> p d t h", d=2, t=NT) for _ in range(3))

        def head(n):
            return small(n, "head", XN)

        qT, kT = head(TOK), head(TOK)
        ktok = head(TOK).rearrange("p (t n) -> p t n", t=NT)
        vtok = head(NT * HV).rearrange("p (t n) -> p t n", t=NT)
        wv = head(NT * HV).rearrange("p (t n) -> p t n", t=NT)
        wt = head(TOK).rearrange("p (t n) -> p t n", t=NT)
        cst = head(NT * HV).rearrange("p (k n) -> p k n", k=NT)
        num = wv
        bn = small(NT * 6).rearrange("p (t n) -> p t n", t=NT)
        mv = small(NT * 2).rearrange("p (t n) -> p t n", t=NT)
        den = small(4 * NT).rearrange("p (a t) -> p a t", a=4)

        def hsum(h):
            return convT[:, h, :].rearrange("p (t n) -> p t n", t=NT)

        S = {}
        for name in (
            "consts pool_consts dve_consts x_in "
            "w_raw w_hi w_lo w_used "
            "ada_raw0 ada_raw1 ada_used fin_mm fin_read silu_c "
            "silu h_done hj_hi hj_lo "
            "y_sq y_copied std1 x_new std2 rs2 xs xT modded xn_hi xn_done "
            "gated gate_in dft_in rows_sb rows_mm out_dma dve act_ms act_ms2 "
            "win_evac mix_const g_abs g_exp g_ln g_lf g_b g_r g_rT g_rmx g_rr g_m g_dec g_bc g_rows g_T g_arg g_w "
            "ab_mm ab_sb xab_mm xab_sb f_mm f_sb conv conv_silu "
            "qkv_mm qkv_sb st_mm mb_mm wt_sb wv_sb cloc_mm cst_sb p_sb io_mm comb hvar hstd hn hnT mix_done"
        ).split():
            S[name] = ctx.enter_context(nc.semaphore("s_" + name))

        S["ada_first"] = [ctx.enter_context(nc.semaphore(f"s_ada_first{i}")) for i in range(4)]
        N_SLOTS = SUBS[-1]["slot"] + SUBS[-1]["in_slots"] + 2 * SUBS[-1]["k_slots"]
        block = ctx.enter_context(nc.Block())

        def in_steps(sub, loop, per):
            n0 = sub["slot"]
            for s in range(2):
                yield s, n0 + s, s, None, None
            done = 2
            if sub["next"]:
                with loop(4, per[0]) as i:
                    for s in range(4):
                        yield i * 4 + (2 + s), i * 4 + (n0 + 2 + s), s, i, s
                done = 18
            with loop((FC - done) // 2, per[1]) as i:
                for s in range(2):
                    yield i * 2 + (done + s), i * 2 + (n0 + done + s), s, None, None

        def out_steps(sub, g, loop, per):
            k = sub["k_slots"]
            n0 = sub["slot"] + sub["in_slots"] + g * k
            s = 0
            if g == 0 and sub["kind"] == "mix":
                for s in range(4):
                    yield s, n0 + s, s, s // 2, (2 * (s % 2), 2 * (s % 2) + 1), None
                return
            if g == 0:
                for i in range(2):
                    for u in range(4):
                        yield i * 4 + u, i * 4 + (n0 + u), i * 4 + u, i, (u,), None
                s = 8
            while g == 1 and s < min(6, k):
                yield s, n0 + s, s, None, None, s
                s += 1
            pairs = (k - 1 - s) // 2
            if pairs > 1:
                with loop(pairs, per[1]) as i:
                    for u in range(2):
                        yield i * 2 + (s + u), i * 2 + (n0 + s + u), s + u, None, None, None
                s += 2 * pairs
            while s < k:
                yield s, n0 + s, s, None, None, None
                s += 1

        def norm_stages(sub, g):
            return sub["groups"][g] + 3

        def plain_loop(eng):
            return lambda trips, per: eng.Fori(0, trips)

        def mixer_act(act, sub, split_w):
            m, n0 = sub["mix"], sub["slot"]
            outs = tiles_of(sub)
            n_out = sum(sub["groups"])
            ctx_out = n_out == NT

            def evac(ch):
                n = n0 + ch // 2 + (1 if ch >= 4 else 0)
                act.wait_ge(S["w_used"], 2 * n + ch % 2 + 1 + START)
                for g in range(2):
                    w = GW if ch < 4 else sub["groups"][g] * P
                    dst = xmT[:, ch, g * GW:g * GW + w] if ch < 4 else mixT[:, g, ch - 4, 0:w]
                    ins = nc.scalar.activation(dst, ps[:, 2 * (ch % 3) + g, 0:w], ACT.Sigmoid if ch >= 8 else ACT.Copy)
                ins.then_inc(S["win_evac"], 1)

            def conv_silu(h):
                act.wait_ge(S["conv"], 4 * m + h + 1)
                nc.scalar.activation(convT[:, h, :], convT[:, h, :], ACT.Silu).then_inc(S["conv_silu"], 1)

            def split(s):
                split_w(n0 + s, (n0 + s) % 2, KC * 16 if s == 2 else SLOT)

            evac(0)
            evac(1)
            split(2)
            evac(2)
            evac(3)
            split(3)
            conv_silu(0)
            split(4)
            act.wait_ge(S["g_abs"], m + 1)
            nc.scalar.activation(g_abs, g_abs, ACT.Exp, scale=-1.0).then_inc(S["g_exp"], 1)
            act.wait_ge(S["g_exp"], m + 1)
            nc.scalar.activation(g_abs, g_abs, ACT.Ln, bias=ones[:, 0:1]).then_inc(S["g_ln"], 1)
            conv_silu(1)
            evac(4)
            evac(5)
            split(5)
            evac(6)
            conv_silu(2)
            evac(7)
            split(6)
            act.wait_ge(S["g_m"], m + 1)
            nc.scalar.activation(dec0, dec0, ACT.Exp).then_inc(S["g_dec"], 1)
            evac(8)
            conv_silu(3)
            evac(9)
            split(7)
            act.wait_ge(S["g_arg"], m + 1)
            em_v = em_arg.rearrange("p (d k h) -> p d k h", d=2, k=8)
            t_v = ps[:, 7, 0:192].rearrange("p (a d k h) -> p a d k h", a=3, d=2, k=8)
            for dst, src in ((em, em_v), (wi, t_v[:, 1]), (wst, t_v[:, 2])):
                nc.scalar.activation(dst[:, 0, 0:4, :], src[:, 0, 2:6, :], ACT.Exp)
                nc.scalar.activation(dst[:, 0, 4:6, :], src[:, 0, 0:2, :], ACT.Exp)
                ins = nc.scalar.activation(dst[:, 1, 0:6, :], src[:, 1, 5::-1, :], ACT.Exp)
            ins.then_inc(S["g_w"], 1)
            evac(10)
            evac(11)
            for dst, src in ((dft_l, dft_l_in), (dft_c, dft_c_in)):
                act.dma_start(dst, src).then_inc(S["dft_in"], 16)

            def take(dst, src, scale, signal):
                nc.scalar.activation(dst, src, ACT.Copy, scale=scale).then_inc(S[signal], 1)

            def project(h, a):
                dst, b0 = ((qT, 0), (kT, 2), (ktok, 4), (vtok, 0))[a]
                act.wait_ge(S["qkv_mm"], 4 * (4 * m + h) + a + 1)
                for g in range(2):
                    w = (len(outs[g]) if a == 0 else GT) * P
                    src = ps[:, b0 + g, 0:w]
                    if a < 2:
                        to = dst[:, g * GW:g * GW + w]
                    else:
                        to = dst[:, g * GT:(g + 1) * GT, 0:HD]
                        src = src.rearrange("p (t n) -> p t n", n=P)
                    ins = nc.scalar.activation(to, src, ACT.Copy, scale=float(HD) ** -0.5 if a in (1, 2) else 1.0)
                ins.then_inc(S["qkv_sb"], 1)

            def weights(h, d):
                md = 2 * (4 * m + h) + d
                act.wait_ge(S["mb_mm"], md + 1)
                if md:
                    act.wait_ge(S["io_mm"], md)
                for t in outs[0] + outs[1]:
                    col = scan_col(d, scan_k(d, t), h)
                    ins = nc.scalar.activation(wt[:, t, :], ps[:, 2 + t // GT, (t % GT) * P:(t % GT + 1) * P], ACT.Exp,
                                               bias=r_tok[:, col:col + 1])
                ins.then_inc(S["wt_sb"], 1)

            for h in range(HEADS):
                k = 4 * m + h
                for a in range(4):
                    project(h, a)
                weights(h, 0)
                act.wait_ge(S["ab_mm"], k + 1)
                take(ab, ps[:, 6, 0:256], 1.0, "ab_sb")
                act.wait_ge(S["xab_mm"], (2 * k if ctx_out else k + HEADS) + 1)
                for b in range(2):
                    ins = nc.scalar.activation(xab[:, 2 * b:2 * b + 2, :].rearrange("p t n -> p (t n)"), ps[:, 6 + b, :], ACT.Copy)
                ins.then_inc(S["xab_sb"], 1)
                if ctx_out:
                    act.wait_ge(S["xab_mm"], 2 * k + 2)
                    take(xab[:, 4:6, :].rearrange("p t n -> p (t n)"), ps[:, 6, :], 1.0, "xab_sb")
                weights(h, 1)
                act.wait_ge(S["f_mm"], k + 1)
                nc.scalar.activation(mixT[:, 0, h, :], ps[:, 7, 0:GW], ACT.Copy)
                ins = nc.scalar.activation(mixT[:, 1, h, 0:P], ps[:, 7, GW:512], ACT.Copy)
                if ctx_out:
                    ins = nc.scalar.activation(mixT[:, 1, h, P:GW], ps[:, 6, 0:CTX], ACT.Copy)
                ins.then_inc(S["f_sb"], 1)
                act.wait_ge(S["hvar"], k + 1)
                nc.scalar.activation(den[:, 0, 0:n_out], mv[:, 0:n_out, 1], ACT.Sqrt, bias=eps[:, 0:1]).then_inc(S["hstd"], 1)

        def mixer_dve(dve, own, sub, split_w, unit, finish_col):
            m, n0, l = sub["mix"], sub["slot"], sub["l"]
            u0, half0 = sub["unit"], sub["half"]
            nl, nj = sub["next"]
            outs = tiles_of(sub)
            n_out = sum(sub["groups"])
            link = own.link
            g5 = g16.rearrange("p (t d b h) -> p t d b h", t=NT, d=2, b=2)
            v8 = lambda a: a.rearrange("p (d c) -> p d c", d=2)

            def split(s):
                split_w(n0 + s, (n0 + s) % 2, KC * 16 if s == 2 else SLOT)

            def units(half):
                for u in range(4):
                    unit(u0 + 4 * half + u, u)

            def finish(half):
                finish_col(half0 + half, half, 3 * nj * KC, nl, 6)

            def conv(h):
                dve.wait_ge(S["win_evac"], 12 * m + h + 1)
                src = xmT[:, h, 0:SEQ].rearrange("p (r c) -> p r c", c=64)
                dst = convT[:, h, 0:SEQ].rearrange("p (r c) -> p r c", c=64)
                csrc, cdst = xmT[:, h, SEQ:TOK], convT[:, h, SEQ:TOK]
                w = convw[:, l, h, :]
                link(nc.vector.tensor_scalar(convT[:, h, :], xmT[:, h, :], w[:, 4:5], convb[:, l, h:h + 1], ALU.mult, ALU.add))

                def tap(o, s, k):
                    return nc.vector.scalar_tensor_tensor(out=o, in0=s, scalar=w[:, k:k + 1], in1=o, op0=ALU.mult, op1=ALU.add)

                R, C = SEQ // 64, 64
                for dy in (-1, 0, 1):
                    for dx in (-1, 0, 1):
                        if dy == 0 and dx == 0:
                            continue
                        r0, r1 = max(0, -dy), R - max(0, dy)
                        c0, c1 = max(0, -dx), C - max(0, dx)
                        link(tap(dst[:, r0:r1, c0:c1], src[:, r0 + dy:r1 + dy, c0 + dx:c1 + dx], (dy + 1) * 3 + dx + 1))
                link(tap(cdst[:, 1:CTX], csrc[:, 0:CTX - 1], 3))
                tap(cdst[:, 0:CTX - 1], csrc[:, 1:CTX], 5).then_inc(S["conv"], 1)

            def gates_abs():
                dve.wait_ge(S["w_used"], 2 * (n0 + 3) + START)
                gv = g16.rearrange("p (a b h) -> p a b h", b=2, h=4)
                link(nc.vector.tensor_tensor(g16.rearrange("p (t j) -> p t j", t=NT), ps[:, 7, 0:96].rearrange("p (t j) -> p t j", t=NT),
                                             gate_b[:, l, :].unsqueeze(1).to_broadcast([P, NT, 16]), ALU.add))
                nc.vector.scalar_tensor_tensor(out=g_abs, in0=gv[:, :, 1, :], scalar=-1.0, in1=gv[:, :, 1, :], op0=ALU.mult,
                                               op1=ALU.max).then_inc(S["g_abs"], 1)
                nc.vector.memset(lfs, 0.0)
                link(nc.vector.memset(igs, 0.0))

            def gates_log():
                a4 = g_abs.rearrange("p (t d) h -> p t d h", d=2)
                dve.wait_ge(S["g_ln"], m + 1)
                for d, dst, src in ((0, slice(2, 6), slice(0, 4)), (0, slice(0, 2), slice(4, 6)), (1, slice(0, 6), slice(5, None, -1))):
                    nc.vector.tensor_copy(igs[:, d, dst, :], g5[:, src, d, 0, :])
                    ins = nc.vector.scalar_tensor_tensor(out=lfs[:, d, dst, :], in0=g5[:, src, d, 1, :], scalar=0.0,
                                                         in1=a4[:, src, d, :], op0=ALU.min, op1=ALU.subtract)
                ins.then_inc(S["g_lf"], 1)

            def gates_r():
                dve.wait_ge(S["g_b"], m + 1)
                nc.vector.tensor_copy(b_tok, ps[:, 7, 96:160])
                nc.vector.tensor_copy(btot0, ps[0:1, 7, 160:224])
                nc.vector.tensor_tensor(r_tok, igs.rearrange("p d k h -> p (d k h)"), ps[:, 7, 96:160], ALU.subtract).then_inc(S["g_r"], 1)

            def gates_max():
                dve.wait_ge(S["g_rT"], m + 1)
                link(nc.vector.tensor_copy(r_row[0:64], ps[0:64, 7, 224:352]))
                nc.vector.tensor_reduce(cols[0:64, 2:3], r_row[0:64], AX_X, ALU.max).then_inc(S["g_rmx"], 1)
                nc.vector.tensor_tensor_scan(cm_row[0:32], r_row[0:32], r_row[0:32], NEG, ALU.max, ALU.max)
                back = r_row[32:64, P - 1::-1]
                link(nc.vector.tensor_tensor_scan(cm_row[32:64, P - 1::-1], back, back, NEG, ALU.max, ALU.max))

            def gates_m():
                dve.wait_ge(S["g_rr"], m + 1)
                link(nc.vector.tensor_copy(rmax0, ps[0:1, 7, 352:416]))
                link(nc.vector.memset(mprev0, 0.0))
                for d in range(2):
                    for h in range(HEADS):
                        sl = slice(d * 32 + h, d * 32 + h + 21, 4)
                        ins = nc.vector.tensor_tensor_scan(m0[:, sl], rmax0[:, sl], btot0[:, sl], 0.0, ALU.max, ALU.add)
                link(ins)
                link(nc.vector.tensor_copy(v8(mprev0)[:, :, 4:24], v8(m0)[:, :, 0:20]))
                link(nc.vector.tensor_tensor(mlast0, mprev0, rmax0, ALU.max))
                nc.vector.tensor_tensor(dec0, mprev0, mlast0, ALU.subtract).then_inc(S["g_m"], 1)

            def gates_rows():
                dve.wait_ge(S["g_bc"], m + 1)
                nc.vector.tensor_copy(dec, ps[:, 7, 420:484])
                link(nc.vector.tensor_copy(cols[0:64, 0:2], ps[0:64, 7, 416:418]))
                link(nc.vector.tensor_scalar(m_row[0:64], cm_row[0:64], cols[0:64, 0:1], None, ALU.max))
                nc.vector.tensor_scalar(d_row[0:64], m_row[0:64], -1.0, cols[0:64, 0:1], ALU.mult, ALU.add)
                nc.vector.tensor_scalar(nm_row[0:64], m_row[0:64], -1.0, None, ALU.mult)
                nc.vector.tensor_scalar(rw_row[0:64], r_row[0:64], cols[0:64, 1:2], None, ALU.subtract).then_inc(S["g_rows"], 1)

            def gates_arg():
                dve.wait_ge(S["g_T"], m + 1)
                nc.vector.scalar_tensor_tensor(out=em_arg, in0=ps[:, 7, 0:64], scalar=-1.0, in1=b_tok, op0=ALU.mult,
                                               op1=ALU.subtract).then_inc(S["g_arg"], 1)

            units(0)
            split(2)
            conv(0)
            finish(0)
            split(3)
            units(1)
            gates_abs()
            conv(1)
            split(4)
            gates_log()
            finish(1)
            gates_r()
            conv(2)
            split(5)
            gates_max()
            units(2)
            gates_m()
            finish(2)
            split(6)
            conv(3)
            gates_rows()
            units(3)
            split(7)
            gates_arg()
            finish(3)

            def values(h, d):
                md = 2 * (4 * m + h) + d
                if d == 0:
                    dve.wait_ge(S["qkv_sb"], 4 * (4 * m + h) + 4)
                nc.vector.tensor_tensor(wv, vtok, wst[:, d, :, h].unsqueeze(2).to_broadcast([P, NT, HV]), ALU.mult).then_inc(S["wv_sb"], 1)
                if md:
                    dve.wait_ge(S["io_mm"], md)
                link(nc.vector.memset(cst[:, 0, :], 0.0))

            def states(h, d):
                md = 2 * (4 * m + h) + d
                dve.wait_ge(S["cloc_mm"], md + 1)
                for k in range(NT - 1):
                    col = scan_col(d, k, h)
                    ins = nc.vector.scalar_tensor_tensor(out=cst[:, k + 1, :], in0=cst[:, k, :], scalar=dec[:, col:col + 1],
                                                         in1=ps[:, 4 + k // 3, (k % 3) * HV:(k % 3 + 1) * HV],
                                                         op0=ALU.mult, op1=ALU.add)
                    if k < NT - 2:
                        link(ins)
                ins.then_inc(S["cst_sb"], 1)

            def scores(h, d):
                md = 2 * (4 * m + h) + d
                dve.wait_ge(S["wt_sb"], md + 1)
                dve.wait_ge(S["st_mm"], 4 * m + h + 1)
                for g in range(2):
                    nt = len(outs[g])
                    wg = wt[:, g * GT:g * GT + nt, :].rearrange("p t n -> p (t n)")
                    ins = nc.vector.tensor_tensor(wg, wg, ps[:, g, 0:nt * P], ALU.mult)
                ins.then_inc(S["p_sb"], 1)

            def combine(h, d):
                md = 2 * (4 * m + h) + d
                dve.wait_ge(S["io_mm"], md + 1)
                for g in range(2):
                    nt = len(outs[g])
                    sl = slice(g * GT, g * GT + nt)
                    ng = num[:, sl, :]
                    link(nc.vector.tensor_tensor(ng, ps[:, 2 + g, 0:nt * HV].rearrange("p (t n) -> p t n", n=HV),
                                                 wi[:, d, sl, h].unsqueeze(2).to_broadcast([P, nt, HV]), ALU.mult))
                    ins = nc.vector.tensor_tensor(ng, ng, ps[:, 4 + g, 0:nt * HV].rearrange("p (t n) -> p t n", n=HV), ALU.add)
                    if g == 0:
                        own.mark(ins)
                ins.then_inc(S["comb"], 1)
                dve.wait_ge(S["comb"], md + 1)
                dn = num[:, 0:n_out, HD]
                link(nc.vector.scalar_tensor_tensor(out=den[:, 1, 0:n_out], in0=dn, scalar=-1.0, in1=dn, op0=ALU.mult, op1=ALU.max))
                link(nc.vector.tensor_tensor(den[:, 2, 0:n_out], den[:, 1, 0:n_out], em[:, d, 0:n_out, h], ALU.max))
                link(nc.vector.reciprocal(den[:, 3, 0:n_out], den[:, 2, 0:n_out]))
                rd = den[:, 3, 0:n_out].unsqueeze(2).to_broadcast([P, n_out, HD])
                hs = hsum(h)[:, 0:n_out, :]
                if d == 0:
                    link(nc.vector.tensor_tensor(hs, num[:, 0:n_out, 0:HD], rd, ALU.mult))
                else:
                    link(nc.vector.tensor_tensor(num[:, 0:n_out, 0:HD], num[:, 0:n_out, 0:HD], rd, ALU.mult))
                    link(nc.vector.tensor_tensor(hs, hs, num[:, 0:n_out, 0:HD], ALU.add))

            dve.wait_ge(S["w_used"], 2 * (n0 + 7) + START)
            link(nc.vector.memset(vtok[:, :, HD:HV], 1.0))
            dve.wait_ge(S["g_w"], m + 1)
            for h in range(HEADS):
                mh = 4 * m + h
                for d in range(2):
                    values(h, d)
                    states(h, d)
                    scores(h, d)
                    combine(h, d)
                for t in range(n_out):
                    ins = nc.vector.bn_stats(bn[:, t, :], hsum(h)[:, t, :])
                link(ins)
                for t in range(n_out):
                    ins = nc.vector.bn_aggr(mv[:, t, :], bn[:, t, :])
                ins.then_inc(S["hvar"], 1)
                dve.wait_ge(S["hstd"], mh + 1)
                link(nc.vector.reciprocal(den[:, 1, 0:n_out], den[:, 0, 0:n_out]))
                for t in range(n_out):
                    ins = nc.vector.tensor_scalar(hsum(h)[:, t, :], hsum(h)[:, t, :], mv[:, t, 0:1], den[:, 1, t:t + 1], ALU.subtract, ALU.mult)
                ins.then_inc(S["hn"], 1)
                dve.wait_ge(S["hnT"], mh + 1)
                for g in range(2):
                    w = len(outs[g]) * P
                    mg = mixT[:, g, 4 + h, 0:w]
                    ins = nc.vector.scalar_tensor_tensor(out=mg, in0=ps[:, 6 + g, 0:w], scalar=hn_w[:, l, h:h + 1], in1=mg,
                                                         op0=ALU.mult, op1=ALU.mult)
                ins.then_inc(S["mix_done"], 1)

        def mixer_pe(pe, sub, finish_col, turn):
            mm = nc.tensor.matmul
            m, n0 = sub["mix"], sub["slot"]
            u0, half0 = sub["unit"], sub["half"]
            outs = tiles_of(sub)
            n_out = sum(sub["groups"])
            ctx_out = n_out == NT

            def chunk(ch, groups):
                n = n0 + ch // 2 + (1 if ch >= 4 else 0)
                pe.wait_ge(S["w_lo"], n + 1 + START)
                if ch >= 3:
                    pe.wait_ge(S["win_evac"], 12 * m + ch - 2)
                hi = w_hi[n % 2][:].rearrange("p (k n) -> p k n", k=KC)
                lo = w_lo[n % 2][:].rearrange("p (k n) -> p k n", k=KC)
                c = ch % 2
                for k in range(KC):
                    for i, (w, xx) in enumerate(((hi, xn_hi), (hi, xn_lo), (lo, xn_hi))):
                        for g in groups:
                            wd = GW if ch < 4 else sub["groups"][g] * P
                            ins = mm(ps[:, 2 * (ch % 3) + g, 0:wd], w[:, k, c * P:(c + 1) * P], xx[:, k, g * GW:g * GW + wd],
                                     start=(k == 0 and i == 0), stop=(k == KC - 1 and i == 2))
                if 1 in groups:
                    ins.then_inc(S["w_used"], 1)

            pe.wait_ge(S["xn_done"], sub["xn"] - GT)
            pe.wait_ge(S["y_copied"], sub["y"])
            for i in range(GT):
                chunk(i, [0])
                turn(sub["xn"] - GT + i, i, half0)
            pe.wait_ge(S["xn_done"], sub["xn"])
            for ch in range(3):
                chunk(ch, [1])
            finish_col(half0, u0 + 4, 6)
            chunk(3, [0, 1])
            n = n0 + 2
            pe.wait_ge(S["w_lo"], n + 1 + START)
            hi = w_hi[n % 2][:, 0:KC * 16].rearrange("p (k j) -> p k j", k=KC)
            lo = w_lo[n % 2][:, 0:KC * 16].rearrange("p (k j) -> p k j", k=KC)
            for t in range(NT):
                for k in range(KC):
                    for i, (xx, w) in enumerate(((xn_hi, hi), (xn_hi, lo), (xn_lo, hi))):
                        ins = mm(ps[:, 7, t * 16:t * 16 + 16], xx[:, k, t * P:(t + 1) * P], w[:, k, :],
                                 start=(k == 0 and i == 0), stop=(k == KC - 1 and i == 2))
            ins.then_inc(S["w_used"], 2)
            chunk(4, [0, 1])
            finish_col(half0 + 1, u0 + 8, 6)
            chunk(5, [0, 1])
            pe.wait_ge(S["mix_const"], 64 * (m + 1))
            pe.wait_ge(S["g_lf"], m + 1)
            for d in range(2):
                mm(ps[:, 7, 96 + 32 * d:128 + 32 * d], tri[:, d, :], lfs[:, d].rearrange("p k h -> p (k h)"), start=True, stop=True)
            mm(ps[0:1, 7, 160:224], ones[:, 0:1], lfs.rearrange("p d k h -> p (d k h)"), start=True, stop=True).then_inc(S["g_b"], 1)
            chunk(6, [0, 1])
            pe.wait_ge(S["g_r"], m + 1)
            nc.tensor.transpose(ps[0:64, 7, 224:352], r_tok, ident[:]).then_inc(S["g_rT"], 1)
            chunk(7, [0, 1])
            pe.wait_ge(S["g_rmx"], m + 1)
            mm(ps[0:1, 7, 352:416], cols[0:64, 2:3], ident[0:64, 0:64], start=True, stop=True).then_inc(S["g_rr"], 1)
            finish_col(half0 + 2, u0 + 12, 6)
            chunk(8, [0, 1])
            pe.wait_ge(S["g_dec"], m + 1)
            mm(ps[0:64, 7, 416:417], mprev0, ones[0:1, 0:1], start=True, stop=True)
            mm(ps[0:64, 7, 417:418], mlast0, ones[0:1, 0:1], start=True, stop=True)
            mm(ps[:, 7, 420:484], ones[0:1, 0:1].to_broadcast([1, P]), dec0, start=True, stop=True).then_inc(S["g_bc"], 1)
            chunk(9, [0, 1])
            pe.wait_ge(S["g_rows"], m + 1)
            for i, row in enumerate((m_row, d_row, rw_row)):
                ins = nc.tensor.transpose(ps[:, 7, 64 * i:64 * i + 64], row[0:64], ident[0:64, 0:64])
            ins.then_inc(S["g_T"], 1)
            chunk(10, [0, 1])
            chunk(11, [0, 1])
            finish_col(half0 + 3, u0 + 16, 6)

            def head_out(h):
                mh = 4 * m + h
                pe.wait_ge(S["hn"], mh + 1)
                pe.wait_ge(S["f_sb"], mh + 1)
                for t in range(n_out):
                    ins = nc.tensor.transpose(ps[:, 6 + t // GT, (t % GT) * P:(t % GT + 1) * P], hsum(h)[:, t, :], ident[:])
                ins.then_inc(S["hnT"], 1)

            def project(h, a):
                for g in range(2):
                    if a < 2:
                        w = (len(outs[g]) if a == 0 else GT) * P
                        ins = mm(ps[:, 2 * a + g, 0:w], qkv_w[:, a, h, :], convT[:, h, g * GW:g * GW + w], start=True, stop=True)
                    else:
                        for t in range(g * GT, (g + 1) * GT):
                            src = (convT if a == 2 else xmT)[:, h, t * P:(t + 1) * P]
                            ins = mm(ps[:, (4 if a == 2 else 0) + g, (t % GT) * P:(t % GT + 1) * P], src, qkv_w[:, a - 1, h, :],
                                     start=True, stop=True)
                ins.then_inc(S["qkv_mm"], 1)

            def maxima(h, d):
                for g in range(2):
                    nt = len(outs[g])
                    mm(ps[:, 2 + g, 0:nt * P], ident_bf[:], mask[:, d, :].unsqueeze(1).to_broadcast([P, nt, P]), start=True, stop=False)
                    for i, t in enumerate(outs[g]):
                        col = scan_col(d, scan_k(d, t), h)
                        ins = mm(ps[:, 2 + g, i * P:(i + 1) * P], ident[0:64, col:col + 1].to_broadcast([64, P]), nm_row[0:64],
                                 start=False, stop=(i == nt - 1))
                ins.then_inc(S["mb_mm"], 1)

            def added(h, d):
                pe.wait_ge(S["wv_sb"], 2 * (4 * m + h) + d + 1)
                for k in range(NT - 1):
                    t = scan_t(d, k)
                    ins = mm(ps[:, 4 + k // 3, (k % 3) * HV:(k % 3 + 1) * HV], ktok[:, t, :], wv[:, t, :], start=True, stop=True)
                ins.then_inc(S["cloc_mm"], 1)

            def outputs(h, d):
                md = 2 * (4 * m + h) + d
                pe.wait_ge(S["cst_sb"], md + 1)
                pe.wait_ge(S["p_sb"], md + 1)
                for t in outs[0] + outs[1]:
                    g, i = t // GT, t % GT
                    mm(ps[:, 4 + g, i * HV:(i + 1) * HV], wt[:, t, :], vtok[:, t, :], start=True, stop=True)
                    ins = mm(ps[:, 2 + g, i * HV:(i + 1) * HV], qT[:, t * P:(t + 1) * P], cst[:, scan_k(d, t), :], start=True, stop=True)
                ins.then_inc(S["io_mm"], 1)

            def dft_part(tiles, first, last):
                for t in tiles:
                    for c in range(2):
                        ins = mm(ps[:, 7, :], xab[:, t, c * P:(c + 1) * P], dft_l[:, t, c, :], start=first and t == tiles[0] and c == 0,
                                 stop=last and t == tiles[-1] and c == 1)
                return ins

            for h in range(HEADS):
                k = 4 * m + h
                if h == 0:
                    pe.wait_ge(S["g_w"], m + 1)
                    pe.wait_ge(S["win_evac"], 12 * m + 12)
                    pe.wait_ge(S["fin_read"], half0 + 4)
                else:
                    pe.wait_ge(S["comb"], 2 * k)
                pe.wait_ge(S["conv_silu"], k + 1)
                for a in range(3):
                    project(h, a)
                if h:
                    head_out(h - 1)
                pe.wait_ge(S["qkv_sb"], 4 * k + 1)
                project(h, 3)
                pe.wait_ge(S["qkv_sb"], 4 * k + 2)
                maxima(h, 0)
                if h:
                    pe.wait_ge(S["mix_done"], k)
                mm(ps[:, 6, 0:P], dft_g[:, 0:P], fmix_w[:, h, :], start=True, stop=True)
                mm(ps[:, 6, P:2 * P], dft_g[:, P:2 * P], fmix_w[:, h, :], start=True, stop=True).then_inc(S["ab_mm"], 1)
                pe.wait_ge(S["qkv_sb"], 4 * k + 4)
                for t in outs[0] + outs[1]:
                    sl = slice(t * P, (t + 1) * P)
                    ins = mm(ps[:, t // GT, (t % GT) * P:(t % GT + 1) * P], kT[:, sl], qT[:, sl], start=True, stop=True)
                ins.then_inc(S["st_mm"], 1)
                added(h, 0)
                pe.wait_ge(S["ab_sb"], k + 1)
                for t in range(n_out):
                    if t == 4:
                        pe.wait_ge(S["xab_sb"], 2 * k + 1)
                    ins = mm(ps[:, 6 + t // 2 % 2, (t % 2) * 256:(t % 2) * 256 + 256],
                             mixT[:, t // GT, h, (t % GT) * P:(t % GT + 1) * P], ab, start=True, stop=True)
                    if t in (3, 5):
                        ins.then_inc(S["xab_mm"], 1)
                xabs = 2 * k + 2 if ctx_out else k + HEADS + 1
                pe.wait_ge(S["xab_sb"], xabs)
                if h == 0:
                    pe.wait_ge(S["dft_in"], 32 * (m + 1))
                dft_part([0, 1], True, False)
                outputs(h, 0)
                pe.wait_ge(S["comb"], 2 * k + 1)
                maxima(h, 1)
                added(h, 1)
                ins = dft_part([2, 3], False, True)
                if ctx_out:
                    for t in range(2):
                        for c in range(2):
                            ins = mm(ps[:, 6, 0:CTX], xab[:, NTL + t, c * P:(c + 1) * P], dft_c[:, t, c, :],
                                     start=(t == 0 and c == 0), stop=(t == 1 and c == 1))
                ins.then_inc(S["f_mm"], 1)
                outputs(h, 1)
            head_out(HEADS - 1)
            pe.wait_ge(S["mix_done"], HEADS * (m + 1))

        @block.sync
        def _(sp):
            loop = plain_loop(sp)

            def load(n, src, width=SLOT):
                if not isinstance(n, int) or n > 0:
                    sp.wait_ge(S["w_lo"], n + START)
                sp.dma_start(raw[:, 0:width], src).then_inc(S["w_raw"], 16)

            def unit(count, l, col, u):
                if not isinstance(count, int) or count >= 2:
                    sp.wait_ge(S["ada_used"], count - 1 + START)
                src = w_ada[l].rearrange("(u c p) n -> u p c n", c=2, p=P)[u, :, :, bass.ds(col, HB)]
                sp.dma_start(raw_ada[u % 2][:], src).then_inc(S[f"ada_raw{u % 2}"], 16)

            for dst, src in ((cvec[:], cvec_in), (b_col[:], b_col_in), (nw_col[:], nw_col_in), (convw[:], convw_in),
                             (convb[:], convb_in), (hn_w[:], hn_w_in), (tri, tri_in), (gate_b[:], gate_b_in)):
                sp.dma_start(dst, src).then_inc(S["consts"], 16)
            for i in range(4):
                src = w_ada[0].rearrange("(k p) n -> p k n", p=P)[:, :, i * HB:(i + 1) * HB]
                sp.dma_start(ada0(i), src).then_inc(S["ada_first"][i], 16)

            for sub in SUBS:
                l, j, n0 = sub["l"], sub["j"], sub["slot"]
                u0 = sub["unit"]
                if sub["kind"] == "ffn":
                    for f, n, s, half, u in in_steps(sub, loop, (0, 0)):
                        load(n, w_ff_in[l, j // 2, f])
                        if half is not None:
                            nl, nj = sub["next"]
                            unit(half * 4 + (u0 + u), nl, half * HB + 3 * nj * D, u)
                    w = w_ff_out[l, j // 2].rearrange("(s c p) n -> s p c n", c=2, p=P)
                    u0 += 16 if sub["next"] else 0
                else:
                    nl, nj = sub["next"]
                    src = w_in[l].rearrange("(k p) n -> p k n", p=P)
                    for s in range(7):
                        if s == 2:
                            load(n0 + 2, w_gates[l], KC * 16)
                        else:
                            c0 = (D // 2, 3 * D // 4, 0, 0, D // 4, D, 5 * D // 4)[s]
                            sp.wait_ge(S["w_lo"], n0 + s + START)
                            sp.dma_start(raw[:].rearrange("p (k n) -> p k n", k=KC), src[:, :, c0:c0 + 256]).then_inc(S["w_raw"], 16)
                        if s in (1, 3, 5, 6):
                            half = (1, 3, 5, 6).index(s)
                            for u in range(4):
                                unit(u0 + 4 * half + u, nl, 3 * nj * D + half * HB, u)
                    u0 += 16
                    w = w_out[l].rearrange("(s c p) n -> s p c n", c=2, p=P)
                for g in range(2):
                    for s, n, par, half, u, st in out_steps(sub, g, loop, (0, 0)):
                        sp.wait_ge(S["w_lo"], n + START)
                        sp.dma_start(raw[:].rearrange("p (c n) -> p c n", c=2), w[s]).then_inc(S["w_raw"], 16)
                        if half is not None:
                            for uu in u:
                                unit(half * 4 + (u0 + uu), l, half * HB + (3 * j + 2) * D, uu)
            for p_ in range(NTL):
                sp.wait_ge(S["x_new"], SUBS[-1]["y"] + p_ + 1)
                sp.dma_start(out[p_], x[:, p_, :]).then_inc(S["out_dma"], 16)
            sp.wait_ge(S["out_dma"], 16 * NTL)

        @block.gpsimd
        def _(pool):
            nc.gpsimd.memset(ones[:], 1.0)
            nc.gpsimd.memset(eps[:], EPS)
            nc.gpsimd.memset(ident[:], 0.0).then_inc(S["pool_consts"], 1)
            pool.wait_ge(S["pool_consts"], 1)
            nc.gpsimd.affine_select(out=ident[:], in_=ident[:], compare_op=ALU.not_equal, fill=1.0, base=0,
                                    pattern=[[-1, P]], channel_multiplier=1).then_inc(S["pool_consts"], 1)
            pool.wait_ge(S["x_in"], 16 * NT)
            for sub in SUBS:
                for i, t in enumerate(sum(tiles_of(sub), [])):
                    pool.wait_ge(S["gated"], sub["y"] + i + 1)
                    nc.gpsimd.tensor_tensor(x[:, t, :], x[:, t, :], ys(i % GT), ALU.add).then_inc(S["x_new"], 1)

        @block.scalar
        def _(act):
            loop = plain_loop(act)

            def split_w(n, par, width=SLOT):
                if isinstance(n, int) and n >= N_SLOTS:
                    return
                act.wait_ge(S["w_raw"], n * 16 + 16)
                if not isinstance(n, int) or n >= 2:
                    act.wait_ge(S["w_used"], n * 2 - 2 + START)
                nc.scalar.activation(w_hi[par][:, 0:width], raw[:, 0:width], ACT.Copy).then_inc(S["w_hi"], 1)

            def hj(sub, g, c, hs, b):
                w = sub["groups"][g] * P
                if g == 0:
                    if sub["kind"] == "ffn":
                        act.wait_ge(S["h_done"], c + (sub["proj"] + 1))
                    else:
                        act.wait_ge(S["mix_done"], HEADS * (sub["mix"] + 1))
                act.wait_ge(S["w_used"], hs - 1 + START)
                src = hid[:, g, c, 0:w] if isinstance(c, int) else hid[:, g, bass.ds(c, 1), 0:w].rearrange("p a w -> p (a w)")
                nc.scalar.activation(hj_hi[b][:, 0:w], src, ACT.Copy).then_inc(S["hj_hi"], 1)

            def stage(sub, g, s):
                tiles, y0, x0 = tiles_of(sub)[g], sub["y"] + g * GT, sub["xn"] + g * GT
                if 0 <= s - 3 < len(tiles) and not sub["final"]:
                    prenorm_split(x0 + s - 3, tiles[s - 3])
                if 0 <= s - 1 < len(tiles) and not sub["final"]:
                    prenorm_scale(x0 + s - 1, tiles[s - 1], s - 1)
                if 0 <= s < len(tiles):
                    act.wait_ge(S["y_sq"], y0 + s + 1)
                    nc.scalar.activation(stat[:, s, 1:2], stat[:, s, 0:1], ACT.Sqrt, bias=eps[:, 0:1]).then_inc(S["std1"], 1)
                    if not sub["final"]:
                        act.wait_ge(S["x_new"], y0 + s + 1)
                        prenorm_stat(x0 + s, tiles[s], s)

            def prenorm_stat(xi, t, i):
                nc.scalar.activation(dummy, x[:, t, :], ACT.Square, scale=1.0 / 32,
                                     accum_out=stat[:, i, 3:4]).then_inc(S["act_ms2"], 1)
                act.wait_ge(S["act_ms2"], xi + 1)
                nc.scalar.activation(stat[:, i, 4:5], stat[:, i, 3:4], ACT.Sqrt, bias=eps[:, 0:1]).then_inc(S["std2"], 1)

            def prenorm_scale(xi, t, i):
                act.wait_ge(S["rs2"], xi + 1)
                nc.scalar.activation(ys(i), x[:, t, :], ACT.Copy, scale=stat[:, i, 5:6]).then_inc(S["xs"], 1)

            def prenorm_split(xi, t):
                act.wait_ge(S["modded"], xi + 1)
                nc.scalar.activation(xn_hi[:, :, t * P:(t + 1) * P], ps[:, 6:8, :].rearrange("p b (c w) -> p (b c) w", w=P),
                                     ACT.Copy).then_inc(S["xn_hi"], 1)

            def evacuate(sub, g):
                for i in range(sub["groups"][g]):
                    act.wait_ge(S["y_copied"], sub["y"] + g * GT + i + 1)
                    nc.scalar.activation(dummy, ys(i), ACT.Square, scale=1.0 / 32, accum_out=stat[:, i, 0:1]).then_inc(S["y_sq"], 1)
                    act.wait_ge(S["y_sq"], sub["y"] + g * GT + i + 1)

            def load_constants(sub):
                l, j = sub["l"], sub["j"]
                if sub["y"]:
                    act.wait_ge(S["x_new"], sub["y"])
                nw = norm_w[l, 2 * j + 1:2 * j + 2, :]
                for s in range(2):
                    act.dma_start(gate_row[:, s, :], nw.to_broadcast([P, D])).then_inc(S["gate_in"], 16)
                act.dma_start(b_gate[:], b_ada[l, (3 * j + 2) * D:(3 * j + 3) * D].rearrange("(a b) -> a b", b=P)).then_inc(S["gate_in"], 16)
                if sub["kind"] == "mix":
                    act.wait_ge(S["xn_done"], sub["xn"])
                    act.dma_start(qkv_w, w_qkv[l].rearrange("a h d e -> d a h e")).then_inc(S["mix_const"], 16)
                    for dst, src in ((fmix_w, fmix_in[l]), (dft_g, dft_g_in), (tri, tri_in)):
                        act.dma_start(dst, src).then_inc(S["mix_const"], 16)

            for t in range(NT):
                act.dma_start(x[:, t, :], x_in[t]).then_inc(S["x_in"], 16)
            act.wait_ge(S["consts"], 16 * 8)
            nc.scalar.activation(silu_c[:], cvec[:], ACT.Silu).then_inc(S["silu_c"], 1)
            act.wait_ge(S["x_in"], 16 * NT)
            act.wait_ge(S["pool_consts"], 2)
            for t in range(NT):
                prenorm_stat(t, t, t)
            for t in range(NT):
                prenorm_scale(t, t, t)
            split_w(0, 0)
            split_w(1, 1)
            for t in range(NT):
                prenorm_split(t, t)

            for sub in SUBS:
                l, j, n0 = sub["l"], sub["j"], sub["slot"]
                par0 = n0 % 2
                load_constants(sub)
                if sub["kind"] == "ffn":
                    for f, n, s, half, u in in_steps(sub, loop, (0, 0)):
                        if not (isinstance(f, int) and f == 0):
                            split_w(n + 1, (par0 + s + 1) % 2)
                        act.wait_ge(S["w_used"], n * 2 + 2 + START)
                        for g in range(2):
                            w = sub["in_groups"][g] * P
                            dst = hid[:, g, bass.ds(f, 1), 0:w].rearrange("p a w -> p (a w)")
                            ins = nc.scalar.activation(dst, ps[:, (s % 2) * 4 + 2 * g, 0:w], ACT.Silu)
                        ins.then_inc(S["silu"], 1)
                else:
                    mixer_act(act, sub, split_w)
                for g in range(2):
                    nb = n0 + sub["in_slots"] + g * sub["k_slots"]
                    pb = nb % 2
                    hj(sub, g, 0, 2 * nb, 0)
                    if g == 1:
                        evacuate(sub, 0)
                    done = 0
                    for s, n, par, half, u, st in out_steps(sub, g, loop, (0, 0)):
                        hj(sub, g, s * 2 + 1, n * 2 + 1, 1)
                        split_w(n + 1, (pb + par + 1) % 2)
                        if not (isinstance(s, int) and s == sub["k_slots"] - 1):
                            hj(sub, g, s * 2 + 2, n * 2 + 2, 0)
                        if st is not None:
                            stage(sub, 0, st)
                            done = st + 1
                for s in range(done, norm_stages(sub, 0)):
                    stage(sub, 0, s)
                evacuate(sub, 1)
                split_w(n0 + sub["in_slots"] + 2 * sub["k_slots"] + 1, (par0 + sub["in_slots"] + 1) % 2)
                for s in range(norm_stages(sub, 1)):
                    stage(sub, 1, s)

        @block.vector
        def _(dve):
            own = Count(dve, S["dve"])
            dve.sem_inc(S["w_lo"], START)
            dve.sem_inc(S["ada_used"], START)

            def split_w(n, par, width=SLOT):
                if isinstance(n, int) and n >= N_SLOTS:
                    return
                dve.wait_ge(S["w_hi"], n + 1)
                if not isinstance(n, int) or n >= 2:
                    dve.wait_ge(S["w_used"], n * 2 - 2 + START)
                nc.vector.tensor_tensor(w_lo[par][:, 0:width], raw[:, 0:width], w_hi[par][:, 0:width].bitcast(F32),
                                        ALU.subtract).then_inc(S["w_lo"], 1)

            def hj(sub, g, c, q, hs, b):
                w = sub["groups"][g] * P
                dve.wait_ge(S["hj_hi"], q + 1)
                dve.wait_ge(S["w_used"], hs - 1 + START)
                src = hid[:, g, c, 0:w] if isinstance(c, int) else hid[:, g, bass.ds(c, 1), 0:w].rearrange("p a w -> p (a w)")
                nc.vector.tensor_tensor(hj_lo[b][:, 0:w], src, hj_hi[b][:, 0:w].bitcast(F32), ALU.subtract).then_inc(S["hj_lo"], 1)

            def unit(count, u):
                if u == 0:
                    own.link(nc.vector.memset(acc[:], 0.0))
                dve.wait_ge(S[f"ada_raw{u % 2}"], (count - u % 2) * 8 + 16)
                for c in range(2):
                    for s in range(2):
                        k = 2 * u + c
                        if c == 1:
                            own.wait_back(1)
                        elif u and s == 0:
                            own.wait_back(0)
                        elif u:
                            dve.wait_ge(S["ada_used"], count + START)
                        ins = nc.vector.scalar_tensor_tensor(out=acc[:, s, :], in0=raw_ada[u % 2][:, c, :], scalar=silu_c[:, k, s:s + 1],
                                                             in1=acc[:, s, :], op0=ALU.mult, op1=ALU.add)
                        if c == 1 and s == 1:
                            ins.then_inc(S["ada_used"], 1)
                        else:
                            own.mark(ins)

            def finish_col(half, i, b_off, l, bank_):
                dve.wait_ge(S["fin_mm"], half + 1)
                bias = b_col[:, l, bass.ds(i * 4 + b_off, 4)].unsqueeze(2).to_broadcast([P, 4, 2])
                dst = mcol[:, bass.ds(i, 1), :, :].rearrange("p a c s -> p (a c) s")
                nc.vector.tensor_tensor(dst, ps[:, bank_, GW:GW + 8].rearrange("p (c s) -> p c s", s=2), bias,
                                        ALU.add).then_inc(S["fin_read"], 1)

            def finish_gate(half, i, b0, factor, sub):
                dve.wait_ge(S["fin_mm"], half + 1)
                dve.wait_ge(S["gate_in"], 48 * (sub["gate"] + 1))
                for s in range(2):
                    row = gate_row[:, s, bass.ds(i * HB, HB)]
                    ins = nc.vector.scalar_tensor_tensor(out=row, in0=ps[:, b0 + s, :], scalar=factor, in1=row,
                                                         op0=ALU.mult, op1=ALU.mult)
                ins.then_inc(S["fin_read"], 1)

            def make_mod(l, j, half):
                dve.wait_ge(S["fin_read"], half)
                nc.vector.tensor_copy(m_shift[:], mcol[:, 0:2].rearrange("p a c s -> p (a c) s"))
                own.link(nc.vector.scalar_tensor_tensor(
                    out=m_scale[:], in0=mcol[:, 2:4].rearrange("p a c s -> p (a c) s"), scalar=1.0,
                    in1=nw_col[:, l, j, :].unsqueeze(2).to_broadcast([P, KC, 2]), op0=ALU.add, op1=ALU.mult))

            def prenorm_rs(xi, i):
                dve.wait_ge(S["std2"], xi + 1)
                nc.vector.reciprocal(stat[:, i, 5:6], stat[:, i, 4:5]).then_inc(S["rs2"], 1)

            def prenorm_mod(xi, t):
                s = 0 if t < NTL else 1
                tile = ps[:, 6:8, :].rearrange("p b (c w) -> p (b c) w", w=P)
                dve.wait_ge(S["xT"], xi + 1)
                own.link(nc.vector.tensor_tensor(tile, tile, m_scale[:, :, s].unsqueeze(2).to_broadcast([P, KC, P]), ALU.mult))
                nc.vector.tensor_tensor(tile, tile, m_shift[:, :, s].unsqueeze(2).to_broadcast([P, KC, P]),
                                        ALU.add).then_inc(S["modded"], 1)
                dve.wait_ge(S["xn_hi"], xi + 1)
                nc.vector.tensor_tensor(xn_lo[:, :, t * P:(t + 1) * P], tile, xn_hi[:, :, t * P:(t + 1) * P].bitcast(F32),
                                        ALU.subtract).then_inc(S["xn_done"], 1)

            def stage(sub, g, s):
                tiles, y0, x0 = tiles_of(sub)[g], sub["y"] + g * GT, sub["xn"] + g * GT
                if 0 <= s - 3 < len(tiles) and not sub["final"]:
                    prenorm_mod(x0 + s - 3, tiles[s - 3])
                if 0 <= s - 1 < len(tiles) and not sub["final"]:
                    prenorm_rs(x0 + s - 1, s - 1)
                if 0 <= s < len(tiles):
                    t = tiles[s]
                    dve.wait_ge(S["std1"], y0 + s + 1)
                    own.link(nc.vector.reciprocal(stat[:, s, 2:3], stat[:, s, 1:2]))
                    nc.vector.scalar_tensor_tensor(out=ys(s), in0=ys(s), scalar=stat[:, s, 2:3],
                                                   in1=gate_row[:, 0 if t < NTL else 1, :], op0=ALU.mult, op1=ALU.mult
                                                   ).then_inc(S["gated"], 1)

            def evacuate(sub, g):
                n_end = sub["slot"] + sub["in_slots"] + (g + 1) * sub["k_slots"]
                dve.wait_ge(S["w_used"], 2 * n_end + START)
                if sub["y"] + g * GT:
                    dve.wait_ge(S["x_new"], sub["y"] + g * GT)
                for i in range(sub["groups"][g]):
                    nc.vector.tensor_copy(ys(i), ps[:, 2 * i:2 * i + 2, :].rearrange("p b n -> p (b n)")).then_inc(S["y_copied"], 1)
                dve.wait_ge(S["y_copied"], sub["y"] + g * GT + sub["groups"][g])

            dve.wait_ge(S["consts"], 16 * 8)
            dve.wait_ge(S["pool_consts"], 2)
            nc.vector.tensor_copy(ident_bf[:], ident[:])
            nc.vector.tensor_scalar(mask[:], tri, -1.0, -NEG, ALU.add, ALU.mult).then_inc(S["dve_consts"], 1)
            for t in range(NT):
                prenorm_rs(t, t)
            for i in range(4):
                dve.wait_ge(S["rows_mm"], i + 1)
                nc.vector.tensor_copy(acc[0:2, i % 2, :], ps[0:2, 5, :]).then_inc(S["rows_sb"], 1)
                finish_col(i, i, 0, 0, 6)
            make_mod(0, 0, 4)
            split_w(0, 0)
            split_w(1, 1)
            for t in range(NT):
                prenorm_mod(t, t)

            for sub in SUBS:
                l, j, n0 = sub["l"], sub["j"], sub["slot"]
                par0 = n0 % 2
                u0, half0 = sub["unit"], sub["half"]
                if sub["kind"] == "ffn":
                    for f, n, s, half, u in in_steps(sub, own.loop, (13, 0)):
                        if not (isinstance(f, int) and f == 0):
                            split_w(n + 1, (par0 + s + 1) % 2)
                        if half is not None:
                            unit(half * 4 + (u0 + u), u)
                        dve.wait_ge(S["silu"], f + (sub["proj"] + 1))
                        for g in range(2):
                            w = sub["in_groups"][g] * P
                            hd = hid[:, g, bass.ds(f, 1), 0:w].rearrange("p a w -> p (a w)")
                            ins = nc.vector.tensor_tensor(hd, hd, ps[:, (s % 2) * 4 + 2 * g + 1, 0:w], ALU.mult)
                        ins.then_inc(S["h_done"], 1)
                        if half is not None and u == 3:
                            finish_col(half + half0, half, 3 * sub["next"][1] * KC, sub["next"][0], 0)
                else:
                    mixer_dve(dve, own, sub, split_w, unit, finish_col)
                if sub["next"]:
                    make_mod(*sub["next"], half0 + 4)
                    u0, half0 = u0 + 16, half0 + 4
                for g in range(2):
                    nb = n0 + sub["in_slots"] + g * sub["k_slots"]
                    q0 = sub["hj"] + g * 2 * sub["k_slots"]
                    pb = nb % 2
                    hj(sub, g, 0, q0, 2 * nb, 0)
                    if g == 1:
                        evacuate(sub, 0)
                    done = 0
                    for s, n, par, half, u, st in out_steps(sub, g, own.loop, (13, 0)):
                        hj(sub, g, s * 2 + 1, s * 2 + (q0 + 1), n * 2 + 1, 1)
                        split_w(n + 1, (pb + par + 1) % 2)
                        if not (isinstance(s, int) and s == sub["k_slots"] - 1):
                            hj(sub, g, s * 2 + 2, s * 2 + (q0 + 2), n * 2 + 2, 0)
                        if half is not None:
                            for uu in u:
                                unit(half * 4 + (u0 + uu), uu)
                            if u[-1] == 3:
                                finish_gate(half + half0, half, 6, 0.5 if sub["kind"] == "ffn" else 1.0, sub)
                        if st is not None:
                            stage(sub, 0, st)
                            done = st + 1
                for s in range(done, norm_stages(sub, 0)):
                    stage(sub, 0, s)
                evacuate(sub, 1)
                split_w(n0 + sub["in_slots"] + 2 * sub["k_slots"] + 1, (par0 + sub["in_slots"] + 1) % 2)
                for s in range(norm_stages(sub, 1)):
                    stage(sub, 1, s)

        @block.tensor
        def _(pe):
            loop = plain_loop(pe)
            mm = nc.tensor.matmul
            pe.sem_inc(S["w_used"], START)

            def project_in(n, par, b, widths, groups=(0, 1)):
                pe.wait_ge(S["w_lo"], n + 1 + START)
                hi = w_hi[par][:].rearrange("p (k c n) -> p k c n", k=KC, c=2)
                lo = w_lo[par][:].rearrange("p (k c n) -> p k c n", k=KC, c=2)
                for c in range(2):
                    for k in range(KC):
                        for i, (w, xx) in enumerate(((hi, xn_hi), (hi, xn_lo), (lo, xn_hi))):
                            for g in groups:
                                wd = widths[g] * P
                                ins = mm(ps[:, 4 * b + 2 * g + c, 0:wd], w[:, k, c, :], xx[:, k, g * GW:g * GW + wd],
                                         start=(k == 0 and i == 0), stop=(k == KC - 1 and i == 2))
                if 1 in groups:
                    ins.then_inc(S["w_used"], 2)

            def project_out(sub, g, s, n, par, q0, first, last):
                hi = w_hi[par][:].rearrange("p (c n) -> p c n", c=2)
                lo = w_lo[par][:].rearrange("p (c n) -> p c n", c=2)
                pe.wait_ge(S["w_lo"], n + 1 + START)
                for c in range(2):
                    pe.wait_ge(S["hj_lo"], s * 2 + (q0 + c + 1))
                    for i in range(sub["groups"][g]):
                        for a, (xx, w) in enumerate(((hj_hi[c], hi), (hj_hi[c], lo), (hj_lo[c], hi))):
                            for hf in range(2):
                                ins = mm(ps[:, 2 * i + hf, :], xx[:, i * P:(i + 1) * P], w[:, c, hf * 512:(hf + 1) * 512],
                                         start=first and c == 0 and a == 0, stop=last and c == 1 and a == 2,
                                         skip_group_check=True)
                    ins.then_inc(S["w_used"], 1)

            def finish_col(half, units, bank_):
                pe.wait_ge(S["ada_used"], units + START)
                pe.wait_ge(S["fin_read"], half)
                for c in range(4):
                    for s in range(2):
                        ins = mm(ps[:, bank_, GW + 2 * c + s:GW + 2 * c + s + 1], acc[:, s, c * P:(c + 1) * P], ones[:, 0:1],
                                 start=True, stop=True)
                ins.then_inc(S["fin_mm"], 1)

            def finish_gate(half, units, i, b0, sub):
                pe.wait_ge(S["ada_used"], units + START)
                pe.wait_ge(S["fin_read"], half)
                pe.wait_ge(S["gate_in"], 48 * (sub["gate"] + 1))
                for s in range(2):
                    mm(ps[:, b0 + s, :], ones[:, 0:1].to_broadcast([P, P]), acc[:, s, :], start=True, stop=False)
                    for c in range(4):
                        ins = mm(ps[:, b0 + s, c * P:(c + 1) * P], ident[0:KC, 4 * i + c:4 * i + c + 1].to_broadcast([KC, P]),
                                 b_gate[:], start=False, stop=(c == 3))
                ins.then_inc(S["fin_mm"], 1)

            def turn(xi, i, half):
                pe.wait_ge(S["xs"], xi + 1)
                if xi:
                    pe.wait_ge(S["xn_done"], xi)
                pe.wait_ge(S["fin_read"], half)
                for c in range(KC):
                    ins = nc.tensor.transpose(ps[:, 6 + c // 4, (c % 4) * P:(c % 4 + 1) * P], ys(i)[:, c * P:(c + 1) * P], ident[:])
                ins.then_inc(S["xT"], 1)

            pe.wait_ge(S["pool_consts"], 2)
            pe.wait_ge(S["dve_consts"], 1)
            pe.wait_ge(S["silu_c"], 1)
            for i in range(4):
                pe.wait_ge(S["ada_first"][i], 16)
                for k in range(KC):
                    ins = mm(ps[0:2, 5, :], silu_c[:, k, :], ada0(i)[:, k, :], start=(k == 0), stop=(k == KC - 1))
                ins.then_inc(S["rows_mm"], 1)
                pe.wait_ge(S["rows_sb"], i + 1)
                if i:
                    pe.wait_ge(S["fin_read"], i)
                for c in range(4):
                    ins = nc.tensor.transpose(ps[:, 6, GW + 2 * c:GW + 2 * c + 2], acc[0:2, i % 2, c * P:(c + 1) * P], ident[0:2, 0:2])
                ins.then_inc(S["fin_mm"], 1)
            for t in range(NT):
                turn(t, t, 4)

            for sub in SUBS:
                n0, half0, u0 = sub["slot"], sub["half"], sub["unit"]
                par0 = n0 % 2
                if sub["kind"] == "ffn":
                    first = sub is SUBS[0]
                    x0 = sub["xn"] - (sub["in_groups"][1] if not first else 0)
                    for f, n, s, half, u in in_steps(sub, loop, (0, 0)):
                        if isinstance(f, int) and f < 2:
                            if f == 0:
                                pe.wait_ge(S["xn_done"], x0)
                                pe.wait_ge(S["y_copied"], sub["y"]) if sub["y"] else None
                                project_in(n, par0, 0, sub["in_groups"], (0,))
                                if not first:
                                    turn(x0, 0, half0)
                                project_in(n + 1, 1 - par0, 1, sub["in_groups"], (0,))
                                if not first:
                                    for i in range(1, sub["in_groups"][1]):
                                        turn(x0 + i, i, half0)
                                pe.wait_ge(S["xn_done"], sub["xn"])
                            project_in(n, (par0 + f) % 2, f, sub["in_groups"], (1,))
                            continue
                        pe.wait_ge(S["h_done"], f + (sub["proj"] - 1))
                        project_in(n, (par0 + s) % 2, s % 2, sub["in_groups"])
                        if half is not None and u == 3:
                            finish_col(half + half0, half * 4 + (u0 + 4), 0)
                            pe.wait_ge(S["fin_read"], half + (half0 + 1))
                    pe.wait_ge(S["h_done"], sub["proj"] + FC)
                else:
                    mixer_pe(pe, sub, finish_col, turn)
                if sub["next"]:
                    u0, half0 = u0 + 16, half0 + 4
                for g in range(2):
                    nb = n0 + sub["in_slots"] + g * sub["k_slots"]
                    q0 = sub["hj"] + g * 2 * sub["k_slots"]
                    pb = nb % 2
                    if g == 1:
                        pe.wait_ge(S["y_copied"], sub["y"] + GT)
                    done = 0
                    for s, n, par, half, u, st in out_steps(sub, g, loop, (0, 0)):
                        dyn = not isinstance(s, int)
                        project_out(sub, g, s, n, (pb + par) % 2, q0,
                                    first=(not dyn and s == 0), last=(not dyn and s == sub["k_slots"] - 1))
                        if half is not None and u[-1] == 3:
                            finish_gate(half + half0, half * 4 + (u0 + 4), half, 6, sub)
                        if st is not None and not sub["final"]:
                            if 0 <= st - 2 < GT:
                                turn(sub["xn"] + st - 2, st - 2, sub["half_end"])
                            done = st + 1
                if not sub["final"]:
                    nh = sub["half_end"]
                    for s in range(max(2, done), GT + 2):
                        turn(sub["xn"] + s - 2, s - 2, nh)

def kernel(x, c, ctx, c_ctx, w_ada, b_ada, norm_w, w_ff_in, w_ff_out, w_in, w_fmix, conv_w, conv_b, w_qkv, gate_b,
           mlstm_norm_w, w_out):
    import concourse.bacc as bacc
    from concourse.bass_utils import run_bass_kernel_spmd

    def cols(a, n):
        a = a.reshape(a.shape[:-1] + (n, P))
        return np.ascontiguousarray(np.moveaxis(a, -1, 0))

    def dft(s, norm):
        a = np.outer(np.arange(s), np.arange(s)) % s * (2 * np.pi / s)
        both = np.stack([np.cos(a), -np.sin(a)], 1) / norm
        return np.ascontiguousarray(both.reshape(s // P, P, 2, s).transpose(1, 0, 2, 3).astype(np.float32))

    group = D // 2 // 8
    ag = np.outer(np.arange(group), np.arange(group)) % group * (2 * np.pi / group)
    dft_g = np.zeros((P, 2 * P), np.float32)
    fmix = np.zeros((DEPTH, P, 4, P), np.float32)
    for i in range(2):
        s = slice(i * group, (i + 1) * group)
        dft_g[s, s] = np.cos(ag)
        dft_g[s, P + i * group:P + (i + 1) * group] = np.sin(ag)
        fmix[:, s, :, s] = np.asarray(w_fmix)[:, i::2].transpose(0, 2, 1, 3)
    tri = np.stack([np.triu(np.ones((P, P), np.float32)), np.tril(np.ones((P, P), np.float32))], 1)
    arrays = {
        "x_in": np.concatenate([np.asarray(x)[0], np.asarray(ctx)[0]]).reshape(NT, P, D),
        "w_ada": np.asarray(w_ada),
        "norm_w": np.asarray(norm_w),
        "w_ff_in": np.ascontiguousarray(np.asarray(w_ff_in).reshape(DEPTH, 2, KC, P, 2, FC, P).transpose(0, 1, 5, 3, 2, 4, 6)
                                        ).reshape(DEPTH, 2, FC, P, SLOT),
        "w_ff_out": np.asarray(w_ff_out),
        "w_in": np.asarray(w_in),
        "w_gates": np.ascontiguousarray(np.asarray(w_in)[:, :, 1536:].reshape(DEPTH, KC, P, 16).transpose(0, 2, 1, 3)
                                        ).reshape(DEPTH, P, KC * 16),
        "w_out": np.asarray(w_out),
        "w_qkv": np.asarray(w_qkv),
        "b_ada": np.asarray(b_ada),
        "cvec_in": np.ascontiguousarray(np.stack([np.asarray(c)[0], np.asarray(c_ctx)]).reshape(2, KC, P).transpose(2, 1, 0)),
        "gate_b_in": np.ascontiguousarray(np.broadcast_to(np.asarray(gate_b).reshape(1, DEPTH, 16), (P, DEPTH, 16))),
        "b_col_in": cols(np.asarray(b_ada), 9 * KC),
        "nw_col_in": cols(np.asarray(norm_w)[:, 0::2], KC),
        "convw_in": np.ascontiguousarray(np.asarray(conv_w).reshape(DEPTH, 9, HEADS, P).transpose(3, 0, 2, 1)),
        "convb_in": cols(np.asarray(conv_b), HEADS),
        "hn_w_in": cols(np.asarray(mlstm_norm_w), HEADS),
        "fmix_in": fmix,
        "dft_l_in": dft(SEQ, np.sqrt(SEQ * group)),
        "dft_c_in": dft(CTX, np.sqrt(CTX * group)),
        "dft_g_in": dft_g,
        "tri_in": np.ascontiguousarray(tri),
    }
    nc = bacc.Bacc("TRN2", target_bir_lowering=False, num_devices=1)
    args = {k: nc.dram_tensor(k, a.shape, mybir.dt.from_np(a.dtype), kind="ExternalInput").ap() for k, a in arrays.items()}
    args["out"] = nc.dram_tensor("out", (NTL, P, D), F32, kind="ExternalOutput").ap()
    build(nc, **args)
    r = run_bass_kernel_spmd(nc, [arrays], core_ids=[0])
    return r.results[0]["out"].reshape(1, SEQ, D)
```

```python
from contextlib import ExitStack, contextmanager

import numpy as np

import concourse.bass as bass
from concourse import mybir

F32 = mybir.dt.float32
F32R = mybir.dt.float32r
BF16 = mybir.dt.bfloat16
ALU = mybir.AluOpType
ACT = mybir.ActivationFunctionType
AX_X = mybir.AxisListType.X

P = 128
D = 1024
KC = D // P
SEQ, CTX = 512, 256
TOK = SEQ + CTX
NT, NTL = TOK // P, SEQ // P
DEPTH = 2
D_FF = 2816
FC = D_FF // P
HEADS, HD = 4, 128
GW = 384
GT = GW // P
SLOT = 2048
HB = 512
EPS = 1e-6
NEG = -1e30
START = 1
HV = HD + 1

XN = 2 * KC * TOK
HG = FC * GW
A_H = XN
A_YS = A_H + 8 * GW
A_DUMMY = A_YS + 3 * D
A_XM = A_YS
A_QKVW = A_XM + HEADS * TOK
A_FW = A_QKVW + 12 * P
A_TRI = A_FW + 4 * P
A_DFTG = A_H + 2 * HG - 256
A_CONV = A_H + HG + 8 * GW
A_GATE = A_CONV + HEADS * TOK
A_DFT = 0
A_XAB = A_DFT + 8 * SEQ + 4 * CTX
A_HEAD = A_XAB + NT * 256


HALVES = 9 * D // HB
ADA_IN = {(0, 0): [(0, 4, 10)], (0, 2): [(0, 16, 2), (1, 0, 8)], (1, 0): [(1, 10, 8)]}
ADA_OUT = {(0, 0): (0, 14), (0, 2): (1, 8)}


def plan():
    subs = []
    slot = hj = y = proj = mix = gate = 0
    xn = NT
    for l in range(DEPTH):
        for j in range(3):
            kind = "mix" if j == 1 else "ffn"
            last = l == DEPTH - 1
            final = last and j == 2
            groups = [NTL] if final else [GT, NTL - GT] if last and j == 1 else [GT, GT]
            k_slots = 4 if kind == "mix" else FC // 2
            s = dict(l=l, j=j, kind=kind, final=final, groups=groups, k_slots=k_slots, slot=slot, hj=hj, y=y,
                     xn=xn, proj=proj, mix=mix, gate=gate,
                     next=None if final else ((l, j + 1) if j < 2 else (l + 1, 0)))
            s["in_slots"] = 7 if kind == "mix" else FC
            s["in_groups"] = [GT, NTL - GT] if final else [GT, GT]
            s["late"] = s["in_groups"][1]
            s["ada_in"], s["ada_out"] = ADA_IN.get((l, j), []), ADA_OUT.get((l, j))
            subs.append(s)
            slot += s["in_slots"] + len(groups) * k_slots
            hj += 2 * len(groups) * k_slots
            y += sum(groups)
            xn += 0 if final else sum(groups)
            gate += 1
            if kind == "mix":
                mix += 1
            else:
                proj += FC
    return subs


SUBS = plan()


class Count:

    def __init__(self, eng, sem):
        self.eng, self.sem, self.n, self.term = eng, sem, 0, 0

    def mark(self, ins):
        ins.then_inc(self.sem, 1)
        self.n += 1

    def wait(self):
        self.eng.wait_ge(self.sem, self.n + self.term)

    def link(self, ins):
        self.mark(ins)
        self.wait()

    def wait_back(self, back):
        self.eng.wait_ge(self.sem, self.n - back + self.term)

    @contextmanager
    def loop(self, trips, per):
        base = self.n
        with self.eng.Fori(0, trips) as i:
            self.term = i * per
            yield i
        assert self.n - base == per, (self.n - base, per)
        self.term = 0
        self.n = base + trips * per


def scan_k(d, t):
    return (t + 2) % NT if d == 0 else NT - 1 - t


def scan_t(d, k):
    return (k + 4) % NT if d == 0 else NT - 1 - k


def scan_col(d, k, h):
    return d * 32 + k * 4 + h


def tiles_of(sub):
    first = sub["groups"][0]
    return [list(range(first)), list(range(first, sum(sub["groups"])))]


def build(nc, x_in, w_ada, norm_w, w_ff_in, w_ff_out, w_in, w_gates, w_out, w_qkv, cvec_in, gate_b_in,
          b_col_in, nw_col_in, convw_in, convb_in, hn_w_in, fmix_in, dft_l_in, dft_c_in, dft_g_in, tri_in, out):
    ctx = ExitStack()
    with ctx:
        def sb(name, shape, dt=F32):
            return ctx.enter_context(nc.sbuf_tensor(name, shape, dt))

        x = sb("x", [P, NT, D])
        inner = ExitStack()
        xn_hi = inner.enter_context(nc.sbuf_tensor("xn_hi", [P, KC, TOK], F32R))
        xn_lo = inner.enter_context(nc.sbuf_tensor("xn_lo", [P, KC, TOK], F32R))
        inner.close()
        arena = sb("arena", [P, XN + 2 * HG])
        hj_hi = [sb(f"hj_hi{i}", [P, GW], F32R) for i in range(2)]
        hj_lo = [sb(f"hj_lo{i}", [P, GW], F32R) for i in range(2)]
        raw = sb("raw", [P, SLOT])
        w_hi = [sb(f"w_hi{i}", [P, SLOT], F32R) for i in range(2)]
        w_lo = [sb(f"w_lo{i}", [P, SLOT], F32R) for i in range(2)]
        raw_ada = [sb(f"raw_ada{i}", [P, 2, HB]) for i in range(2)]
        acc = sb("acc", [P, 2, HB])
        gate_row = sb("gate_row", [P, 2, D])
        ident = sb("ident", [P, P])
        mask = sb("mask", [P, 2, P], BF16)
        ident_bf = sb("ident_bf", [P, P], BF16)
        ones = sb("ones", [P, 8])
        cvec = sb("cvec", [P, KC, 2])
        silu_c = sb("silu_c", [P, KC, 2])
        b_col = sb("b_col", [P, DEPTH * HALVES * 4])
        nw_col = sb("nw_col", [P, DEPTH, 3, KC])
        vecs = sb("vecs", [P, HALVES, 4, 2])
        m_scale = sb("m_scale", [P, KC, 2])
        m_shift = sb("m_shift", [P, KC, 2])
        stat = sb("stat", [P, 6, 8])
        convw = sb("convw", [P, DEPTH, HEADS, 9])
        convb = sb("convb", [P, DEPTH, HEADS])
        hn_w = sb("hn_w", [P, DEPTH, HEADS])
        gate_b = sb("gate_b", [P, DEPTH, 16])
        eps = sb("eps", [P, 1])
        ps = ctx.enter_context(nc.psum_tensor("ps", [P, 8, 512], F32))

        def at(off, n):
            return arena[:, off:off + n]

        hid = at(A_H, 2 * HG).rearrange("p (g c w) -> p g c w", g=2, c=FC)
        hid_w = at(A_H, FC * SEQ).rearrange("p (c w) -> p c w", c=FC)
        dummy = at(A_DUMMY, D)

        def hidden(sub, g, c):
            w = sub["groups"][g] * P
            src = hid_w if sub["final"] else hid[:, g]
            return src[:, c, 0:w] if isinstance(c, int) else src[:, bass.ds(c, 1), 0:w].rearrange("p a w -> p (a w)")

        def split_h(sub, b):
            if sub["final"]:
                return xn_hi[:, b, 0:SEQ], xn_lo[:, b, 0:SEQ]
            return hj_hi[b][:], hj_lo[b][:]

        def ada0(i):
            off = i * KC * HB if i < 3 else A_TRI + 2 * P
            return at(off, KC * HB).rearrange("p (k n) -> p k n", k=KC)

        def ys(i):
            return at(A_YS + i * D, D) if i < 3 else at(A_H + (i - 3) * D, D)

        mixT = hid
        xmT = at(A_XM, HEADS * TOK).rearrange("p (h t) -> p h t", h=HEADS)
        convT = at(A_CONV, HEADS * TOK).rearrange("p (h t) -> p h t", h=HEADS)
        qkv_w = at(A_QKVW, 12 * P).rearrange("p (a h e) -> p a h e", a=3, h=HEADS)
        fmix_w = at(A_FW, 4 * P).rearrange("p (f n) -> p f n", f=4)
        dft_l = at(A_DFT, 8 * SEQ).rearrange("p (t c s) -> p t c s", t=4, c=2)
        dft_c = at(A_DFT + 8 * SEQ, 4 * CTX).rearrange("p (t c s) -> p t c s", t=2, c=2)
        dft_g = at(A_DFTG, 256)
        tri = at(A_TRI, 2 * P).rearrange("p (d t) -> p d t", d=2)
        xab = at(A_XAB, NT * 256).rearrange("p (t n) -> p t n", t=NT)
        place = {"gate": A_GATE, "head": A_HEAD}

        def small(n, which="gate", end=A_DFTG):
            place[which] += n
            assert place[which] <= end
            return at(place[which] - n, n)

        ab = at(A_GATE, 256)
        g16 = small(NT * 16)
        g_abs = small(48).rearrange("p (a h) -> p a h", h=4)
        lfs = small(64).rearrange("p (d k h) -> p d k h", d=2, k=8)
        igs = small(64).rearrange("p (d k h) -> p d k h", d=2, k=8)
        b_tok = small(64)
        r_tok = small(64)
        r_row = small(P)
        cm_row = small(P)
        m_row = small(P)
        nm_row = small(P)
        d_row = small(P)
        rw_row = small(P)
        p0 = small(6 * 64)
        rmax0, btot0, m0, mprev0, mlast0, dec0 = (p0[0:1, 64 * i:64 * i + 64] for i in range(6))
        cols = small(4)
        dec = small(64)
        em_arg = small(64)
        wi, em, wst = (small(48).rearrange("p (d t h) -> p d t h", d=2, t=NT) for _ in range(3))

        def head(n):
            return small(n, "head", XN)

        qT, kT = head(TOK), head(TOK)
        ktok = head(TOK).rearrange("p (t n) -> p t n", t=NT)
        vtok = head(NT * HV).rearrange("p (t n) -> p t n", t=NT)
        wv = head(NT * HV).rearrange("p (t n) -> p t n", t=NT)
        wt = head(TOK).rearrange("p (t n) -> p t n", t=NT)
        cst = head(NT * HV).rearrange("p (k n) -> p k n", k=NT)
        num = wv
        bn = small(NT * 6).rearrange("p (t n) -> p t n", t=NT)
        mv = small(NT * 2).rearrange("p (t n) -> p t n", t=NT)
        den = small(4 * NT).rearrange("p (a t) -> p a t", a=4)

        def hsum(h):
            return convT[:, h, :].rearrange("p (t n) -> p t n", t=NT)

        S = {}
        for name in (
            "consts pool_consts dve_consts x_in "
            "w_raw w_hi w_lo w_used "
            "ada_raw0 ada_raw1 ada_used fin_mm fin_read row_mm row_read silu_c "
            "silu h_done hj_hi hj_lo "
            "y_sq y_copied std1 x_new std2 rs2 xs xT modded xn_hi xn_done "
            "gated gate_in dft_in rows_sb rows_mm out_dma dve act_ms act_ms2 "
            "win_evac mix_const g_cp g_tok g_abs g_exp g_ln g_lf g_b g_r g_rT g_rmx g_rr g_m g_dec g_bc g_rows g_T g_arg g_w "
            "ab_mm ab_sb xab_mm xab_sb f_mm f_sb conv conv_silu "
            "qkv_mm qkv_sb st_mm mb_mm wt_sb wv_sb cloc_mm cst_sb p_sb io_mm comb hvar hstd hn hnT mix_done"
        ).split():
            S[name] = ctx.enter_context(nc.semaphore("s_" + name))

        S["ada_first"] = [ctx.enter_context(nc.semaphore(f"s_ada_first{i}")) for i in range(4)]
        N_SLOTS = SUBS[-1]["slot"] + SUBS[-1]["in_slots"] + SUBS[-1]["k_slots"]
        block = ctx.enter_context(nc.Block())

        def in_steps(sub, loop, per):
            n0 = sub["slot"]
            for s in range(2):
                yield s, n0 + s, s, None
            done = 2
            for l, h0, count in sub["ada_in"]:
                with loop(count, per[0]) as i:
                    for s in range(2):
                        yield i * 2 + (done + s), i * 2 + (n0 + done + s), s, (l, i, h0, l * HALVES + h0)
                done += 2 * count
            if done < FC:
                with loop((FC - done) // 2, per[1]) as i:
                    for s in range(2):
                        yield i * 2 + (done + s), i * 2 + (n0 + done + s), s, None

        def out_steps(sub, g, loop, per):
            k = sub["k_slots"]
            n0 = sub["slot"] + sub["in_slots"] + g * k
            s = 0
            if g == 0:
                if sub["ada_out"]:
                    l, h = sub["ada_out"]
                    for i in range(2):
                        for u in range(4):
                            yield i * 4 + u, n0 + i * 4 + u, i * 4 + u, (l, h + i, l * HALVES + h + i), u, None
                    s = 8
                else:
                    for s in range(2):
                        yield s, n0 + s, s, None, None, None
                    s = 2
            while g == 1 and s < min(norm_stages(sub, 0), k):
                yield s, n0 + s, s, None, None, s
                s += 1
            pairs = (k - 1 - s) // 2
            if pairs > 1:
                with loop(pairs, per) as i:
                    for u in range(2):
                        yield i * 2 + (s + u), i * 2 + (n0 + s + u), s + u, None, None, None
                s += 2 * pairs
            while s < k:
                yield s, n0 + s, s, None, None, None
                s += 1

        def psum_tile(i):
            return ps[:, 2 * i:2 * i + 2, :].rearrange("p b n -> p (b n)")

        def norm_work(sub, g, s):
            n = sub["groups"][g]
            a, b, t, c = s, s - 1, s - 2, s - 3
            lo = c if g == 0 else s - 4
            if sub["kind"] == "ffn" and g == 0 and not sub["final"]:
                t = t // 2 if t % 2 == 0 else -1
                c = lo = c // 2 if c % 2 == 0 else -1
            if sub["final"]:
                b = t = c = lo = -1
            return [i if 0 <= i < n else None for i in (a, b, t, c, lo)]

        def norm_stages(sub, g):
            if sub["kind"] == "ffn" and g == 0 and not sub["final"]:
                return 2 * sub["groups"][g] + 2
            return sub["groups"][g] + 3 + g

        def turn_bank(nxt, i):
            return 6 if i % 2 == 0 else 4 if nxt[1] == 1 else 2

        def plain_loop(eng):
            return lambda trips, per: eng.Fori(0, trips)

        def mixer_act(act, sub, split_w, first_out):
            m, n0 = sub["mix"], sub["slot"]
            outs = tiles_of(sub)
            n_out = sum(sub["groups"])
            ctx_out = n_out == NT

            def evac(ch):
                n = n0 + ch // 2 + (1 if ch >= 4 else 0)
                act.wait_ge(S["w_used"], 2 * n + ch % 2 + 1 + START)
                for g in range(2):
                    w = GW if ch < 4 else sub["groups"][g] * P
                    dst = xmT[:, ch, g * GW:g * GW + w] if ch < 4 else mixT[:, g, ch - 4, 0:w]
                    b = ch % 3
                    src = ps[:, b + 3 * g, 0:w] if ch < 4 or ctx_out else ps[:, b, g * GW:g * GW + w]
                    ins = nc.scalar.activation(dst, src, ACT.Sigmoid if ch >= 8 else ACT.Copy)
                ins.then_inc(S["win_evac"], 1)

            def conv_silu(h):
                act.wait_ge(S["conv"], 4 * m + h + 1)
                nc.scalar.activation(convT[:, h, :], convT[:, h, :], ACT.Silu).then_inc(S["conv_silu"], 1)

            def split(s):
                split_w(n0 + s, (n0 + s) % 2, KC * 16 if s == 2 else SLOT)

            evac(0)
            evac(1)
            split(2)
            evac(2)
            evac(3)
            split(3)
            conv_silu(0)
            split(4)
            evac(4)
            act.wait_ge(S["g_abs"], m + 1)
            nc.scalar.activation(g_abs, g_abs, ACT.Exp, scale=-1.0).then_inc(S["g_exp"], 1)
            act.wait_ge(S["g_exp"], m + 1)
            nc.scalar.activation(g_abs, g_abs, ACT.Ln, bias=ones[:, 0:1]).then_inc(S["g_ln"], 1)
            conv_silu(1)
            evac(5)
            split(5)
            evac(6)
            conv_silu(2)
            evac(7)
            split(6)
            act.wait_ge(S["g_m"], m + 1)
            nc.scalar.activation(dec0, dec0, ACT.Exp).then_inc(S["g_dec"], 1)
            evac(8)
            conv_silu(3)
            evac(9)
            split(7)
            act.wait_ge(S["g_arg"], m + 1)
            em_v = em_arg.rearrange("p (d k h) -> p d k h", d=2, k=8)
            t_v = ps[:, 7, 0:192].rearrange("p (a d k h) -> p a d k h", a=3, d=2, k=8)
            for dst, src in ((em, em_v), (wi, t_v[:, 1]), (wst, t_v[:, 2])):
                nc.scalar.activation(dst[:, 0, 0:4, :], src[:, 0, 2:6, :], ACT.Exp)
                nc.scalar.activation(dst[:, 0, 4:6, :], src[:, 0, 0:2, :], ACT.Exp)
                ins = nc.scalar.activation(dst[:, 1, 0:6, :], src[:, 1, 5::-1, :], ACT.Exp)
            ins.then_inc(S["g_w"], 1)
            evac(10)
            evac(11)
            for dst, src in ((dft_l, dft_l_in), (dft_c, dft_c_in)):
                act.dma_start(dst, src).then_inc(S["dft_in"], 16)

            def take(dst, src, scale, signal):
                nc.scalar.activation(dst, src, ACT.Copy, scale=scale).then_inc(S[signal], 1)

            def project(h, a):
                dst, b0 = ((qT, 0), (kT, 2), (ktok, 4), (vtok, 0))[a]
                act.wait_ge(S["qkv_mm"], 4 * (4 * m + h) + a + 1)
                for g in range(2):
                    w = (len(outs[g]) if a == 0 else GT) * P
                    src = ps[:, b0 + g, 0:w]
                    if a < 2:
                        to = dst[:, g * GW:g * GW + w]
                    else:
                        to = dst[:, g * GT:(g + 1) * GT, 0:HD]
                        src = src.rearrange("p (t n) -> p t n", n=P)
                    ins = nc.scalar.activation(to, src, ACT.Copy, scale=float(HD) ** -0.5 if a in (1, 2) else 1.0)
                ins.then_inc(S["qkv_sb"], 1)

            def weights(h, d):
                md = 2 * (4 * m + h) + d
                act.wait_ge(S["mb_mm"], md + 1)
                if md:
                    act.wait_ge(S["io_mm"], md)
                for t in outs[0] + outs[1]:
                    col = scan_col(d, scan_k(d, t), h)
                    ins = nc.scalar.activation(wt[:, t, :], ps[:, 2 + t // GT, (t % GT) * P:(t % GT + 1) * P], ACT.Exp,
                                               bias=r_tok[:, col:col + 1])
                ins.then_inc(S["wt_sb"], 1)

            for h in range(HEADS):
                k = 4 * m + h
                for a in range(4):
                    project(h, a)
                weights(h, 0)
                act.wait_ge(S["ab_mm"], k + 1)
                take(ab, ps[:, 6, 0:256], 1.0, "ab_sb")
                act.wait_ge(S["xab_mm"], (2 * k if ctx_out else k + HEADS) + 1)
                for b in range(2):
                    ins = nc.scalar.activation(xab[:, 2 * b:2 * b + 2, :].rearrange("p t n -> p (t n)"), ps[:, 6 + b, :], ACT.Copy)
                ins.then_inc(S["xab_sb"], 1)
                if ctx_out:
                    act.wait_ge(S["xab_mm"], 2 * k + 2)
                    take(xab[:, 4:6, :].rearrange("p t n -> p (t n)"), ps[:, 6, :], 1.0, "xab_sb")
                weights(h, 1)
                act.wait_ge(S["f_mm"], k + 1)
                nc.scalar.activation(mixT[:, 0, h, :], ps[:, 7, 0:GW], ACT.Copy)
                ins = nc.scalar.activation(mixT[:, 1, h, 0:P], ps[:, 7, GW:512], ACT.Copy)
                if ctx_out:
                    ins = nc.scalar.activation(mixT[:, 1, h, P:GW], ps[:, 6, 0:CTX], ACT.Copy)
                ins.then_inc(S["f_sb"], 1)
                if h == HEADS - 1:
                    first_out(sub)
                act.wait_ge(S["hvar"], k + 1)
                nc.scalar.activation(den[:, 0, 0:n_out], mv[:, 0:n_out, 1], ACT.Sqrt, bias=eps[:, 0:1]).then_inc(S["hstd"], 1)

        def mixer_dve(dve, own, sub, split_w, first_out):
            m, n0, l = sub["mix"], sub["slot"], sub["l"]
            outs = tiles_of(sub)
            n_out = sum(sub["groups"])
            link = own.link
            g5 = g16.rearrange("p (t d b h) -> p t d b h", t=NT, d=2, b=2)
            v8 = lambda a: a.rearrange("p (d c) -> p d c", d=2)

            def split(s):
                split_w(n0 + s, (n0 + s) % 2, KC * 16 if s == 2 else SLOT)

            def conv(h):
                dve.wait_ge(S["win_evac"], 12 * m + h + 1)
                src = xmT[:, h, 0:SEQ].rearrange("p (r c) -> p r c", c=64)
                dst = convT[:, h, 0:SEQ].rearrange("p (r c) -> p r c", c=64)
                csrc, cdst = xmT[:, h, SEQ:TOK], convT[:, h, SEQ:TOK]
                w = convw[:, l, h, :]
                link(nc.vector.tensor_scalar(convT[:, h, :], xmT[:, h, :], w[:, 4:5], convb[:, l, h:h + 1], ALU.mult, ALU.add))

                def tap(o, s, k):
                    return nc.vector.scalar_tensor_tensor(out=o, in0=s, scalar=w[:, k:k + 1], in1=o, op0=ALU.mult, op1=ALU.add)

                R, C = SEQ // 64, 64
                for dy in (-1, 0, 1):
                    for dx in (-1, 0, 1):
                        if dy == 0 and dx == 0:
                            continue
                        r0, r1 = max(0, -dy), R - max(0, dy)
                        c0, c1 = max(0, -dx), C - max(0, dx)
                        link(tap(dst[:, r0:r1, c0:c1], src[:, r0 + dy:r1 + dy, c0 + dx:c1 + dx], (dy + 1) * 3 + dx + 1))
                link(tap(cdst[:, 1:CTX], csrc[:, 0:CTX - 1], 3))
                tap(cdst[:, 0:CTX - 1], csrc[:, 1:CTX], 5).then_inc(S["conv"], 1)

            def gates_copy():
                dve.wait_ge(S["w_used"], 2 * (n0 + 3) + START)
                nc.vector.tensor_copy(acc[0:16, :, 0:GW], ps[0:16, 6:8, 0:GW]).then_inc(S["g_cp"], 1)

            def gates_abs():
                dve.wait_ge(S["g_tok"], m + 1)
                gv = g16.rearrange("p (a b h) -> p a b h", b=2, h=4)
                link(nc.vector.tensor_tensor(g16.rearrange("p (t j) -> p t j", t=NT), ps[:, 7, 0:96].rearrange("p (t j) -> p t j", t=NT),
                                             gate_b[:, l, :].unsqueeze(1).to_broadcast([P, NT, 16]), ALU.add))
                nc.vector.scalar_tensor_tensor(out=g_abs, in0=gv[:, :, 1, :], scalar=-1.0, in1=gv[:, :, 1, :], op0=ALU.mult,
                                               op1=ALU.max).then_inc(S["g_abs"], 1)
                nc.vector.memset(lfs, 0.0)
                link(nc.vector.memset(igs, 0.0))

            def gates_log():
                a4 = g_abs.rearrange("p (t d) h -> p t d h", d=2)
                dve.wait_ge(S["g_ln"], m + 1)
                for d, dst, src in ((0, slice(2, 6), slice(0, 4)), (0, slice(0, 2), slice(4, 6)), (1, slice(0, 6), slice(5, None, -1))):
                    nc.vector.tensor_copy(igs[:, d, dst, :], g5[:, src, d, 0, :])
                    ins = nc.vector.scalar_tensor_tensor(out=lfs[:, d, dst, :], in0=g5[:, src, d, 1, :], scalar=0.0,
                                                         in1=a4[:, src, d, :], op0=ALU.min, op1=ALU.subtract)
                ins.then_inc(S["g_lf"], 1)

            def gates_r():
                dve.wait_ge(S["g_b"], m + 1)
                nc.vector.tensor_copy(b_tok, ps[:, 7, 96:160])
                nc.vector.tensor_copy(btot0, ps[0:1, 7, 160:224])
                nc.vector.tensor_tensor(r_tok, igs.rearrange("p d k h -> p (d k h)"), ps[:, 7, 96:160], ALU.subtract).then_inc(S["g_r"], 1)

            def gates_max():
                dve.wait_ge(S["g_rT"], m + 1)
                link(nc.vector.tensor_copy(r_row[0:64], ps[0:64, 7, 224:352]))
                nc.vector.tensor_reduce(cols[0:64, 2:3], r_row[0:64], AX_X, ALU.max).then_inc(S["g_rmx"], 1)
                nc.vector.tensor_tensor_scan(cm_row[0:32], r_row[0:32], r_row[0:32], NEG, ALU.max, ALU.max)
                back = r_row[32:64, P - 1::-1]
                link(nc.vector.tensor_tensor_scan(cm_row[32:64, P - 1::-1], back, back, NEG, ALU.max, ALU.max))

            def gates_m():
                dve.wait_ge(S["g_rr"], m + 1)
                link(nc.vector.tensor_copy(rmax0, ps[0:1, 7, 352:416]))
                link(nc.vector.memset(mprev0, 0.0))
                for d in range(2):
                    for h in range(HEADS):
                        sl = slice(d * 32 + h, d * 32 + h + 21, 4)
                        ins = nc.vector.tensor_tensor_scan(m0[:, sl], rmax0[:, sl], btot0[:, sl], 0.0, ALU.max, ALU.add)
                link(ins)
                link(nc.vector.tensor_copy(v8(mprev0)[:, :, 4:24], v8(m0)[:, :, 0:20]))
                link(nc.vector.tensor_tensor(mlast0, mprev0, rmax0, ALU.max))
                nc.vector.tensor_tensor(dec0, mprev0, mlast0, ALU.subtract).then_inc(S["g_m"], 1)

            def gates_rows():
                dve.wait_ge(S["g_bc"], m + 1)
                nc.vector.tensor_copy(dec, ps[:, 7, 420:484])
                link(nc.vector.tensor_copy(cols[0:64, 0:2], ps[0:64, 7, 416:418]))
                link(nc.vector.tensor_scalar(m_row[0:64], cm_row[0:64], cols[0:64, 0:1], None, ALU.max))
                nc.vector.tensor_scalar(d_row[0:64], m_row[0:64], -1.0, cols[0:64, 0:1], ALU.mult, ALU.add)
                nc.vector.tensor_scalar(nm_row[0:64], m_row[0:64], -1.0, None, ALU.mult)
                nc.vector.tensor_scalar(rw_row[0:64], r_row[0:64], cols[0:64, 1:2], None, ALU.subtract).then_inc(S["g_rows"], 1)

            def gates_arg():
                dve.wait_ge(S["g_T"], m + 1)
                nc.vector.scalar_tensor_tensor(out=em_arg, in0=ps[:, 7, 0:64], scalar=-1.0, in1=b_tok, op0=ALU.mult,
                                               op1=ALU.subtract).then_inc(S["g_arg"], 1)

            split(2)
            conv(0)
            split(3)
            gates_copy()
            conv(1)
            gates_abs()
            split(4)
            gates_log()
            gates_r()
            conv(2)
            split(5)
            gates_max()
            gates_m()
            split(6)
            conv(3)
            gates_rows()
            split(7)
            gates_arg()

            def values(h, d):
                md = 2 * (4 * m + h) + d
                if d == 0:
                    dve.wait_ge(S["qkv_sb"], 4 * (4 * m + h) + 4)
                nc.vector.tensor_tensor(wv, vtok, wst[:, d, :, h].unsqueeze(2).to_broadcast([P, NT, HV]), ALU.mult).then_inc(S["wv_sb"], 1)
                if md:
                    dve.wait_ge(S["io_mm"], md)
                link(nc.vector.memset(cst[:, 0, :], 0.0))

            def states(h, d):
                md = 2 * (4 * m + h) + d
                dve.wait_ge(S["cloc_mm"], md + 1)
                for k in range(NT - 1):
                    col = scan_col(d, k, h)
                    ins = nc.vector.scalar_tensor_tensor(out=cst[:, k + 1, :], in0=cst[:, k, :], scalar=dec[:, col:col + 1],
                                                         in1=ps[:, 4 + k // 3, (k % 3) * HV:(k % 3 + 1) * HV],
                                                         op0=ALU.mult, op1=ALU.add)
                    if k < NT - 2:
                        link(ins)
                ins.then_inc(S["cst_sb"], 1)

            def scores(h, d):
                md = 2 * (4 * m + h) + d
                dve.wait_ge(S["wt_sb"], md + 1)
                dve.wait_ge(S["st_mm"], 4 * m + h + 1)
                for g in range(2):
                    nt = len(outs[g])
                    wg = wt[:, g * GT:g * GT + nt, :].rearrange("p t n -> p (t n)")
                    ins = nc.vector.tensor_tensor(wg, wg, ps[:, g, 0:nt * P], ALU.mult)
                ins.then_inc(S["p_sb"], 1)

            def combine(h, d):
                md = 2 * (4 * m + h) + d
                dve.wait_ge(S["io_mm"], md + 1)
                for g in range(2):
                    nt = len(outs[g])
                    sl = slice(g * GT, g * GT + nt)
                    ng = num[:, sl, :]
                    link(nc.vector.tensor_tensor(ng, ps[:, 2 + g, 0:nt * HV].rearrange("p (t n) -> p t n", n=HV),
                                                 wi[:, d, sl, h].unsqueeze(2).to_broadcast([P, nt, HV]), ALU.mult))
                    ins = nc.vector.tensor_tensor(ng, ng, ps[:, 4 + g, 0:nt * HV].rearrange("p (t n) -> p t n", n=HV), ALU.add)
                    if g == 0:
                        own.mark(ins)
                ins.then_inc(S["comb"], 1)
                dve.wait_ge(S["comb"], md + 1)
                dn = num[:, 0:n_out, HD]
                link(nc.vector.scalar_tensor_tensor(out=den[:, 1, 0:n_out], in0=dn, scalar=-1.0, in1=dn, op0=ALU.mult, op1=ALU.max))
                link(nc.vector.tensor_tensor(den[:, 2, 0:n_out], den[:, 1, 0:n_out], em[:, d, 0:n_out, h], ALU.max))
                link(nc.vector.reciprocal(den[:, 3, 0:n_out], den[:, 2, 0:n_out]))
                rd = den[:, 3, 0:n_out].unsqueeze(2).to_broadcast([P, n_out, HD])
                hs = hsum(h)[:, 0:n_out, :]
                if d == 0:
                    link(nc.vector.tensor_tensor(hs, num[:, 0:n_out, 0:HD], rd, ALU.mult))
                else:
                    link(nc.vector.tensor_tensor(num[:, 0:n_out, 0:HD], num[:, 0:n_out, 0:HD], rd, ALU.mult))
                    link(nc.vector.tensor_tensor(hs, hs, num[:, 0:n_out, 0:HD], ALU.add))

            dve.wait_ge(S["w_used"], 2 * (n0 + 7) + START)
            link(nc.vector.memset(vtok[:, :, HD:HV], 1.0))
            dve.wait_ge(S["g_w"], m + 1)
            for h in range(HEADS):
                mh = 4 * m + h
                for d in range(2):
                    values(h, d)
                    states(h, d)
                    scores(h, d)
                    if (h, d) == (HEADS - 1, 1):
                        first_out(sub)
                    combine(h, d)
                for t in range(n_out):
                    ins = nc.vector.bn_stats(bn[:, t, :], hsum(h)[:, t, :])
                link(ins)
                for t in range(n_out):
                    ins = nc.vector.bn_aggr(mv[:, t, :], bn[:, t, :])
                ins.then_inc(S["hvar"], 1)
                dve.wait_ge(S["hstd"], mh + 1)
                link(nc.vector.reciprocal(den[:, 1, 0:n_out], den[:, 0, 0:n_out]))
                for t in range(n_out):
                    ins = nc.vector.tensor_scalar(hsum(h)[:, t, :], hsum(h)[:, t, :], mv[:, t, 0:1], den[:, 1, t:t + 1], ALU.subtract, ALU.mult)
                ins.then_inc(S["hn"], 1)
                dve.wait_ge(S["hnT"], mh + 1)
                for g in range(2):
                    w = len(outs[g]) * P
                    mg = mixT[:, g, 4 + h, 0:w]
                    ins = nc.vector.scalar_tensor_tensor(out=mg, in0=ps[:, 6 + g, 0:w], scalar=hn_w[:, l, h:h + 1], in1=mg,
                                                         op0=ALU.mult, op1=ALU.mult)
                ins.then_inc(S["mix_done"], 1)

        def head_out(pe, sub, h):
            mh = 4 * sub["mix"] + h
            n_out = sum(sub["groups"])
            pe.wait_ge(S["hn"], mh + 1)
            pe.wait_ge(S["f_sb"], mh + 1)
            for t in range(n_out):
                ins = nc.tensor.transpose(ps[:, 6 + t // GT, (t % GT) * P:(t % GT + 1) * P], hsum(h)[:, t, :], ident[:])
            ins.then_inc(S["hnT"], 1)

        def mixer_pe(pe, sub, turn_late, banks_free):
            mm = nc.tensor.matmul
            m, n0 = sub["mix"], sub["slot"]
            outs = tiles_of(sub)
            n_out = sum(sub["groups"])
            ctx_out = n_out == NT

            def chunk(ch, groups):
                n = n0 + ch // 2 + (1 if ch >= 4 else 0)
                pe.wait_ge(S["w_lo"], n + 1 + START)
                if ch >= 3:
                    pe.wait_ge(S["win_evac"], 12 * m + ch - 2)
                hi = w_hi[n % 2][:].rearrange("p (k n) -> p k n", k=KC)
                lo = w_lo[n % 2][:].rearrange("p (k n) -> p k n", k=KC)
                c = ch % 2
                for k in range(KC):
                    for i, (w, xx) in enumerate(((hi, xn_hi), (hi, xn_lo), (lo, xn_hi))):
                        for g in groups:
                            wd = GW if ch < 4 or ctx_out else SEQ
                            ins = mm(ps[:, ch % 3 + 3 * g, 0:wd], w[:, k, c * P:(c + 1) * P], xx[:, k, g * GW:g * GW + wd],
                                     start=(k == 0 and i == 0), stop=(k == KC - 1 and i == 2))
                if groups != [0] or ch >= 4:
                    ins.then_inc(S["w_used"], 1)

            pe.wait_ge(S["xn_done"], sub["xn"] - GT)
            for i in range(GT):
                banks_free(sub, 1 if i < 2 else 2)
                chunk(i, [0])
                if i:
                    turn_late(sub, i - 1)
            turn_late(sub, GT - 1)
            pe.wait_ge(S["xn_done"], sub["xn"])
            for ch in range(3):
                chunk(ch, [1])
            chunk(3, [0, 1])
            out_groups = [0, 1] if ctx_out else [0]
            n = n0 + 2
            pe.wait_ge(S["w_lo"], n + 1 + START)
            hi = w_hi[n % 2][:, 0:KC * 16].rearrange("p (k j) -> p k j", k=KC)
            lo = w_lo[n % 2][:, 0:KC * 16].rearrange("p (k j) -> p k j", k=KC)
            for k in range(KC):
                for i, (xx, w) in enumerate(((xn_hi, hi), (xn_lo, hi), (xn_hi, lo))):
                    for g in range(2):
                        ins = mm(ps[0:16, 6 + g, 0:GW], w[:, k, :], xx[:, k, g * GW:(g + 1) * GW],
                                 start=(k == 0 and i == 0), stop=(k == KC - 1 and i == 2))
            ins.then_inc(S["w_used"], 2)
            chunk(4, out_groups)
            pe.wait_ge(S["g_cp"], m + 1)
            for t in range(NT):
                ins = nc.tensor.transpose(ps[:, 7, t * 16:t * 16 + 16], acc[0:16, t // GT, (t % GT) * P:(t % GT + 1) * P], ident[0:16, 0:16])
            ins.then_inc(S["g_tok"], 1)
            chunk(5, out_groups)
            pe.wait_ge(S["mix_const"], 64 * (m + 1))
            pe.wait_ge(S["g_lf"], m + 1)
            for d in range(2):
                mm(ps[:, 7, 96 + 32 * d:128 + 32 * d], tri[:, d, :], lfs[:, d].rearrange("p k h -> p (k h)"), start=True, stop=True)
            mm(ps[0:1, 7, 160:224], ones[:, 0:1], lfs.rearrange("p d k h -> p (d k h)"), start=True, stop=True).then_inc(S["g_b"], 1)
            chunk(6, out_groups)
            pe.wait_ge(S["g_r"], m + 1)
            nc.tensor.transpose(ps[0:64, 7, 224:352], r_tok, ident[:]).then_inc(S["g_rT"], 1)
            chunk(7, out_groups)
            pe.wait_ge(S["g_rmx"], m + 1)
            mm(ps[0:1, 7, 352:416], cols[0:64, 2:3], ident[0:64, 0:64], start=True, stop=True).then_inc(S["g_rr"], 1)
            chunk(8, out_groups)
            pe.wait_ge(S["g_dec"], m + 1)
            mm(ps[0:64, 7, 416:417], mprev0, ones[0:1, 0:1], start=True, stop=True)
            mm(ps[0:64, 7, 417:418], mlast0, ones[0:1, 0:1], start=True, stop=True)
            mm(ps[:, 7, 420:484], ones[0:1, 0:1].to_broadcast([1, P]), dec0, start=True, stop=True).then_inc(S["g_bc"], 1)
            chunk(9, out_groups)
            pe.wait_ge(S["g_rows"], m + 1)
            for i, row in enumerate((m_row, d_row, rw_row)):
                ins = nc.tensor.transpose(ps[:, 7, 64 * i:64 * i + 64], row[0:64], ident[0:64, 0:64])
            ins.then_inc(S["g_T"], 1)
            chunk(10, out_groups)
            chunk(11, out_groups)

            def project(h, a):
                for g in range(2):
                    if a < 2:
                        w = (len(outs[g]) if a == 0 else GT) * P
                        ins = mm(ps[:, 2 * a + g, 0:w], qkv_w[:, a, h, :], convT[:, h, g * GW:g * GW + w], start=True, stop=True)
                    else:
                        for t in range(g * GT, (g + 1) * GT):
                            src = (convT if a == 2 else xmT)[:, h, t * P:(t + 1) * P]
                            ins = mm(ps[:, (4 if a == 2 else 0) + g, (t % GT) * P:(t % GT + 1) * P], src, qkv_w[:, a - 1, h, :],
                                     start=True, stop=True)
                ins.then_inc(S["qkv_mm"], 1)

            def maxima(h, d):
                for g in range(2):
                    nt = len(outs[g])
                    mm(ps[:, 2 + g, 0:nt * P], ident_bf[:], mask[:, d, :].unsqueeze(1).to_broadcast([P, nt, P]), start=True, stop=False)
                    for i, t in enumerate(outs[g]):
                        col = scan_col(d, scan_k(d, t), h)
                        ins = mm(ps[:, 2 + g, i * P:(i + 1) * P], ident[0:64, col:col + 1].to_broadcast([64, P]), nm_row[0:64],
                                 start=False, stop=(i == nt - 1))
                ins.then_inc(S["mb_mm"], 1)

            def added(h, d):
                pe.wait_ge(S["wv_sb"], 2 * (4 * m + h) + d + 1)
                for k in range(NT - 1):
                    t = scan_t(d, k)
                    ins = mm(ps[:, 4 + k // 3, (k % 3) * HV:(k % 3 + 1) * HV], ktok[:, t, :], wv[:, t, :], start=True, stop=True)
                ins.then_inc(S["cloc_mm"], 1)

            def outputs(h, d):
                md = 2 * (4 * m + h) + d
                pe.wait_ge(S["cst_sb"], md + 1)
                pe.wait_ge(S["p_sb"], md + 1)
                for t in outs[0] + outs[1]:
                    g, i = t // GT, t % GT
                    mm(ps[:, 4 + g, i * HV:(i + 1) * HV], wt[:, t, :], vtok[:, t, :], start=True, stop=True)
                    ins = mm(ps[:, 2 + g, i * HV:(i + 1) * HV], qT[:, t * P:(t + 1) * P], cst[:, scan_k(d, t), :], start=True, stop=True)
                ins.then_inc(S["io_mm"], 1)

            def dft_part(tiles, first, last):
                for t in tiles:
                    for c in range(2):
                        ins = mm(ps[:, 7, :], xab[:, t, c * P:(c + 1) * P], dft_l[:, t, c, :], start=first and t == tiles[0] and c == 0,
                                 stop=last and t == tiles[-1] and c == 1)
                return ins

            for h in range(HEADS):
                k = 4 * m + h
                if h == 0:
                    pe.wait_ge(S["g_w"], m + 1)
                    pe.wait_ge(S["win_evac"], 12 * m + 12)
                else:
                    pe.wait_ge(S["comb"], 2 * k)
                pe.wait_ge(S["conv_silu"], k + 1)
                for a in range(3):
                    project(h, a)
                if h:
                    head_out(pe, sub, h - 1)
                pe.wait_ge(S["qkv_sb"], 4 * k + 1)
                project(h, 3)
                pe.wait_ge(S["qkv_sb"], 4 * k + 2)
                maxima(h, 0)
                if h:
                    pe.wait_ge(S["mix_done"], k)
                mm(ps[:, 6, 0:P], dft_g[:, 0:P], fmix_w[:, h, :], start=True, stop=True)
                mm(ps[:, 6, P:2 * P], dft_g[:, P:2 * P], fmix_w[:, h, :], start=True, stop=True).then_inc(S["ab_mm"], 1)
                pe.wait_ge(S["qkv_sb"], 4 * k + 4)
                for t in outs[0] + outs[1]:
                    sl = slice(t * P, (t + 1) * P)
                    ins = mm(ps[:, t // GT, (t % GT) * P:(t % GT + 1) * P], kT[:, sl], qT[:, sl], start=True, stop=True)
                ins.then_inc(S["st_mm"], 1)
                added(h, 0)
                pe.wait_ge(S["ab_sb"], k + 1)
                for t in range(n_out):
                    if t == 4:
                        pe.wait_ge(S["xab_sb"], 2 * k + 1)
                    ins = mm(ps[:, 6 + t // 2 % 2, (t % 2) * 256:(t % 2) * 256 + 256],
                             mixT[:, t // GT, h, (t % GT) * P:(t % GT + 1) * P], ab, start=True, stop=True)
                    if t in (3, 5):
                        ins.then_inc(S["xab_mm"], 1)
                xabs = 2 * k + 2 if ctx_out else k + HEADS + 1
                pe.wait_ge(S["xab_sb"], xabs)
                if h == 0:
                    pe.wait_ge(S["dft_in"], 32 * (m + 1))
                dft_part([0, 1], True, False)
                outputs(h, 0)
                pe.wait_ge(S["comb"], 2 * k + 1)
                maxima(h, 1)
                added(h, 1)
                ins = dft_part([2, 3], False, True)
                if ctx_out:
                    for t in range(2):
                        for c in range(2):
                            ins = mm(ps[:, 6, 0:CTX], xab[:, NTL + t, c * P:(c + 1) * P], dft_c[:, t, c, :],
                                     start=(t == 0 and c == 0), stop=(t == 1 and c == 1))
                ins.then_inc(S["f_mm"], 1)
                outputs(h, 1)
            pe.wait_ge(S["comb"], 2 * HEADS * (m + 1))

        @block.sync
        def _(sp):
            loop = plain_loop(sp)

            def load(n, src, width=SLOT):
                if not isinstance(n, int) or n > 0:
                    sp.wait_ge(S["w_lo"], n + START)
                sp.dma_start(raw[:, 0:width], src).then_inc(S["w_raw"], 16)

            def unit(count, l, col, u):
                if not isinstance(count, int) or count >= 2:
                    sp.wait_ge(S["ada_used"], count - 1 + START)
                src = w_ada[l].rearrange("(u c p) n -> u p c n", c=2, p=P)[u, :, :, bass.ds(col, HB)]
                sp.dma_start(raw_ada[u % 2][:], src).then_inc(S[f"ada_raw{u % 2}"], 16)

            for dst, src in ((cvec[:], cvec_in), (b_col[:], b_col_in), (nw_col[:], nw_col_in), (convw[:], convw_in),
                             (convb[:], convb_in), (hn_w[:], hn_w_in), (tri, tri_in), (gate_b[:], gate_b_in)):
                sp.dma_start(dst, src).then_inc(S["consts"], 16)
            for i in range(4):
                if i == 3:
                    load(0, w_ff_in[0, 0, 0])
                src = w_ada[0].rearrange("(k p) n -> p k n", p=P)[:, :, i * HB:(i + 1) * HB]
                sp.dma_start(ada0(i), src).then_inc(S["ada_first"][i], 16)

            for sub in SUBS:
                l, j, n0 = sub["l"], sub["j"], sub["slot"]
                if sub["kind"] == "ffn":
                    for f, n, s, half in in_steps(sub, loop, (0, 0)):
                        if not (isinstance(n, int) and n == 0):
                            load(n, w_ff_in[l, j // 2, f])
                        if half is not None:
                            hl, i, h0, g0 = half
                            for u in (2 * s, 2 * s + 1):
                                unit(i * 4 + (4 * g0 - 16 + u), hl, i * HB + h0 * HB, u)
                    w = w_ff_out[l, j // 2].rearrange("(s c p) n -> s p c n", c=2, p=P)
                else:
                    src = w_in[l].rearrange("(k p) n -> p k n", p=P)
                    for s in range(7):
                        if s == 2:
                            load(n0 + 2, w_gates[l], KC * 16)
                        else:
                            c0 = (D // 2, 3 * D // 4, 0, 0, D // 4, D, 5 * D // 4)[s]
                            sp.wait_ge(S["w_lo"], n0 + s + START)
                            sp.dma_start(raw[:].rearrange("p (k n) -> p k n", k=KC), src[:, :, c0:c0 + 256]).then_inc(S["w_raw"], 16)
                    w = w_out[l].rearrange("(s c p) n -> s p c n", c=2, p=P)
                for g in range(len(sub["groups"])):
                    for s, n, par, half, u, st in out_steps(sub, g, loop, 0):
                        sp.wait_ge(S["w_lo"], n + START)
                        sp.dma_start(raw[:].rearrange("p (c n) -> p c n", c=2), w[s]).then_inc(S["w_raw"], 16)
                        if half is not None:
                            hl, h, g0 = half
                            unit(4 * g0 - 16 + u, hl, h * HB, u)
            for p_ in range(NTL):
                sp.wait_ge(S["x_new"], SUBS[-1]["y"] + p_ + 1)
                sp.dma_start(out[p_], x[:, p_, :]).then_inc(S["out_dma"], 16)
            sp.wait_ge(S["out_dma"], 16 * NTL)

        @block.gpsimd
        def _(pool):
            nc.gpsimd.memset(ones[:], 1.0)
            nc.gpsimd.memset(eps[:], EPS)
            nc.gpsimd.memset(ident[:], 0.0).then_inc(S["pool_consts"], 1)
            pool.wait_ge(S["pool_consts"], 1)
            nc.gpsimd.affine_select(out=ident[:], in_=ident[:], compare_op=ALU.not_equal, fill=1.0, base=0,
                                    pattern=[[-1, P]], channel_multiplier=1).then_inc(S["pool_consts"], 1)
            pool.wait_ge(S["x_in"], 16 * NT)
            for sub in SUBS:
                for tiles in tiles_of(sub):
                    for i, t in enumerate(tiles):
                        pool.wait_ge(S["gated"], sub["y"] + t + 1)
                        nc.gpsimd.tensor_tensor(x[:, t, :], x[:, t, :], ys(i), ALU.add).then_inc(S["x_new"], 1)

        @block.scalar
        def _(act):
            loop = plain_loop(act)

            def split_w(n, par, width=SLOT):
                if isinstance(n, int) and n >= N_SLOTS:
                    return
                act.wait_ge(S["w_raw"], n * 16 + 16)
                if not isinstance(n, int) or n >= 2:
                    act.wait_ge(S["w_used"], n * 2 - 2 + START)
                nc.scalar.activation(w_hi[par][:, 0:width], raw[:, 0:width], ACT.Copy).then_inc(S["w_hi"], 1)

            def hj(sub, g, c, hs, b):
                if g == 0:
                    if sub["kind"] == "ffn":
                        act.wait_ge(S["h_done"], c + (sub["proj"] + 1))
                    elif c < HEADS:
                        act.wait_ge(S["f_sb"], HEADS * sub["mix"] + c + 1)
                    else:
                        act.wait_ge(S["mix_done"], HEADS * sub["mix"] + c - HEADS + 1)
                act.wait_ge(S["w_used"], hs - 1 + START)
                w = sub["groups"][g] * P
                nc.scalar.activation(split_h(sub, b)[0][:, 0:w], hidden(sub, g, c), ACT.Copy).then_inc(S["hj_hi"], 1)

            def stage(sub, g, s):
                tiles, y0, x0 = tiles_of(sub)[g], sub["y"] + g * GT, sub["xn"] + g * GT
                a, b, _, c, _ = norm_work(sub, g, s)
                if b is not None:
                    prenorm_scale(x0 + b, tiles[b], b)
                if c is not None:
                    prenorm_split(x0 + c, tiles[c], turn_bank(sub["next"], c) if g else 6)
                if a is not None:
                    if not sub["final"]:
                        act.wait_ge(S["x_new"], y0 + s + 1)
                        prenorm_stat(x0 + s, tiles[s], s)

            def prenorm_stat(xi, t, i):
                nc.scalar.activation(dummy, x[:, t, :], ACT.Square, scale=1.0 / 32,
                                     accum_out=stat[:, i, 3:4]).then_inc(S["act_ms2"], 1)
                act.wait_ge(S["act_ms2"], xi + 1)
                nc.scalar.activation(stat[:, i, 4:5], stat[:, i, 3:4], ACT.Sqrt, bias=eps[:, 0:1]).then_inc(S["std2"], 1)

            def prenorm_scale(xi, t, i):
                act.wait_ge(S["rs2"], xi + 1)
                nc.scalar.activation(ys(i), x[:, t, :], ACT.Copy, scale=stat[:, i, 5:6]).then_inc(S["xs"], 1)

            def prenorm_split(xi, t, b):
                act.wait_ge(S["modded"], xi + 1)
                nc.scalar.activation(xn_hi[:, :, t * P:(t + 1) * P], ps[:, b:b + 2, :].rearrange("p b (c w) -> p (b c) w", w=P),
                                     ACT.Copy).then_inc(S["xn_hi"], 1)

            def mean_square(yi, i, src):
                nc.scalar.activation(dummy, src, ACT.Square, scale=1.0 / 32, accum_out=stat[:, i, 0:1]).then_inc(S["y_sq"], 1)
                act.wait_ge(S["y_sq"], yi + 1)
                nc.scalar.activation(stat[:, i, 1:2], stat[:, i, 0:1], ACT.Sqrt, bias=eps[:, 0:1]).then_inc(S["std1"], 1)

            def evacuate(sub, g):
                if sub["final"]:
                    act.wait_ge(S["w_used"], 2 * N_SLOTS + START)
                    for i in range(NTL):
                        mean_square(sub["y"] + i, i, psum_tile(i))
                    return
                for i in range(sub["groups"][g]):
                    act.wait_ge(S["y_copied"], sub["y"] + g * GT + i + 1)
                    mean_square(sub["y"] + g * GT + i, i, ys(i))

            def load_constants(sub):
                l, j = sub["l"], sub["j"]
                if sub["y"]:
                    act.wait_ge(S["x_new"], sub["y"])
                nw = norm_w[l, 2 * j + 1:2 * j + 2, :]
                for s in range(2):
                    act.dma_start(gate_row[:, s, :], nw.to_broadcast([P, D])).then_inc(S["gate_in"], 16)
                if sub["kind"] == "mix":
                    act.wait_ge(S["xn_done"], sub["xn"])
                    act.dma_start(qkv_w, w_qkv[l].rearrange("a h d e -> d a h e")).then_inc(S["mix_const"], 16)
                    for dst, src in ((fmix_w, fmix_in[l]), (dft_g, dft_g_in), (tri, tri_in)):
                        act.dma_start(dst, src).then_inc(S["mix_const"], 16)

            def first_out(sub):
                nb = sub["slot"] + sub["in_slots"]
                for c in range(2):
                    hj(sub, 0, c, 2 * nb + c, c)

            for t in range(NT):
                act.dma_start(x[:, t, :], x_in[t]).then_inc(S["x_in"], 16)
            act.wait_ge(S["consts"], 16 * 8)
            nc.scalar.activation(silu_c[:], cvec[:], ACT.Silu).then_inc(S["silu_c"], 1)
            act.wait_ge(S["x_in"], 16 * NT)
            act.wait_ge(S["pool_consts"], 2)
            for t in range(NT):
                prenorm_stat(t, t, t)
            for t in range(NT):
                prenorm_scale(t, t, t)
            split_w(0, 0)
            for t in range(NT):
                if t == GT:
                    split_w(1, 1)
                prenorm_split(t, t, turn_bank((0, 0), t % GT))

            for sub in SUBS:
                l, j, n0 = sub["l"], sub["j"], sub["slot"]
                par0 = n0 % 2
                load_constants(sub)
                if sub["kind"] == "ffn":
                    for f, n, s, half in in_steps(sub, loop, (0, 0)):
                        if not (isinstance(f, int) and f == 0):
                            split_w(n + 1, (par0 + s + 1) % 2)
                        act.wait_ge(S["w_used"], n * 2 + 2 + START)
                        if sub["final"]:
                            nc.scalar.activation(hidden(sub, 0, f), ps[:, s * 4, :], ACT.Silu).then_inc(S["silu"], 1)
                            continue
                        for g in range(2):
                            w = sub["in_groups"][g] * P
                            dst = hid[:, g, bass.ds(f, 1), 0:w].rearrange("p a w -> p (a w)")
                            ins = nc.scalar.activation(dst, ps[:, s * 4 + 2 * g, 0:w], ACT.Silu)
                        ins.then_inc(S["silu"], 1)
                else:
                    mixer_act(act, sub, split_w, first_out)
                for g in range(len(sub["groups"])):
                    nb = n0 + sub["in_slots"] + g * sub["k_slots"]
                    pb = nb % 2
                    early = sub["kind"] == "mix" and g == 0
                    if not early:
                        hj(sub, g, 0, 2 * nb, 0)
                    if g == 1:
                        evacuate(sub, 0)
                    done = 0
                    for s, n, par, half, u, st in out_steps(sub, g, loop, 0):
                        if not (early and s == 0):
                            hj(sub, g, s * 2 + 1, n * 2 + 1, 1)
                        split_w(n + 1, (pb + par + 1) % 2)
                        if not (isinstance(s, int) and s == sub["k_slots"] - 1):
                            hj(sub, g, s * 2 + 2, n * 2 + 2, 0)
                        if st is not None:
                            stage(sub, 0, st)
                            done = st + 1
                if sub["final"]:
                    evacuate(sub, 0)
                for s in range(done, norm_stages(sub, 0)):
                    stage(sub, 0, s)
                if sub["final"]:
                    break
                evacuate(sub, 1)
                split_w(n0 + sub["in_slots"] + 2 * sub["k_slots"] + 1, (par0 + sub["in_slots"] + 1) % 2)
                for s in range(norm_stages(sub, 1)):
                    stage(sub, 1, s)

        @block.vector
        def _(dve):
            own = Count(dve, S["dve"])
            dve.sem_inc(S["w_lo"], START)
            dve.sem_inc(S["ada_used"], START)

            def split_w(n, par, width=SLOT):
                if isinstance(n, int) and n >= N_SLOTS:
                    return
                dve.wait_ge(S["w_hi"], n + 1)
                if not isinstance(n, int) or n >= 2:
                    dve.wait_ge(S["w_used"], n * 2 - 2 + START)
                nc.vector.tensor_tensor(w_lo[par][:, 0:width], raw[:, 0:width], w_hi[par][:, 0:width].bitcast(F32),
                                        ALU.subtract).then_inc(S["w_lo"], 1)

            def hj(sub, g, c, q, hs, b):
                w = sub["groups"][g] * P
                hi, lo = split_h(sub, b)
                dve.wait_ge(S["hj_hi"], q + 1)
                dve.wait_ge(S["w_used"], hs - 1 + START)
                nc.vector.tensor_tensor(lo[:, 0:w], hidden(sub, g, c), hi[:, 0:w].bitcast(F32), ALU.subtract).then_inc(S["hj_lo"], 1)

            def unit(count, u):
                if u == 0:
                    own.link(nc.vector.memset(acc[:], 0.0))
                dve.wait_ge(S[f"ada_raw{u % 2}"], (count - u % 2) * 8 + 16)
                for c in range(2):
                    for s in range(2):
                        k = 2 * u + c
                        if c == 1:
                            own.wait_back(1)
                        elif u and s == 0:
                            own.wait_back(0)
                        elif u:
                            dve.wait_ge(S["ada_used"], count + START)
                        ins = nc.vector.scalar_tensor_tensor(out=acc[:, s, :], in0=raw_ada[u % 2][:, c, :], scalar=silu_c[:, k, s:s + 1],
                                                             in1=acc[:, s, :], op0=ALU.mult, op1=ALU.add)
                        if c == 1 and s == 1:
                            ins.then_inc(S["ada_used"], 1)
                        else:
                            own.mark(ins)

            def finish_col(h, hl, bank_):
                dve.wait_ge(S["fin_mm"], h + 1)
                bias = b_col[:, bass.ds(h * 4, 4)].unsqueeze(2).to_broadcast([P, 4, 2])
                dst = vecs[:, bass.ds(hl, 1), :, :].rearrange("p a c s -> p (a c) s")
                nc.vector.tensor_tensor(dst, ps[:, bank_, GW:GW + 8].rearrange("p (c s) -> p c s", s=2), bias,
                                        ALU.add).then_inc(S["fin_read"], 1)

            def gate_half(sub, i, b0):
                dve.wait_ge(S["row_mm"], 2 * sub["gate"] + i + 1)
                dve.wait_ge(S["gate_in"], 32 * (sub["gate"] + 1))
                for s in range(2):
                    row = gate_row[:, s, i * HB:(i + 1) * HB]
                    ins = nc.vector.scalar_tensor_tensor(out=row, in0=ps[:, b0 + s, :], scalar=0.5 if sub["kind"] == "ffn" else 1.0,
                                                         in1=row, op0=ALU.mult, op1=ALU.mult)
                ins.then_inc(S["row_read"], 1)

            def make_mod(l, j):
                h = 6 * j
                dve.wait_ge(S["fin_read"], l * HALVES + h + 4)
                nc.vector.tensor_copy(m_shift[:], vecs[:, h:h + 2].rearrange("p a c s -> p (a c) s"))
                own.link(nc.vector.scalar_tensor_tensor(
                    out=m_scale[:], in0=vecs[:, h + 2:h + 4].rearrange("p a c s -> p (a c) s"), scalar=1.0,
                    in1=nw_col[:, l, j, :].unsqueeze(2).to_broadcast([P, KC, 2]), op0=ALU.add, op1=ALU.mult))

            def prenorm_rs(xi, i):
                dve.wait_ge(S["std2"], xi + 1)
                nc.vector.reciprocal(stat[:, i, 5:6], stat[:, i, 4:5]).then_inc(S["rs2"], 1)

            def prenorm_mod(xi, t, b):
                s = 0 if t < NTL else 1
                tile = ps[:, b:b + 2, :].rearrange("p b (c w) -> p (b c) w", w=P)
                dve.wait_ge(S["xT"], xi + 1)
                own.link(nc.vector.tensor_tensor(tile, tile, m_scale[:, :, s].unsqueeze(2).to_broadcast([P, KC, P]), ALU.mult))
                nc.vector.tensor_tensor(tile, tile, m_shift[:, :, s].unsqueeze(2).to_broadcast([P, KC, P]),
                                        ALU.add).then_inc(S["modded"], 1)

            def prenorm_lo(xi, t, b):
                tile = ps[:, b:b + 2, :].rearrange("p b (c w) -> p (b c) w", w=P)
                dve.wait_ge(S["xn_hi"], xi + 1)
                nc.vector.tensor_tensor(xn_lo[:, :, t * P:(t + 1) * P], tile, xn_hi[:, :, t * P:(t + 1) * P].bitcast(F32),
                                        ALU.subtract).then_inc(S["xn_done"], 1)

            def residual(sub, g, i):
                dve.wait_ge(S["std1"], sub["y"] + g * GT + i + 1)
                own.link(nc.vector.reciprocal(stat[:, i, 2:3], stat[:, i, 1:2]))
                nc.vector.scalar_tensor_tensor(out=ys(i), in0=psum_tile(i) if sub["final"] else ys(i), scalar=stat[:, i, 2:3],
                                               in1=gate_row[:, 0 if tiles_of(sub)[g][i] < NTL else 1, :],
                                               op0=ALU.mult, op1=ALU.mult).then_inc(S["gated"], 1)

            def stage(sub, g, s):
                tiles, y0, x0 = tiles_of(sub)[g], sub["y"] + g * GT, sub["xn"] + g * GT
                a, b, _, c, lo = norm_work(sub, g, s)
                if b is not None:
                    prenorm_rs(x0 + b, b)
                if c is not None:
                    prenorm_mod(x0 + c, tiles[c], turn_bank(sub["next"], c) if g else 6)
                if lo is not None:
                    prenorm_lo(x0 + lo, tiles[lo], turn_bank(sub["next"], lo) if g else 6)
                if a is not None and g == 0:
                    residual(sub, g, s)

            def evacuate(sub, g):
                if sub["final"]:
                    return
                n_end = sub["slot"] + sub["in_slots"] + (g + 1) * sub["k_slots"]
                dve.wait_ge(S["w_used"], 2 * n_end + START)
                if sub["y"] + g * GT:
                    dve.wait_ge(S["x_new"], sub["y"] + g * GT)
                for i in range(sub["groups"][g]):
                    nc.vector.tensor_copy(ys(i), psum_tile(i)).then_inc(S["y_copied"], 1)
                dve.wait_ge(S["y_copied"], sub["y"] + g * GT + sub["groups"][g])

            def first_out(sub):
                nb = sub["slot"] + sub["in_slots"]
                for c in range(2):
                    hj(sub, 0, c, sub["hj"] + c, 2 * nb + c, c)

            dve.wait_ge(S["consts"], 16 * 8)
            dve.wait_ge(S["pool_consts"], 2)
            nc.vector.tensor_copy(ident_bf[:], ident[:])
            nc.vector.tensor_scalar(mask[:], tri, -1.0, -NEG, ALU.add, ALU.mult).then_inc(S["dve_consts"], 1)
            for t in range(NT):
                prenorm_rs(t, t)
            for i in range(4):
                dve.wait_ge(S["rows_mm"], i + 1)
                nc.vector.tensor_copy(acc[0:2, i % 2, :], ps[0:2, 5, :]).then_inc(S["rows_sb"], 1)
                if i == 2:
                    split_w(0, 0)
                finish_col(i, i, 6)
            make_mod(0, 0)
            for g in range(2):
                for i in range(GT + 1):
                    t = g * GT + i
                    if i < GT:
                        prenorm_mod(t, t, turn_bank((0, 0), i))
                    if i > 0:
                        prenorm_lo(t - 1, t - 1, turn_bank((0, 0), i - 1))
                if g == 0:
                    split_w(1, 1)

            for sub in SUBS:
                l, j, n0 = sub["l"], sub["j"], sub["slot"]
                par0 = n0 % 2
                if sub["kind"] == "ffn":
                    for f, n, s, half in in_steps(sub, own.loop, (13, 0)):
                        if not (isinstance(f, int) and f == 0):
                            split_w(n + 1, (par0 + s + 1) % 2)
                        if half is not None:
                            hl, i, h0, g0 = half
                            for u in (2 * s, 2 * s + 1):
                                unit(i * 4 + (4 * g0 - 16 + u), u)
                            if s == 1:
                                finish_col(i + g0, i + h0, 3)
                        dve.wait_ge(S["silu"], f + (sub["proj"] + 1))
                        if sub["final"]:
                            hd = hidden(sub, 0, f)
                            nc.vector.tensor_tensor(hd, hd, ps[:, s * 4 + 1, :], ALU.mult).then_inc(S["h_done"], 1)
                            if isinstance(f, int) and f == 1:
                                gate_half(sub, 0, 2)
                                gate_half(sub, 1, 6)
                            continue
                        for g in range(2):
                            w = sub["in_groups"][g] * P
                            hd = hid[:, g, bass.ds(f, 1), 0:w].rearrange("p a w -> p (a w)")
                            ins = nc.vector.tensor_tensor(hd, hd, ps[:, s * 4 + 2 * g + 1, 0:w], ALU.mult)
                        ins.then_inc(S["h_done"], 1)
                else:
                    mixer_dve(dve, own, sub, split_w, first_out)
                if sub["next"]:
                    make_mod(*sub["next"])
                for g in range(len(sub["groups"])):
                    nb = n0 + sub["in_slots"] + g * sub["k_slots"]
                    q0 = sub["hj"] + g * 2 * sub["k_slots"]
                    pb = nb % 2
                    early = sub["kind"] == "mix" and g == 0
                    if not early:
                        hj(sub, g, 0, q0, 2 * nb, 0)
                    if g == 1:
                        evacuate(sub, 0)
                    done = 0
                    for s, n, par, half, u, st in out_steps(sub, g, own.loop, 0):
                        if not (early and s == 0):
                            hj(sub, g, s * 2 + 1, s * 2 + (q0 + 1), n * 2 + 1, 1)
                        split_w(n + 1, (pb + par + 1) % 2)
                        if not (isinstance(s, int) and s == sub["k_slots"] - 1):
                            hj(sub, g, s * 2 + 2, s * 2 + (q0 + 2), n * 2 + 2, 0)
                        if not sub["final"] and g == 0 and isinstance(s, int) and s < 2:
                            gate_half(sub, s, 6)
                        if half is not None:
                            unit(4 * half[2] - 16 + u, u)
                            if u == 3:
                                finish_col(half[2], half[1], 6)
                        if st is not None:
                            stage(sub, 0, st)
                            done = st + 1
                if sub["final"]:
                    evacuate(sub, 0)
                for s in range(done, norm_stages(sub, 0)):
                    stage(sub, 0, s)
                if sub["final"]:
                    break
                evacuate(sub, 1)
                for i in range(sub["groups"][1]):
                    residual(sub, 1, i)
                split_w(n0 + sub["in_slots"] + 2 * sub["k_slots"] + 1, (par0 + sub["in_slots"] + 1) % 2)
                for s in range(norm_stages(sub, 1)):
                    stage(sub, 1, s)

        @block.tensor
        def _(pe):
            loop = plain_loop(pe)
            mm = nc.tensor.matmul
            pe.sem_inc(S["w_used"], START)

            def project_in(sub, n, par, b, groups=(0, 1), taken=None, between=None):
                if sub["final"]:
                    spans = [(0, SEQ, 0)] if len(groups) == 2 else [((0, GW, 0), (GW, SEQ - GW, 0))[g] for g in groups]
                else:
                    spans = [(g * GW, GW, g) for g in groups]
                pe.wait_ge(S["w_lo"], n + 1 + START)
                hi = w_hi[par][:].rearrange("p (k c n) -> p k c n", k=KC, c=2)
                lo = w_lo[par][:].rearrange("p (k c n) -> p k c n", k=KC, c=2)
                for c in range(2):
                    if c == 1 and between:
                        between()
                    if c == 1 and taken is not None:
                        pe.wait_ge(S["fin_read"], taken)
                    for k in range(KC):
                        for i, (w, xx) in enumerate(((hi, xn_hi), (hi, xn_lo), (lo, xn_hi))):
                            for t0, wd, g in spans:
                                col = t0 if sub["final"] else 0
                                ins = mm(ps[:, 4 * b + 2 * g + c, col:col + wd], w[:, k, c, :], xx[:, k, t0:t0 + wd],
                                         start=(k == 0 and i == 0), stop=(k == KC - 1 and i == 2))
                if 1 in groups:
                    ins.then_inc(S["w_used"], 2)

            def project_out(sub, g, s, n, par, q0, first, last):
                halves = [split_h(sub, c) for c in range(2)]
                hi = w_hi[par][:].rearrange("p (c n) -> p c n", c=2)
                lo = w_lo[par][:].rearrange("p (c n) -> p c n", c=2)
                pe.wait_ge(S["w_lo"], n + 1 + START)
                for c in range(2):
                    pe.wait_ge(S["hj_lo"], s * 2 + (q0 + c + 1))
                    for i in range(sub["groups"][g]):
                        if g == 1 and first and c == 0:
                            pe.wait_ge(S["y_copied"], sub["y"] + i + 1)
                        for a, (xx, w) in enumerate(((halves[c][0], hi), (halves[c][0], lo), (halves[c][1], hi))):
                            for hf in range(2):
                                ins = mm(ps[:, 2 * i + hf, :], xx[:, i * P:(i + 1) * P], w[:, c, hf * 512:(hf + 1) * 512],
                                         start=first and c == 0 and a == 0, stop=last and c == 1 and a == 2,
                                         skip_group_check=True)
                    ins.then_inc(S["w_used"], 1)

            def finish_col(h, units, bank_):
                pe.wait_ge(S["ada_used"], units + START)
                for c in range(4):
                    for s in range(2):
                        ins = mm(ps[:, bank_, GW + 2 * c + s:GW + 2 * c + s + 1], acc[:, s, c * P:(c + 1) * P], ones[:, 0:1],
                                 start=True, stop=True)
                ins.then_inc(S["fin_mm"], 1)

            def gate_half(sub, i, b0):
                h = 6 * sub["j"] + 4 + i
                pe.wait_ge(S["fin_read"], sub["l"] * HALVES + h + 1)
                if sub["gate"] or i:
                    pe.wait_ge(S["row_read"], 2 * sub["gate"] + (i if b0 == 6 and not sub["final"] else 0))
                for s in range(2):
                    for c in range(4):
                        ins = mm(ps[:, b0 + s, c * P:(c + 1) * P], vecs[:, h, c, s:s + 1].to_broadcast([P, P]), ident[:],
                                 start=True, stop=True)
                ins.then_inc(S["row_mm"], 1)

            def turn(xi, i, rows, b=6, before=0):
                pe.wait_ge(S["xs"], xi + 1)
                if xi > before:
                    pe.wait_ge(S["xn_done"], xi - before)
                if rows:
                    pe.wait_ge(S["row_read"], rows)
                else:
                    pe.wait_ge(S["fin_read"], 4)
                for c in range(KC):
                    ins = nc.tensor.transpose(ps[:, b + c // 4, (c % 4) * P:(c % 4 + 1) * P], ys(i)[:, c * P:(c + 1) * P], ident[:])
                ins.then_inc(S["xT"], 1)

            pe.wait_ge(S["pool_consts"], 2)
            pe.wait_ge(S["dve_consts"], 1)
            pe.wait_ge(S["silu_c"], 1)
            for i in range(4):
                pe.wait_ge(S["ada_first"][i], 16)
                for k in range(KC):
                    ins = mm(ps[0:2, 5, :], silu_c[:, k, :], ada0(i)[:, k, :], start=(k == 0), stop=(k == KC - 1))
                ins.then_inc(S["rows_mm"], 1)
                pe.wait_ge(S["rows_sb"], i + 1)
                if i:
                    pe.wait_ge(S["fin_read"], i)
                for c in range(4):
                    ins = nc.tensor.transpose(ps[:, 6, GW + 2 * c:GW + 2 * c + 2], acc[0:2, i % 2, c * P:(c + 1) * P], ident[0:2, 0:2])
                ins.then_inc(S["fin_mm"], 1)
            def turn_late(sub, i):
                turn(sub["xn"] - sub["late"] + i, i if sub["y"] else GT + i, 2 * sub["gate"],
                     turn_bank((sub["l"], sub["j"]), i), min(i, 1))

            def banks_free(sub, k):
                if sub["y"]:
                    pe.wait_ge(S["y_copied"], sub["y"] - sub["late"] + min(k, sub["late"]))

            for t in range(GT):
                turn(t, t, 0, turn_bank((0, 0), t), min(t, 1))

            for sub in SUBS:
                n0 = sub["slot"]
                par0 = n0 % 2
                if sub["kind"] == "ffn":
                    ada_end = None
                    for hl, h0, count in sub["ada_in"]:
                        ada_end = hl * HALVES + h0 + count
                    late = sub["late"]
                    for f, n, s, half in in_steps(sub, loop, (0, 0)):
                        if isinstance(f, int) and f < 2:
                            if f == 0:
                                pe.wait_ge(S["xn_done"], sub["xn"] - late)
                                banks_free(sub, 1)
                                project_in(sub, n, par0, 0, (0,))
                                turn_late(sub, 0)
                                banks_free(sub, GT)
                                project_in(sub, n + 1, 1 - par0, 1, (0,), between=lambda: turn_late(sub, 1) if late > 1 else None)
                                if late > 2:
                                    turn_late(sub, 2)
                                pe.wait_ge(S["xn_done"], sub["xn"])
                            project_in(sub, n, (par0 + f) % 2, f, (1,))
                            if sub["final"] and f == 1:
                                gate_half(sub, 0, 2)
                                gate_half(sub, 1, 6)
                            continue
                        pe.wait_ge(S["h_done"], f + (sub["proj"] - 1))
                        project_in(sub, n, (par0 + s) % 2, s,
                                   taken=half[1] + half[3] if half is not None else ada_end)
                        if half is not None and s == 1:
                            hl, i, h0, g0 = half
                            pe.wait_ge(S["h_done"], f + sub["proj"])
                            finish_col(i + g0, i * 4 + (4 * g0 - 12), 3)
                    pe.wait_ge(S["h_done"], sub["proj"] + FC)
                    if ada_end:
                        pe.wait_ge(S["fin_read"], ada_end)
                else:
                    mixer_pe(pe, sub, turn_late, banks_free)
                for g in range(len(sub["groups"])):
                    nb = n0 + sub["in_slots"] + g * sub["k_slots"]
                    q0 = sub["hj"] + g * 2 * sub["k_slots"]
                    pb = nb % 2
                    done = 0
                    for s, n, par, half, u, st in out_steps(sub, g, loop, 0):
                        dyn = not isinstance(s, int)
                        project_out(sub, g, s, n, (pb + par) % 2, q0,
                                    first=(not dyn and s == 0), last=(not dyn and s == sub["k_slots"] - 1))
                        if sub["kind"] == "mix" and g == 0 and s == 0:
                            head_out(pe, sub, HEADS - 1)
                            pe.wait_ge(S["mix_done"], HEADS * (sub["mix"] + 1))
                        if not sub["final"] and g == 0 and not dyn and s < 2:
                            gate_half(sub, s, 6)
                        if half is not None and u == 3:
                            pe.wait_ge(S["row_read"], 2 * sub["gate"] + 2)
                            pe.wait_ge(S["fin_read"], half[2])
                            finish_col(half[2], 4 * half[2] - 12, 6)
                        if st is not None and not sub["final"]:
                            t = norm_work(sub, 0, st)[2]
                            if t is not None:
                                turn(sub["xn"] + t, t, 2 * sub["gate"] + 2)
                            done = st + 1
                for s in range(done, norm_stages(sub, 0)):
                    t = norm_work(sub, 0, s)[2]
                    if t is not None:
                        turn(sub["xn"] + t, t, 2 * sub["gate"] + 2)

def kernel(x, c, ctx, c_ctx, w_ada, b_ada, norm_w, w_ff_in, w_ff_out, w_in, w_fmix, conv_w, conv_b, w_qkv, gate_b,
           mlstm_norm_w, w_out):
    import concourse.bacc as bacc
    from concourse.bass_utils import run_bass_kernel_spmd

    def cols(a, n):
        a = a.reshape(a.shape[:-1] + (n, P))
        return np.ascontiguousarray(np.moveaxis(a, -1, 0))

    def dft(s, norm):
        a = np.outer(np.arange(s), np.arange(s)) % s * (2 * np.pi / s)
        both = np.stack([np.cos(a), -np.sin(a)], 1) / norm
        return np.ascontiguousarray(both.reshape(s // P, P, 2, s).transpose(1, 0, 2, 3).astype(np.float32))

    group = D // 2 // 8
    ag = np.outer(np.arange(group), np.arange(group)) % group * (2 * np.pi / group)
    dft_g = np.zeros((P, 2 * P), np.float32)
    fmix = np.zeros((DEPTH, P, 4, P), np.float32)
    for i in range(2):
        s = slice(i * group, (i + 1) * group)
        dft_g[s, s] = np.cos(ag)
        dft_g[s, P + i * group:P + (i + 1) * group] = np.sin(ag)
        fmix[:, s, :, s] = np.asarray(w_fmix)[:, i::2].transpose(0, 2, 1, 3)
    tri = np.stack([np.triu(np.ones((P, P), np.float32)), np.tril(np.ones((P, P), np.float32))], 1)
    arrays = {
        "x_in": np.concatenate([np.asarray(x)[0], np.asarray(ctx)[0]]).reshape(NT, P, D),
        "w_ada": np.asarray(w_ada),
        "norm_w": np.asarray(norm_w),
        "w_ff_in": np.ascontiguousarray(np.asarray(w_ff_in).reshape(DEPTH, 2, KC, P, 2, FC, P).transpose(0, 1, 5, 3, 2, 4, 6)
                                        ).reshape(DEPTH, 2, FC, P, SLOT),
        "w_ff_out": np.asarray(w_ff_out),
        "w_in": np.asarray(w_in),
        "w_gates": np.ascontiguousarray(np.asarray(w_in)[:, :, 1536:].reshape(DEPTH, KC, P, 16).transpose(0, 2, 1, 3)
                                        ).reshape(DEPTH, P, KC * 16),
        "w_out": np.asarray(w_out),
        "w_qkv": np.asarray(w_qkv),
                "cvec_in": np.ascontiguousarray(np.stack([np.asarray(c)[0], np.asarray(c_ctx)]).reshape(2, KC, P).transpose(2, 1, 0)),
        "gate_b_in": np.ascontiguousarray(np.broadcast_to(np.asarray(gate_b).reshape(1, DEPTH, 16), (P, DEPTH, 16))),
        "b_col_in": cols(np.asarray(b_ada), 9 * KC).reshape(P, DEPTH * HALVES * 4),
        "nw_col_in": cols(np.asarray(norm_w)[:, 0::2], KC),
        "convw_in": np.ascontiguousarray(np.asarray(conv_w).reshape(DEPTH, 9, HEADS, P).transpose(3, 0, 2, 1)),
        "convb_in": cols(np.asarray(conv_b), HEADS),
        "hn_w_in": cols(np.asarray(mlstm_norm_w), HEADS),
        "fmix_in": fmix,
        "dft_l_in": dft(SEQ, np.sqrt(SEQ * group)),
        "dft_c_in": dft(CTX, np.sqrt(CTX * group)),
        "dft_g_in": dft_g,
        "tri_in": np.ascontiguousarray(tri),
    }
    nc = bacc.Bacc("TRN2", target_bir_lowering=False, num_devices=1)
    args = {k: nc.dram_tensor(k, a.shape, mybir.dt.from_np(a.dtype), kind="ExternalInput").ap() for k, a in arrays.items()}
    args["out"] = nc.dram_tensor("out", (NTL, P, D), F32, kind="ExternalOutput").ap()
    build(nc, **args)
    r = run_bass_kernel_spmd(nc, [arrays], core_ids=[0])
    return r.results[0]["out"].reshape(1, SEQ, D)
```
